# Optimizing a Trainium2 kernel written in Bass

```python
import jax, jax.numpy as jnp
from jax import lax
import numpy as np

D_MODEL = 1024
BATCH = 1
SEQ = 256
DEPTH = 2

MLSTM_HEADS = 4
MLSTM_QK_DIM = 128
MLSTM_V_DIM = 256
MLSTM_CHUNK = 64
CONV_K = 4
SB_HEADS = 16
SB_HEAD_DIM = D_MODEL // SB_HEADS
Q_BLOCK = 128
N_EXPERTS = 64
TOP_K = 8
N_GROUPS = 8
TOPK_GROUPS = 4
EXPERT_FF = 128
SHARED_FF = 256
ROUTED_SCALE = 2.5
EPS = 1e-6

MLSTM_QK = MLSTM_HEADS * MLSTM_QK_DIM
MLSTM_V = MLSTM_HEADS * MLSTM_V_DIM
SB_WIDTH = SB_HEADS * SB_HEAD_DIM
IN_WIDTH = 2 * MLSTM_QK + 2 * MLSTM_V + 2 * MLSTM_HEADS + 3 * SB_WIDTH + 2 * D_MODEL

kernel_name = 'hybrid_mlstm_stickbreak_moe'

def rms_norm(x, w):
    x32 = x.astype(jnp.float32)
    y = x32 * lax.rsqrt(jnp.mean(x32 * x32, axis=-1, keepdims=True) + EPS)
    return (y * w.astype(jnp.float32)).astype(x.dtype)

def modulate(h, shift, scale):
    return h * (1 + scale[:, None, :]) + shift[:, None, :]

def causal_depthwise_conv(u, w, b):
    k_taps = w.shape[0]
    s = u.shape[1]
    up = jnp.pad(u, ((0, 0), (k_taps - 1, 0), (0, 0)))
    out = b
    for j in range(k_taps):
        out = out + up[:, j:j + s, :] * w[j]
    return out

def _mlstm_chunk_step(carry, xs):
    C, n, m = carry
    q, k, v, ig, lf = xs
    L = q.shape[2]
    b = jnp.cumsum(lf, axis=-1)
    a = b[..., -1]
    causal = jnp.tril(jnp.ones((L, L), dtype=bool))
    dmat = jnp.where(causal, b[..., :, None] - b[..., None, :] + ig[..., None, :], -jnp.inf)
    inter = b + m[..., None]
    m_t = jnp.maximum(inter, jnp.max(dmat, axis=-1))
    w_intra = jnp.exp(dmat - m_t[..., None])
    w_inter = jnp.exp(inter - m_t)
    s = jnp.einsum('bhtd,bhsd->bhts', q, k) * w_intra
    num = jnp.einsum('bhts,bhsv->bhtv', s, v) + w_inter[..., None] * jnp.einsum('bhtd,bhdv->bhtv', q, C)
    den = jnp.sum(s, axis=-1) + w_inter * jnp.einsum('bhtd,bhd->bht', q, n)
    h = num / jnp.maximum(jnp.abs(den), jnp.exp(-m_t))[..., None]
    g = a[..., None] - b + ig
    m_new = jnp.maximum(a + m, jnp.max(g, axis=-1))
    wc = jnp.exp(g - m_new[..., None])
    decay = jnp.exp(a + m - m_new)
    C_new = decay[..., None, None] * C + jnp.einsum('bhsd,bhsv->bhdv', k * wc[..., None], v)
    n_new = decay[..., None] * n + jnp.einsum('bhs,bhsd->bhd', wc, k)
    return (C_new, n_new, m_new), h

def mlstm(q, k, v, i_pre, f_pre):
    bsz, s = q.shape[0], q.shape[1]
    nc = s // MLSTM_CHUNK

    def to_chunks(t):
        t = t.astype(jnp.float32).reshape((bsz, nc, MLSTM_CHUNK) + t.shape[2:])
        return jnp.moveaxis(jnp.moveaxis(t, 3, 2), 1, 0)

    xs = (to_chunks(q) * (MLSTM_QK_DIM ** -0.5), to_chunks(k), to_chunks(v),
          to_chunks(i_pre), to_chunks(jax.nn.log_sigmoid(f_pre.astype(jnp.float32))))
    init = (jnp.zeros((bsz, MLSTM_HEADS, MLSTM_QK_DIM, MLSTM_V_DIM), jnp.float32),
            jnp.zeros((bsz, MLSTM_HEADS, MLSTM_QK_DIM), jnp.float32),
            jnp.zeros((bsz, MLSTM_HEADS), jnp.float32))
    _, h = lax.scan(_mlstm_chunk_step, init, xs)
    h = jnp.moveaxis(jnp.moveaxis(h, 0, 1), 2, 3)
    return h.reshape(bsz, s, MLSTM_HEADS, MLSTM_V_DIM)

def stick_breaking_attention(q, k, v):
    s_len, dh = q.shape[2], q.shape[3]
    scale = dh ** -0.5
    outs = []
    for blk in range(s_len // Q_BLOCK):
        t0, t1 = blk * Q_BLOCK, (blk + 1) * Q_BLOCK
        qb = q[:, :, t0:t1].astype(jnp.float32)
        kp = k[:, :, :t1].astype(jnp.float32)
        vp = v[:, :, :t1].astype(jnp.float32)
        z = jnp.einsum('bhtd,bhsd->bhts', qb, kp) * scale
        mask = jnp.arange(t1)[None, :] < jnp.arange(t0, t1)[:, None]
        log_fail = jnp.where(mask, jax.nn.log_sigmoid(-z), 0.0)
        later = lax.cumsum(log_fail, axis=3, reverse=True) - log_fail
        att = jnp.where(mask, jnp.exp(jax.nn.log_sigmoid(z) + later), 0.0)
        outs.append(jnp.einsum('bhts,bhsd->bhtd', att, vp))
    return jnp.concatenate(outs, axis=2).astype(q.dtype)

def hybrid_mixer(h, w_in, conv_w, conv_b, m_igate_b, m_fgate_b, m_norm_w, w_proj_a, w_proj_b, w_out):
    bsz, s, _ = h.shape
    p = h @ w_in
    sizes = [2 * MLSTM_QK, MLSTM_V, MLSTM_V, MLSTM_HEADS, MLSTM_HEADS, SB_WIDTH, SB_WIDTH, SB_WIDTH, D_MODEL, D_MODEL]
    offs, acc = [], 0
    for sz in sizes[:-1]:
        acc += sz
        offs.append(acc)
    mqk, mv, mo, mi, mf, sq, sk, sv, ga, gb = jnp.split(p, offs, axis=-1)
    mqk = jax.nn.silu(causal_depthwise_conv(mqk, conv_w, conv_b))
    mq, mk = jnp.split(mqk, 2, axis=-1)
    hm = mlstm(mq.reshape(bsz, s, MLSTM_HEADS, MLSTM_QK_DIM),
               mk.reshape(bsz, s, MLSTM_HEADS, MLSTM_QK_DIM),
               mv.reshape(bsz, s, MLSTM_HEADS, MLSTM_V_DIM),
               mi + m_igate_b, mf + m_fgate_b)
    hm = hm * lax.rsqrt(jnp.mean(hm * hm, axis=-1, keepdims=True) + EPS)
    hm = (hm.reshape(bsz, s, MLSTM_V) * m_norm_w.astype(jnp.float32)).astype(h.dtype) * jax.nn.sigmoid(mo)
    to_heads = lambda t: t.reshape(bsz, s, SB_HEADS, SB_HEAD_DIM).transpose(0, 2, 1, 3)
    hs = stick_breaking_attention(to_heads(sq), to_heads(sk), to_heads(sv))
    hs = hs.transpose(0, 2, 1, 3).reshape(bsz, s, SB_WIDTH)
    y = jax.nn.sigmoid(ga) * (hm @ w_proj_a) + jax.nn.sigmoid(gb) * (hs @ w_proj_b)
    return y @ w_out

def moe_ffn(u, router_w, router_b, w_gate, w_up, w_down, sh_gate, sh_up, sh_down):
    bsz, s, d = u.shape
    t = u.reshape(-1, d)
    scores = jax.nn.sigmoid((t @ router_w).astype(jnp.float32))
    sel = scores + router_b.astype(jnp.float32)
    grp = sel.reshape(-1, N_GROUPS, N_EXPERTS // N_GROUPS)
    grp_score = jnp.sum(lax.top_k(grp, 2)[0], axis=-1)
    _, gidx = lax.top_k(grp_score, TOPK_GROUPS)
    gmask = jnp.sum(jax.nn.one_hot(gidx, N_GROUPS, dtype=jnp.float32), axis=-2)
    emask = jnp.repeat(gmask, N_EXPERTS // N_GROUPS, axis=-1) > 0
    _, eidx = lax.top_k(jnp.where(emask, sel, -jnp.inf), TOP_K)
    wts = jnp.take_along_axis(scores, eidx, axis=-1)
    wts = wts / jnp.sum(wts, axis=-1, keepdims=True) * ROUTED_SCALE
    gates = jnp.sum(jax.nn.one_hot(eidx, N_EXPERTS, dtype=jnp.float32) * wts[..., None], axis=-2).astype(u.dtype)
    hid = jax.nn.silu(jnp.einsum('nd,edf->nef', t, w_gate)) * jnp.einsum('nd,edf->nef', t, w_up)
    routed = jnp.einsum('nef,efd->nd', hid * gates[..., None], w_down)
    shared = (jax.nn.silu(t @ sh_gate) * (t @ sh_up)) @ sh_down
    return (routed + shared).reshape(bsz, s, d)

def setup_inputs(seed: int = 0) -> dict:
    key = jax.random.key(seed)
    ks = jax.random.split(key, 24)
    nrm = lambda k, shape, sc: jax.random.normal(k, shape, jnp.float32) * sc
    E, F, FS = N_EXPERTS, EXPERT_FF, SHARED_FF
    return {
        'x': nrm(ks[0], (BATCH, SEQ, D_MODEL), 1.0),
        'c': nrm(ks[1], (BATCH, D_MODEL), 1.0),
        'ada_w': nrm(ks[2], (DEPTH, D_MODEL, 6 * D_MODEL), 0.5 * D_MODEL ** -0.5),
        'ada_b': nrm(ks[3], (DEPTH, 6 * D_MODEL), 0.02),
        'norm1_w': 1.0 + nrm(ks[4], (DEPTH, D_MODEL), 0.05),
        'w_in': nrm(ks[5], (DEPTH, D_MODEL, IN_WIDTH), D_MODEL ** -0.5),
        'conv_w': nrm(ks[6], (DEPTH, CONV_K, 2 * MLSTM_QK), CONV_K ** -0.5),
        'conv_b': nrm(ks[7], (DEPTH, 2 * MLSTM_QK), 0.02),
        'm_igate_b': nrm(ks[8], (DEPTH, MLSTM_HEADS), 0.1),
        'm_fgate_b': 3.0 + nrm(ks[9], (DEPTH, MLSTM_HEADS), 0.5),
        'm_norm_w': 1.0 + nrm(ks[10], (DEPTH, MLSTM_V), 0.05),
        'w_proj_a': nrm(ks[11], (DEPTH, MLSTM_V, D_MODEL), MLSTM_V ** -0.5),
        'w_proj_b': nrm(ks[12], (DEPTH, SB_WIDTH, D_MODEL), SB_WIDTH ** -0.5),
        'w_out': nrm(ks[13], (DEPTH, D_MODEL, D_MODEL), D_MODEL ** -0.5),
        'norm2_w': 1.0 + nrm(ks[14], (DEPTH, D_MODEL), 0.05),
        'router_w': nrm(ks[15], (DEPTH, D_MODEL, E), D_MODEL ** -0.5),
        'router_b': nrm(ks[16], (DEPTH, E), 0.01),
        'w_gate': nrm(ks[17], (DEPTH, E, D_MODEL, F), D_MODEL ** -0.5),
        'w_up': nrm(ks[18], (DEPTH, E, D_MODEL, F), D_MODEL ** -0.5),
        'w_down': nrm(ks[19], (DEPTH, E, F, D_MODEL), F ** -0.5),
        'sh_gate': nrm(ks[20], (DEPTH, D_MODEL, FS), D_MODEL ** -0.5),
        'sh_up': nrm(ks[21], (DEPTH, D_MODEL, FS), D_MODEL ** -0.5),
        'sh_down': nrm(ks[22], (DEPTH, FS, D_MODEL), FS ** -0.5),
        'final_norm_w': 1.0 + nrm(ks[23], (D_MODEL,), 0.05),
    }

def reference(x, c, ada_w, ada_b, norm1_w, w_in, conv_w, conv_b, m_igate_b, m_fgate_b, m_norm_w,
              w_proj_a, w_proj_b, w_out, norm2_w, router_w, router_b, w_gate, w_up, w_down,
              sh_gate, sh_up, sh_down, final_norm_w):
    cond = jax.nn.silu(c)
    for l in range(DEPTH):
        mod = cond @ ada_w[l] + ada_b[l]
        sh1, sc1, g1, sh2, sc2, g2 = jnp.split(mod, 6, axis=-1)
        h = modulate(rms_norm(x, norm1_w[l]), sh1, sc1)
        mix = hybrid_mixer(h, w_in[l], conv_w[l], conv_b[l], m_igate_b[l], m_fgate_b[l], m_norm_w[l],
                           w_proj_a[l], w_proj_b[l], w_out[l])
        x = x + (g1[:, None, :] * mix).astype(x.dtype)
        h = modulate(rms_norm(x, norm2_w[l]), sh2, sc2)
        ffn = moe_ffn(h, router_w[l], router_b[l], w_gate[l], w_up[l], w_down[l], sh_gate[l], sh_up[l], sh_down[l])
        x = x + (g2[:, None, :] * ffn).astype(x.dtype)
    return rms_norm(x, final_norm_w)


_drawn_inputs = setup_inputs


def setup_inputs(seed=0):
    import zlib

    import numpy as np

    out = dict(_drawn_inputs(seed))
    spreads = {}
    factors = {'conv_b': 4.56, 'm_igate_b': 64.0}
    for name, (base, spread) in spreads.items():
        noise = np.random.default_rng([zlib.crc32(name.encode()), seed]).standard_normal(out[name].shape)
        drawn = base * np.exp(spread * noise) if base else spread * noise
        out[name] = __import__('jax').numpy.asarray(drawn.astype(out[name].dtype))
    for name, factor in factors.items():
        out[name] = (out[name] * factor).astype(out[name].dtype)
    return out
```

```python
from contextlib import ExitStack

import concourse.bass as bass
from concourse import mybir

F32 = mybir.dt.float32
F32R = mybir.dt.float32r
ALU = mybir.AluOpType
ACT = mybir.ActivationFunctionType
AX = mybir.AxisListType

P = 128
EPS = 1e-6
ROUTED_SCALE = 2.5
TOP_K, TOPK_GROUPS, N_GROUPS = 8, 4, 8
RING = 4
AHEAD = RING - 1
MASKED = -1e30
FAR = 3e38
N_SMALL = 12
N_CONST = 17
N_HEAD = 23
STEPS = 235
LEXP = "natural_log_exp_and_others"


def ds(i, n=1):
    return bass.ds(i, n)


def hold(eng, sem):
    eng.sem_inc(sem, 1)


class Steps:

    def __init__(self, eng, sem, per_layer):
        self.eng, self.sem, self.per_layer = eng, sem, per_layer
        self.base, self.k = 0, 0

    def at(self, base):
        self.base, self.k = base, 0

    def link(self, ins):
        self.k += 1
        ins.then_inc(self.sem, 1)
        self.eng.wait_ge(self.sem, self.base + self.k)


def trunk(nc, x, c, ada_w, ada_b, norm1_w, w_in, conv_w, conv_b, m_igate_b, m_fgate_b, m_norm_w,
          w_proj_a, w_proj_b, w_out, norm2_w, router_w, router_b, w_gate, w_up, w_down,
          sh_gate, sh_up, sh_down, final_norm_w, gates_dram, out):
    _, T, D = x.shape
    L = ada_w.shape[0]
    TB, KB = T // P, D // P
    E, FF = w_gate.shape[1], w_gate.shape[3]
    H = m_igate_b.shape[1]
    QK = conv_w.shape[2] // (2 * H)
    V = w_proj_a.shape[1] // H
    DH = 64
    NPAIR = D // (2 * DH)
    NT = conv_w.shape[1]
    assert TB == 2 and KB == 8 and QK == P and V == 2 * P and FF == P and E % 4 == 0 and NPAIR == 8
    sizes = [H * QK, H * QK, H * V, H * V, H, H, D, D, D, D, D]
    MQ, MK, MV, MO, MI, MF, SQ, SK, SV, GA, GB = [sum(sizes[:i]) for i in range(11)]
    EG = E // N_GROUPS
    CAUSAL = T + P

    PAIRS_IT, SB_U = 4, 16
    ML_U = 8
    PJ_U = 4
    EXP_IT = 4
    g_sb = 0
    g_ml = g_sb + NPAIR // PAIRS_IT * SB_U // RING
    g_pj = g_ml + H * ML_U // RING
    g_out = g_pj + KB // 2 * PJ_U // RING
    g_moe = g_out + 3
    g_post = g_moe + E * 3 // RING
    GL = g_post + 1

    with ExitStack() as ctx:
        def sb(name, shape, dt=F32):
            return ctx.enter_context(nc.sbuf_tensor(name, shape, dt))

        def sem(name):
            return ctx.enter_context(nc.semaphore(name))

        PS = ctx.enter_context(nc.psum_tensor("PS", [P, 8, 512], F32))

        raw = sb("raw", [P, RING, 1024])
        w_hi = sb("w_hi", [P, RING, 1024], F32R)
        w_lo = sb("w_lo", [P, RING, 1024], F32R)
        ada_raw = sb("ada_raw", [P, 2, 2 * D])
        ada_acc = sb("ada_acc", [P, 2 * D])
        x_sb = sb("x_sb", [P, TB, D])
        h_hi = sb("h_hi", [P, KB, T], F32R)
        h_lo = sb("h_lo", [P, KB, T], F32R)
        hm_hi = sb("hm_hi", [P, KB, T], F32R)
        hm_lo = sb("hm_lo", [P, KB, T], F32R)
        hs_hi = sb("hs_hi", [P, KB, T], F32R)
        hs_lo = sb("hs_lo", [P, KB, T], F32R)
        ga_sb = sb("ga_sb", [P, KB, T])
        gb_sb = sb("gb_sb", [P, KB, T])
        xn = ga_sb[:].rearrange("p a b -> p (a b)").rearrange("p (t d) -> p t d", t=TB)
        g1_sb = sb("g1_sb", [P, D])
        g2_sb = sb("g2_sb", [P, D])
        h_full = gb_sb[:, 0:4, :].rearrange("p (a b) t -> p a (b t)", a=2)
        zt = sb("zt", [P, 2, CAUSAL])
        sp = sb("sp", [P, 2, CAUSAL])
        sp_hi = sb("sp_hi", [P, 2, CAUSAL], F32R)
        sp_lo = sb("sp_lo", [P, 2, CAUSAL], F32R)
        att = sb("att", [P, 2, CAUSAL])
        att_hi = sb("att_hi", [P, 2, CAUSAL], F32R)
        att_lo = sb("att_lo", [P, 2, CAUSAL], F32R)
        qk_hi = sb("qk_hi", [P, 2, T], F32R)
        qk_lo = sb("qk_lo", [P, 2, T], F32R)
        VA = V + 2
        v_hi = sb("v_hi", [P, TB, VA], F32R)
        v_lo = sb("v_lo", [P, TB, VA], F32R)
        sv_hi = sb("sv_hi", [P, 2, TB, P], F32R)
        sv_lo = sb("sv_lo", [P, 2, TB, P], F32R)
        qk_pad = sb("qk_pad", [P, 2, NT - 1 + T])
        conv = sb("conv", [P, 2, T])
        sig = sb("sig", [P, 2, T])
        mo_sb = sb("mo_sb", [P, 2, T])
        M_sb = sb("M_sb", [P, H, T])
        assert H == EXP_IT
        gate_b = M_sb
        ident = sb("ident", [P, P])
        ident_r = sb("ident_r", [P, P], F32R)
        ones = sb("ones", [P, P])
        negmask = sb("negmask", [P, P], F32R)
        negtri = sb("negtri", [P, P], F32R)
        negones = sb("negones", [P, P], F32R)
        zeros_r = sb("zeros_r", [P, P], F32R)
        head_sel = sb("head_sel", [H, H, P])
        cond = sb("cond", [P, KB])
        c_sb = sb("c_sb", [P, 2, KB])
        NROW = NT * KB + 2 * KB
        par_rows = sb("par_rows", [NROW, P])
        par = sb("par", [P, NROW])
        bcol = sb("bcol", [P, 4, KB])
        nw = sb("nw", [P, 2, KB])
        ab = sb("ab", [P, 2, 2, KB])
        gbias = sb("gbias", [H, 2])
        ucol = sb("ucol", [P, TB, H])
        emcol = sb("emcol", [P, TB, H])
        st = sb("st", [P, 8, 2])
        rb = sb("rb", [P, E])
        sc = sb("sc", [P, TB, E])
        sel = sb("sel", [P, TB, E])
        rep = sb("rep", [P, TB, E])
        gts = sb("gts", [P, TB, E])
        m8 = sb("m8", [P, TB, N_GROUPS, 8])
        gp = sb("gp", [P, TB, 16])
        gr = sb("gr", [P, TB, 16])
        t8 = sb("t8", [P, TB, 8])
        gm = sb("gm", [P, 2, TB, N_GROUPS])
        gT = mo_sb[0:E, 0, :]
        row_keep = [conv[0:H, 0, :], conv[0:H, 1, :], mo_sb[0:H, 1, :]]

        rows = [sp[0:H, 0, 0:T], att[0:H, 0, 0:T], sp[0:H, 1, 0:T], att[0:H, 1, 0:T],
                zt[0:H, 0, 0:T], zt[0:H, 1, 0:T]]
        r_i, r_f, r_b, r_m, r_t, r_e = rows
        wT, S_f, S_hi, S_lo = att[:, 0, :], sp[:, 0, :], sp_hi[:, 0, :], sp_lo[:, 0, :]
        hmn = zt[:, :, 0:V]
        y1, y2 = sp[:, 0, 0:T], sp[:, 1, 0:T]
        hid_hi, hid_lo = qk_hi, qk_lo

        raw_loaded = [sem(f"raw_loaded{i}") for i in range(RING)]
        hi_ready = sem("hi_ready")
        lo_ready = sem("lo_ready")
        unit_used = sem("unit_used")
        x_loaded = sem("x_loaded")
        c_loaded = sem("c_loaded")
        par_loaded = sem("par_loaded")
        ada_loaded = [sem("ada_loaded0"), sem("ada_loaded1")]
        ada_used = sem("ada_used")
        consts = sem("consts")
        ss_done = sem("ss_done")
        xn_ready = sem("xn_ready")
        tr_done = sem("tr_done")
        hf_ready = sem("hf_ready")
        hhi_ready = sem("hhi_ready")
        h_ready = sem("h_ready")
        par_t = sem("par_t")
        par_ready = sem("par_ready")
        acc_ready = sem("acc_ready")
        ada_red = sem("ada_red")
        ab_ready = sem("ab_ready")
        row_a = sem("row_a")
        row_v = sem("row_v")
        rows_t = sem("rows_t")
        cols_ready = sem("cols_ready")
        mb_ready = sem("mb_ready")
        g_ready = sem("g_ready")
        qkhi_ready = sem("qkhi_ready")
        qk_ready = sem("qk_ready")
        vhi_ready = sem("vhi_ready")
        v_ready = sem("v_ready")
        z_done = sem("z_done")
        ln_ready = sem("ln_ready")
        sp_ready = sem("sp_ready")
        sphi_ready = sem("sphi_ready")
        splo_ready = sem("splo_ready")
        l_done = sem("l_done")
        att_ready = sem("att_ready")
        atthi_ready = sem("atthi_ready")
        attlo_ready = sem("attlo_ready")
        av_done = sem("av_done")
        hshi_ready = sem("hshi_ready")
        hs_ready = sem("hs_ready")
        g_evac = sem("g_evac")
        pad_ready = sem("pad_ready")
        conv_ready = sem("conv_ready")
        sig_ready = sem("sig_ready")
        qkf_ready = sem("qkf_ready")
        w_ready = sem("w_ready")
        w_masked = sem("w_masked")
        s_done = sem("s_done")
        sf_ready = sem("sf_ready")
        shi_ready = sem("shi_ready")
        s_ready = sem("s_ready")
        num_done = sem("num_done")
        r_ready = sem("r_ready")
        sq_ready = sem("sq_ready")
        hmn_ready = sem("hmn_ready")
        sigo_ready = sem("sigo_ready")
        hmt_done = sem("hmt_done")
        hmf_ready = sem("hmf_ready")
        hmhi_ready = sem("hmhi_ready")
        hm_ready = sem("hm_ready")
        sg_ready = sem("sg_ready")
        yf_ready = sem("yf_ready")
        yhi_ready = sem("yhi_ready")
        y_ready = sem("y_ready")
        mix_added = sem("mix_added")
        rt_ready = sem("rt_ready")
        gts_ready = sem("gts_ready")
        gt_done = sem("gt_done")
        gT_ready = sem("gT_ready")
        gT_stored = sem("gT_stored")
        gate_loaded = [sem("gate_loaded0"), sem("gate_loaded1")]
        silu_ready = sem("silu_ready")
        hid_full = sem("hid_full")
        hidhi_ready = sem("hidhi_ready")
        hid_ready = sem("hid_ready")
        out_ready = sem("out_ready")
        stored = sem("stored")
        dve_step = sem("dve_step")
        pool_held, pe_held, dve_held = sem("pool_held"), sem("pe_held"), sem("dve_held")

        EV = E + 2
        ND = STEPS
        block = ctx.enter_context(nc.Block())

        def dram_rows(w, l):
            return w[ds(l)].rearrange("o a b -> (o a) b")

        @block.sync
        def _(sp_e):
            sp_e.dma_start(x_sb[:], x.rearrange("o (t p) d -> p (o t) d", p=P)).then_inc(x_loaded, 16)

            def load(src, g, i, width=1024):
                sp_e.wait_ge(lo_ready, g * RING + i + 1)
                sp_e.dma_start(raw[:, i % RING, 0:width].rearrange("p (k n) -> p k n", n=src.shape[-1]),
                               src).then_inc(raw_loaded[i % RING], 16)

            def cols(w, l, col, n=P, k0=0, nk=KB):
                v = w[ds(l), :, ds(col, n)].rearrange("o (p k) n -> (o p) k n", k=KB)
                return v[:, k0:k0 + nk, :]

            def cols_std(w, l, col, n=P, k0=0, nk=KB):
                v = w[ds(l), k0 * P:(k0 + nk) * P, ds(col, n)]
                return v.rearrange("o (k p) n -> (o p) k n", p=P)

            with sp_e.Fori(0, L) as l:
                g = l * GL
                load(cols(w_in, l, MI, 2 * H), g, 0, 2 * H * KB)
                with sp_e.Fori(0, NPAIR // PAIRS_IT) as it:
                    gi = g + g_sb + it * (SB_U // RING)
                    for j in range(PAIRS_IT):
                        for n, off in enumerate((SQ, SK, SV, GA)):
                            load(cols(w_in, l, it * (PAIRS_IT * P) + (off + j * P)), gi, 1 + 4 * j + n)
                with sp_e.Fori(0, H) as it:
                    gi = g + g_ml + it * (ML_U // RING)
                    load(cols(w_in, l, it * QK + MQ), gi, 1)
                    load(cols(w_in, l, it * QK + MK), gi, 2)
                    load(cols(w_in, l, it * V + MV, V, 0, 4), gi, 3)
                    load(cols(w_in, l, it * V + MV, V, 4, 4), gi, 4)
                    load(cols(w_in, l, it * V + MO), gi, 5)
                    load(cols(w_in, l, it * V + (MO + P)), gi, 6)
                    load(cols(w_in, l, it * V + GB), gi, 7)
                    load(cols(w_in, l, it * V + (GB + P)), gi, 8)
                with sp_e.Fori(0, KB // 2) as it:
                    gi = g + g_pj + it * (PJ_U // RING)
                    for n in range(2):
                        load(cols_std(w_proj_b, l, it * (2 * P) + n * P), gi, 1 + 2 * n)
                        load(cols_std(w_proj_a, l, it * (2 * P) + n * P), gi, 2 + 2 * n)
                for n in range(8):
                    load(cols_std(w_out, l, (n // 4) * 512, 512, 2 * (n % 4), 2), g + g_out, 1 + n)
                load(cols(router_w, l, 0, E), g + g_out, 9, E * KB)

                def expert_in(w, l, e):
                    return w[ds(l), ds(e)].rearrange("o q (p k) f -> (o q p) k f", k=KB)

                def expert_out(l, e):
                    return w_down[ds(l), ds(e)].rearrange("o q p (k d) -> (o q p) k d", d=D)

                def shared_out(l, b):
                    return sh_down[ds(l), b * P:(b + 1) * P].rearrange("o p (k d) -> (o p) k d", d=D)

                load(cols(sh_gate, l, 0), g + g_out, 10)
                load(cols(sh_up, l, 0), g + g_out, 11)

                def expert_units(e, gi, i, down):
                    load(expert_in(w_gate, l, e), gi, i)
                    load(expert_in(w_up, l, e), gi, i + 1)
                    load(down, gi, i + 2)

                expert_units(0, g + g_moe, 0, shared_out(l, 0))
                with sp_e.Fori(0, E // EXP_IT - 1) as it:
                    for n in range(EXP_IT):
                        expert_units(it * EXP_IT + (n + 1), g + g_moe + it * 3, 3 * (n + 1),
                                     expert_out(l, it * EXP_IT + n))
                for n in range(EXP_IT - 1):
                    e = E - EXP_IT + 1 + n
                    expert_units(e, g + g_moe + (E // EXP_IT - 1) * 3, 3 * (n + 1), expert_out(l, e - 1))
                load(cols(sh_gate, l, P), g + g_post, 0)
                load(cols(sh_up, l, P), g + g_post, 1)
                load(expert_out(l, E - 1), g + g_post, 2)
                load(shared_out(l, 1), g + g_post, 3)
            sp_e.wait_ge(out_ready, 1)
            sp_e.dma_start(out.rearrange("o (t p) d -> p (o t) d", p=P), x_sb[:]).then_inc(stored, 16)
            sp_e.wait_ge(stored, 16)

        @block.gpsimd
        def _(pool):
            pool.dma_start(c_sb[:, 0, :], c.rearrange("o (p k) -> (o p) k", k=KB)).then_inc(c_loaded, 16)
            ks = [0]

            def step(ins):
                ks[0] += 1
                ins.then_inc(consts, 1)
                pool.wait_ge(consts, ks[0])

            step(nc.gpsimd.memset(ones[:], 1.0))
            step(nc.gpsimd.memset(ident[:], 0.0))
            step(nc.gpsimd.affine_select(out=ident[:], in_=ident[:], compare_op=ALU.not_equal, fill=1.0,
                                         base=0, pattern=[[-1, P]], channel_multiplier=1))
            step(nc.gpsimd.tensor_copy(ident_r[:], ident[:]))
            f = sp[:, 0, 0:P]
            step(nc.gpsimd.memset(f, 0.0))
            step(nc.gpsimd.tensor_copy(zeros_r[:], f))
            step(nc.gpsimd.affine_select(out=f, in_=f, compare_op=ALU.is_gt, fill=MASKED,
                                         base=0, pattern=[[1, P]], channel_multiplier=-1))
            step(nc.gpsimd.tensor_copy(negmask[:], f))
            step(nc.gpsimd.memset(f, -1.0))
            step(nc.gpsimd.tensor_copy(negones[:], f))
            step(nc.gpsimd.affine_select(out=f, in_=f, compare_op=ALU.is_ge, fill=0.0,
                                         base=0, pattern=[[-1, P]], channel_multiplier=1))
            step(nc.gpsimd.tensor_copy(negtri[:], f))
            step(nc.gpsimd.memset(head_sel[:], 0.0))
            step(nc.gpsimd.affine_select(out=head_sel[:], in_=head_sel[:], compare_op=ALU.not_equal, fill=1.0,
                                         base=0, pattern=[[-1, H], [0, P]], channel_multiplier=1))
            step(nc.gpsimd.memset(v_lo[:].bitcast(F32), 0.0))
            step(nc.gpsimd.tensor_copy(v_hi[:, :, V:VA], ones[:, 0:4].rearrange("p (a b) -> p a b", b=2)))
            step(nc.gpsimd.memset(qk_pad[:], 0.0))

            def load_ada(l, part, k, i, slot):
                pool.wait_ge(ada_used, i + 1)
                hold(pool, pool_held)
                pool.dma_start(ada_raw[:, slot, :],
                               ada_w[ds(l), :, part * 2 * D:(part + 1) * 2 * D].rearrange(
                                   "o (p k) n -> (o p) k n", k=KB)[:, ds(k), :]).then_inc(ada_loaded[slot], 16)

            assert ks[0] == N_CONST, ks[0]
            with pool.Fori(0, L) as l:
                pool.wait_ge(mix_added, l * 8 + 4)
                hold(pool, pool_held)
                small = []

                def load_small(dst, src):
                    small.append(pool.dma_start(dst, src).then_inc(par_loaded, 16))

                load_small(par_rows[0:NT * KB, :], conv_w[ds(l)].rearrange("o t (b p) -> (o t b) p", p=P))
                load_small(par_rows[NT * KB:NT * KB + KB, :], conv_b[ds(l), :].rearrange("o (b p) -> (o b) p", p=P))
                load_small(par_rows[NT * KB + KB:NROW, :], m_norm_w[ds(l), :].rearrange("o (b p) -> (o b) p", p=P))
                bv = ada_b[ds(l), :].rearrange("o (s p k) -> (o p) s k", k=KB, p=P)
                load_small(bcol[:, 0:2, :], bv[:, 0:2, :])
                load_small(bcol[:, 2:4, :], bv[:, 3:5, :])
                load_small(nw[:, 0, :], norm1_w[ds(l), :].rearrange("o (p k) -> (o p) k", k=KB))
                load_small(nw[:, 1, :], norm2_w[ds(l), :].rearrange("o (p k) -> (o p) k", k=KB))
                load_small(gbias[:, 0:1], m_igate_b[ds(l), :].rearrange("o h -> h o"))
                load_small(gbias[:, 1:2], m_fgate_b[ds(l), :].rearrange("o h -> h o"))
                load_small(g1_sb[:], ada_b[ds(l), 2 * D:3 * D].to_broadcast([P, D]))
                load_small(g2_sb[:], ada_b[ds(l), 5 * D:6 * D].to_broadcast([P, D]))
                load_small(rb[:], router_b[ds(l), :].to_broadcast([P, E]))
                assert len(small) == N_SMALL
                for k in range(KB):
                    load_ada(l, 0, k, l * (3 * KB) + k, k % 2)
                with pool.Fori(0, NPAIR // PAIRS_IT) as it:
                    for j in range(PAIRS_IT):
                        load_ada(l, 1, it * PAIRS_IT + j, l * (3 * KB) + KB + it * PAIRS_IT + j, j % 2)
                with pool.Fori(0, H) as it:
                    pool.wait_ge(w_ready, l * (2 * H) + it * 2 + 2)
                    hold(pool, pool_held)
                    for o in (0, T):
                        nc.gpsimd.affine_select(out=wT[:, o:o + P], in_=wT[:, o:o + P], compare_op=ALU.is_ge,
                                                fill=0.0, base=0, pattern=[[1, P]], channel_multiplier=-1
                                                ).then_inc(w_masked, 1)
                    for j in range(2):
                        load_ada(l, 2, it * 2 + j, l * (3 * KB) + 2 * KB + it * 2 + j, j)
                pool.wait_ge(gT_ready, l * 1 + 1)
                hold(pool, pool_held)
                pool.dma_start(gates_dram, gT).then_inc(gT_stored, 16)
                pool.wait_ge(gT_stored, l * 16 + 16)
                hold(pool, pool_held)
                with pool.Fori(0, E // EXP_IT) as it:
                    for s in range(2):
                        pool.wait_ge(hid_full, l * EV + it * EXP_IT + (2 * s + 2))
                        hold(pool, pool_held)
                        src = gates_dram[ds(it * EXP_IT + 2 * s, 2), :].rearrange("(o e) t -> o (e t)", o=1).to_broadcast([P, 2 * T])
                        pool.dma_start(gate_b[:, 2 * s:2 * s + 2, :].rearrange("p e t -> p (e t)"), src
                                       ).then_inc(gate_loaded[s], 16)
            pool.wait_ge(mix_added, L * 8 + 4)
            pool.dma_start(g1_sb[:], final_norm_w.rearrange("(o d) -> o d", o=1).to_broadcast([P, D])
                           ).then_inc(par_loaded, 16)

        @block.scalar
        def _(act):
            act.wait_ge(c_loaded, 16)
            nc.scalar.activation(c_sb[:, 1, :], c_sb[:, 0, :], ACT.Sigmoid).then_inc(sig_ready, 1)

            def split(g, i, width=1024):
                act.wait_ge(unit_used, g * RING + i + 1)
                act.wait_ge(raw_loaded[i % RING], (g + i // RING + 1) * 16)
                nc.scalar.activation(w_hi[:, i % RING, 0:width], raw[:, i % RING, 0:width], ACT.Copy
                                     ).then_inc(hi_ready, 1)

            def used(g, i):
                act.wait_ge(unit_used, g * RING + (i + 1 + RING))

            def norm_in(n):
                for t in range(TB):
                    nc.scalar.activation(xn[:, t, :], x_sb[:, t, :], ACT.Square,
                                         accum_out=st[:, 0, t:t + 1]).then_inc(ss_done, 1)

            def norm_hi(n):
                for b in range(4):
                    act.wait_ge(hf_ready, n * 4 + (b + 1))
                    nc.scalar.activation(h_hi[:, 2 * b:2 * b + 2, :], h_full[:, b % 2, :].rearrange(
                        "p (k t) -> p k t", t=T), ACT.Copy).then_inc(hhi_ready, 1)

            act.wait_ge(mix_added, 4)
            with act.Fori(0, L) as l:
                g = l * GL
                split(g, 0, 2 * H * KB)
                split(g, 1)
                split(g, 2)
                act.wait_ge(mix_added, l * 8 + 4)
                norm_in(l * 2)
                norm_hi(l * 2)
                split(g, 3)
                nc.scalar.preload_act_table_set(LEXP)
                act.wait_ge(row_v, l * 3 + 2)
                nc.scalar.activation(r_t, r_t, ACT.Exp, scale=-1.0).then_inc(row_a, 1)
                act.wait_ge(row_a, l * 3 + 1)
                nc.scalar.activation(r_t, r_t, ACT.Ln, bias=1.0).then_inc(row_a, 1)
                act.wait_ge(row_v, l * 3 + 3)
                nc.scalar.activation(r_e, r_e, ACT.Exp, scale=-1.0).then_inc(row_a, 1)

                with act.Fori(0, NPAIR // PAIRS_IT) as it:
                    gi = g + g_sb + it * (SB_U // RING)
                    pr = l * NPAIR + it * PAIRS_IT

                    def att_part(n):
                        act.wait_ge(l_done, n + 1)
                        zb = PS[:, 4 + 2 * par2:6 + 2 * par2, 0:CAUSAL]
                        nc.scalar.activation(att[:], zb, ACT.Exp).then_inc(att_ready, 1)
                        act.wait_ge(att_ready, n + 1)
                        nc.scalar.activation(att_hi[:], att[:], ACT.Copy).then_inc(atthi_ready, 1)

                    def av_part(n, jj):
                        act.wait_ge(av_done, n + 1)
                        for a in range(2):
                            q = slice(a * DH, (a + 1) * DH)
                            nc.scalar.activation(hs_hi[q, ds(jj), :],
                                                 PS[q, 3:4, a * T:(a + 1) * T], ACT.Copy).then_inc(hshi_ready, 1)

                    for j in range(PAIRS_IT):
                        n = pr + j
                        split(gi, 4 * j + 1 + AHEAD)
                        split(gi, 4 * j + 2 + AHEAD)
                        used(gi, 4 * j + 2)
                        nc.scalar.activation(qk_hi[:, 0, :], PS[:, 0, 0:T], ACT.Copy, scale=DH ** -0.5
                                             ).then_inc(qkhi_ready, 1)
                        nc.scalar.activation(qk_hi[:, 1, :], PS[:, 0, T:2 * T], ACT.Copy).then_inc(qkhi_ready, 1)
                        if j:
                            par2 = (j - 1) % 2
                            att_part(n - 1)
                        split(gi, 4 * j + 3 + AHEAD)
                        used(gi, 4 * j + 3)
                        nc.scalar.activation(sv_hi[:, j % 2, :, :].rearrange("p a b -> p (a b)"),
                                             PS[:, 1, 0:T], ACT.Copy).then_inc(vhi_ready, 1)
                        act.wait_ge(z_done, n + 1)
                        nc.scalar.activation(zt[:], PS[:, 4 + 2 * (j % 2):6 + 2 * (j % 2), 0:CAUSAL], ACT.Abs
                                             ).then_inc(ln_ready, 1)
                        act.wait_ge(ln_ready, n * 3 + 1)
                        nc.scalar.activation(zt[:], zt[:], ACT.Exp, scale=-1.0).then_inc(ln_ready, 1)
                        act.wait_ge(ln_ready, n * 3 + 2)
                        nc.scalar.activation(zt[:], zt[:], ACT.Ln, bias=1.0).then_inc(ln_ready, 1)
                        split(gi, 4 * j + 4 + AHEAD)
                        used(gi, 4 * j + 4)
                        nc.scalar.activation(ga_sb[:, ds(it * PAIRS_IT + j), :], PS[:, 2:3, 0:T], ACT.Copy
                                             ).then_inc(g_evac, 1)
                        if j:
                            av_part(n - 1, it * PAIRS_IT + (j - 1))
                    par2 = (PAIRS_IT - 1) % 2
                    att_part(pr + (PAIRS_IT - 1))
                    av_part(pr + (PAIRS_IT - 1), it * PAIRS_IT + (PAIRS_IT - 1))

                act.wait_ge(rows_t, l * 1 + 1)
                nc.scalar.activation(M_sb[:].rearrange("p (a b) t -> p a (b t)", a=2), PS[:, 6:8, :], ACT.Copy
                                     ).then_inc(mb_ready, 1)

                with act.Fori(0, H) as it:
                    gi = g + g_ml + it * (ML_U // RING)
                    n = l * H + it
                    split(gi, 1 + AHEAD)
                    split(gi, 2 + AHEAD)
                    used(gi, 2)
                    nc.scalar.activation(qk_pad[:, :, NT - 1:NT - 1 + T], PS[:, 0, :].rearrange(
                        "p (a t) -> p a t", t=T), ACT.Copy).then_inc(pad_ready, 1)
                    act.wait_ge(mb_ready, l * 1 + 1)
                    act.wait_ge(cols_ready, l * 1 + 1)
                    act.wait_ge(s_ready, n + 1)
                    nc.scalar.activation(wT[:, 0:T], M_sb[:, ds(it), :].rearrange("p a t -> p (a t)"), ACT.Exp,
                                         bias=ucol[:, 0, ds(it)], scale=-1.0).then_inc(w_ready, 1)
                    nc.scalar.activation(wT[:, T:CAUSAL], M_sb[:, ds(it), P:T].rearrange("p a t -> p (a t)"), ACT.Exp,
                                         bias=ucol[:, 1, ds(it)], scale=-1.0).then_inc(w_ready, 1)
                    split(gi, 3 + AHEAD)
                    split(gi, 4 + AHEAD)
                    act.wait_ge(conv_ready, n + 1)
                    nc.scalar.activation(sig[:], conv[:], ACT.Sigmoid).then_inc(sig_ready, 1)
                    used(gi, 4)
                    nc.scalar.activation(v_hi[:, :, 0:V], PS[:, 1, :].rearrange("p (a v) -> p a v", v=V), ACT.Copy
                                         ).then_inc(vhi_ready, 1)
                    act.wait_ge(qkf_ready, n + 1)
                    nc.scalar.activation(qk_hi[:], conv[:], ACT.Copy).then_inc(qkhi_ready, 1)
                    split(gi, 5 + AHEAD)
                    act.wait_ge(sf_ready, n + 1)
                    nc.scalar.activation(S_hi, S_f, ACT.Copy).then_inc(shi_ready, 1)
                    split(gi, 6 + AHEAD)
                    used(gi, 6)
                    nc.scalar.activation(mo_sb[:], PS[:, 2, :].rearrange("p (a t) -> p a t", t=T), ACT.Sigmoid
                                         ).then_inc(sigo_ready, 1)
                    split(gi, 7 + AHEAD)
                    act.wait_ge(r_ready, n + 1)
                    for t in range(TB):
                        nc.scalar.activation(hmn[:, t, :], PS[:, 4 + t, 0:V], ACT.Square, scale=st[:, 2, t:t + 1],
                                             accum_out=st[:, 3, t:t + 1]).then_inc(sq_ready, 1)
                    split(gi, 8 + AHEAD)
                    used(gi, 8)
                    nc.scalar.activation(gb_sb[:, ds(it * 2, 2), :], PS[:, 7, :].rearrange("p (a t) -> p a t", t=T),
                                         ACT.Copy).then_inc(g_evac, 1)
                    act.wait_ge(hmf_ready, n + 1)
                    nc.scalar.activation(hm_hi[:, ds(it * 2, 2), :], conv[:], ACT.Copy).then_inc(hmhi_ready, 1)

                with act.Fori(0, KB // 2) as it:
                    gi = g + g_pj + it * (PJ_U // RING)
                    for b in range(2):
                        n = l * KB + it * 2 + b
                        split(gi, 2 * b + 1 + AHEAD)
                        act.wait_ge(yf_ready, n + 2)
                        nc.scalar.activation(sig[:, 0, :], ga_sb[:, ds(it * 2 + b), :].rearrange("p a t -> p (a t)"),
                                             ACT.Sigmoid).then_inc(sg_ready, 1)
                        nc.scalar.activation(sig[:, 1, :], gb_sb[:, ds(it * 2 + b), :].rearrange("p a t -> p (a t)"),
                                             ACT.Sigmoid).then_inc(sg_ready, 1)
                        split(gi, 2 * b + 2 + AHEAD)
                        act.wait_ge(yf_ready, n + 3)
                        nc.scalar.activation(h_hi[:, ds(it * 2 + b), :], y1.rearrange("p (a t) -> p a t", a=1),
                                             ACT.Copy).then_inc(yhi_ready, 1)
                for i in range(8):
                    split(g + g_out, i + 1 + AHEAD, E * KB if i + 1 + AHEAD == 9 else 1024)
                split(g + g_out, 9 + AHEAD)
                act.wait_ge(mix_added, l * 8 + 8)
                norm_in(l * 2 + 1)
                norm_hi(l * 2 + 1)
                used(g + g_out, 9)
                nc.scalar.activation(sc[:], PS[:, 4, 0:TB * E].rearrange("p (t e) -> p t e", e=E), ACT.Sigmoid
                                     ).then_inc(rt_ready, 1)
                split(g + g_out, 10 + AHEAD)

                def hidden(n, par, gi, i):
                    used(gi, i)
                    nc.scalar.activation(sig[:, par, :], PS[:, 6 + par, 0:T], ACT.Silu).then_inc(silu_ready, 1)
                    act.wait_ge(hid_full, n + 4)
                    nc.scalar.activation(hid_hi[:, par, :], conv[:, par, :], ACT.Copy).then_inc(hidhi_ready, 1)

                split(g + g_out, 11 + AHEAD)
                hidden(l * EV, 1, g + g_out, 11)
                with act.Fori(0, E // EXP_IT) as it:
                    gi = g + g_moe + it * 3
                    for e in range(EXP_IT):
                        split(gi, 3 * e + AHEAD)
                        split(gi, 3 * e + 1 + AHEAD)
                        hidden(l * EV + it * EXP_IT + (e + 1), e % 2, gi, 3 * e + 1)
                        split(gi, 3 * e + 2 + AHEAD)
                split(g + g_post, AHEAD)
                hidden(l * EV + (E + 1), 0, g + g_post, 1)
            act.wait_ge(mix_added, L * 8 + 4)
            norm_in(L * 2)

        @block.vector
        def _(dve):
            steps = Steps(dve, dve_step, ND)
            link = steps.link
            v = nc.vector
            dve.sem_inc(lo_ready, RING)
            dve.sem_inc(ada_used, 2)
            dve.sem_inc(s_ready, 1)
            dve.sem_inc(yf_ready, 2)
            dve.sem_inc(hm_ready, 1)
            dve.sem_inc(y_ready, 1)
            dve.sem_inc(hid_full, 3)
            dve.wait_ge(x_loaded, 16)
            dve.sem_inc(mix_added, 4)
            dve.wait_ge(sig_ready, 1)
            v.tensor_tensor(cond[:], c_sb[:, 0, :], c_sb[:, 1, :], ALU.mult).then_inc(row_v, 1)
            dve.wait_ge(row_v, 1)

            def split(g, i, width=1024):
                dve.wait_ge(hi_ready, g * RING + i + 1)
                s = i % RING
                v.tensor_tensor(w_lo[:, s, 0:width], raw[:, s, 0:width], w_hi[:, s, 0:width].bitcast(F32),
                                ALU.subtract).then_inc(lo_ready, 1)

            def used(g, i):
                dve.wait_ge(unit_used, g * RING + (i + 1 + RING))

            def rsqrt(a, y, t):
                link(v.tensor_scalar(y.bitcast(mybir.dt.int32), a.bitcast(mybir.dt.int32), -0.5, 1597463007.0,
                                     ALU.mult, ALU.add))
                for i in range(3):
                    link(v.scalar_tensor_tensor(t, y, -0.5, y, ALU.mult, ALU.mult))
                    link(v.tensor_tensor(t, t, a, ALU.mult))
                    link(v.scalar_tensor_tensor(a if i == 2 else y, t, 1.5, y, ALU.add, ALU.mult))

            def rstd(n):
                dve.wait_ge(ss_done, n * 2 + 2)
                link(v.tensor_scalar(st[:, 1, :], st[:, 0, :], 1.0 / D, EPS, ALU.mult, ALU.add))
                rsqrt(st[:, 1, :], st[:, 7, :], st[:, 6, :])

            def norm(n):
                rstd(n)
                for t in range(TB):
                    v.tensor_scalar(xn[:, t, :], x_sb[:, t, :], st[:, 1, t:t + 1], None, ALU.mult
                                    ).then_inc(xn_ready, 1)

            def modulated(n, which):
                def full(b):
                    if b >= 2:
                        dve.wait_ge(h_ready, n * 4 + (b - 1))
                    dve.wait_ge(tr_done, n * 4 + b + 1)
                    for k in range(2):
                        kk = 2 * b + k
                        ins = v.tensor_scalar(h_full[:, b % 2, k * T:(k + 1) * T], PS[:, b, k * T:(k + 1) * T],
                                              ab[:, which, 0, kk:kk + 1], ab[:, which, 1, kk:kk + 1],
                                              ALU.mult, ALU.add)
                    ins.then_inc(hf_ready, 1)

                def low(b):
                    dve.wait_ge(hhi_ready, n * 4 + b + 1)
                    v.tensor_tensor(h_lo[:, 2 * b:2 * b + 2, :], h_full[:, b % 2, :].rearrange("p (k t) -> p k t", t=T),
                                    h_hi[:, 2 * b:2 * b + 2, :].bitcast(F32), ALU.subtract).then_inc(h_ready, 1)

                full(0)
                for b in range(1, 4):
                    full(b)
                    low(b - 1)
                low(3)

            def ada_add(i, k, slot, first):
                dve.wait_ge(ada_loaded[slot], first)
                v.scalar_tensor_tensor(ada_acc[:], ada_raw[:, slot, :], cond[:, k], ada_acc[:], ALU.mult, ALU.add
                                       ).then_inc(ada_used, 1)

            def factor(which, cols):
                link(v.tensor_tensor(ab[:, which, 0, :], cols, bcol[:, 2 * which + 1, :], ALU.add))
                link(v.scalar_tensor_tensor(ab[:, which, 0, :], ab[:, which, 0, :], 1.0, nw[:, which, :],
                                            ALU.add, ALU.mult))

            with dve.Fori(0, L) as l:
                g = l * GL
                steps.at(l * ND)
                split(g, 0, 2 * H * KB)
                split(g, 1)
                split(g, 2)
                norm(l * 2)
                link(v.memset(ada_acc[:], 0.0))
                for k in range(KB):
                    ada_add(0, slice(k, k + 1), k % 2, (l * 12 + k // 2 + 1) * 16)
                    dve.wait_ge(ada_used, l * (3 * KB) + k + 3)
                dve.sem_inc(acc_ready, 1)
                dve.wait_ge(par_t, l * 1 + 1)
                link(v.tensor_copy(par[:], PS[:, 6, 0:NROW]))
                dve.wait_ge(ada_red, l * 3 + 1)
                link(v.tensor_tensor(ab[:, 0, 1, :], PS[:, 7, 0:KB], bcol[:, 0, :], ALU.add))
                factor(0, PS[:, 7, KB:2 * KB])
                modulated(l * 2, 0)
                split(g, 3)
                used(g, 0)
                link(v.tensor_scalar(r_i, PS[0:H, 4, 0:T], gbias[:, 0:1], None, ALU.add))
                link(v.tensor_scalar(r_f, PS[0:H, 4, T:2 * T], gbias[:, 1:2], None, ALU.add))
                link(v.tensor_scalar(r_b, r_f, -1.0, None, ALU.mult))
                v.tensor_tensor(r_t, r_f, r_b, ALU.max).then_inc(row_v, 1)
                dve.wait_ge(row_a, l * 3 + 2)
                link(v.scalar_tensor_tensor(r_f, r_f, 0.0, r_t, ALU.min, ALU.subtract))
                link(v.memset(r_m, 0.0))
                link(v.tensor_tensor_scan(r_b, r_f, r_m, 0.0, ALU.add, ALU.add))
                link(v.tensor_tensor(r_i, r_i, r_b, ALU.subtract))
                link(v.tensor_tensor_scan(r_f, r_i, r_m, 0.0, ALU.max, ALU.max))
                v.tensor_tensor(r_e, r_b, r_f, ALU.add).then_inc(row_v, 1)
                dve.wait_ge(row_a, l * 3 + 3)
                for r, src in enumerate((r_i, r_f, r_e)):
                    ins = v.tensor_copy(row_keep[r], src)
                ins.then_inc(row_v, 1)
                link(v.memset(ada_acc[:], 0.0))
                hold(dve, dve_held)
                n_head = steps.k

                with dve.Fori(0, NPAIR // PAIRS_IT) as it:
                    gi = g + g_sb + it * (SB_U // RING)
                    pr = l * NPAIR + it * PAIRS_IT

                    def att_part(n):
                        dve.wait_ge(atthi_ready, n + 1)
                        v.tensor_tensor(att_lo[:], att[:], att_hi[:].bitcast(F32), ALU.subtract).then_inc(attlo_ready, 1)

                    def av_part(n, jj):
                        dve.wait_ge(hshi_ready, n * 2 + 2)
                        for a in range(2):
                            q = slice(a * DH, (a + 1) * DH)
                            ins = v.tensor_tensor(hs_lo[q, ds(jj), :], PS[q, 3:4, a * T:(a + 1) * T],
                                                  hs_hi[q, ds(jj), :].bitcast(F32), ALU.subtract)
                        ins.then_inc(hs_ready, 1)

                    for j in range(PAIRS_IT):
                        n = pr + j
                        split(gi, 4 * j + 1 + AHEAD)
                        split(gi, 4 * j + 2 + AHEAD)
                        dve.wait_ge(qkhi_ready, l * (2 * NPAIR + H) + (it * (2 * PAIRS_IT) + 2 * j) + 2)
                        v.scalar_tensor_tensor(qk_lo[:, 0, :], PS[:, 0, 0:T], DH ** -0.5, qk_hi[:, 0, :].bitcast(F32),
                                               ALU.mult, ALU.subtract)
                        v.tensor_tensor(qk_lo[:, 1, :], PS[:, 0, T:2 * T], qk_hi[:, 1, :].bitcast(F32),
                                        ALU.subtract).then_inc(qk_ready, 1)
                        if j:
                            att_part(n - 1)
                        split(gi, 4 * j + 3 + AHEAD)
                        dve.wait_ge(vhi_ready, l * (NPAIR + H) + (it * PAIRS_IT + j) + 1)
                        v.tensor_tensor(sv_lo[:, j % 2, :, :].rearrange("p a b -> p (a b)"), PS[:, 1, 0:T],
                                        sv_hi[:, j % 2, :, :].rearrange("p a b -> p (a b)").bitcast(F32),
                                        ALU.subtract).then_inc(v_ready, 1)
                        dve.wait_ge(ada_used, l * (3 * KB) + (KB + 2) + (it * PAIRS_IT + j))
                        ada_add(0, ds(it * PAIRS_IT + j), j % 2, (l * 12 + 4 + it * 2 + (j // 2 + 1)) * 16)
                        dve.wait_ge(ln_ready, n * 3 + 3)
                        v.scalar_tensor_tensor(sp[:], PS[:, 4 + 2 * (j % 2):6 + 2 * (j % 2), 0:CAUSAL], 0.0, zt[:],
                                               ALU.max, ALU.add).then_inc(sp_ready, 1)
                        dve.wait_ge(sp_ready, n + 1)
                        v.tensor_copy(sp_hi[:], sp[:]).then_inc(sphi_ready, 1)
                        dve.wait_ge(sphi_ready, n + 1)
                        v.tensor_tensor(sp_lo[:], sp[:], sp_hi[:].bitcast(F32), ALU.subtract).then_inc(splo_ready, 1)
                        split(gi, 4 * j + 4 + AHEAD)
                        if j:
                            av_part(n - 1, it * PAIRS_IT + (j - 1))
                    att_part(pr + (PAIRS_IT - 1))
                    av_part(pr + (PAIRS_IT - 1), it * PAIRS_IT + (PAIRS_IT - 1))

                steps.at(l * ND + n_head)
                dve.wait_ge(ada_used, l * (3 * KB) + (2 * KB + 2))
                dve.sem_inc(acc_ready, 1)
                dve.wait_ge(rows_t, l * 1 + 1)
                v.tensor_copy(ucol[:], PS[:, 1, 0:TB * H].rearrange("p (a h) -> p a h", h=H))
                v.tensor_copy(emcol[:], PS[:, 1, TB * H:2 * TB * H].rearrange("p (a h) -> p a h", h=H)
                              ).then_inc(cols_ready, 1)
                dve.wait_ge(cols_ready, l * 1 + 1)
                dve.wait_ge(ada_red, l * 3 + 2)
                link(v.tensor_tensor(ab[:, 1, 1, :], PS[:, 1, 64:64 + KB], bcol[:, 2, :], ALU.add))
                v.tensor_tensor(g1_sb[:], PS[:, 4:6, :].rearrange("p a b -> p (a b)"), g1_sb[:], ALU.add
                                ).then_inc(g_ready, 1)
                link(v.memset(ada_acc[:], 0.0))
                hold(dve, dve_held)
                n_mid = n_head + steps.k

                with dve.Fori(0, H) as it:
                    gi = g + g_ml + it * (ML_U // RING)
                    n = l * H + it
                    steps.at(l * ND + n_mid + it * N_HEAD)
                    split(gi, 1 + AHEAD)
                    split(gi, 2 + AHEAD)
                    dve.wait_ge(hm_ready, n + 1)
                    dve.wait_ge(pad_ready, n + 1)

                    def tap(a, j):
                        return par[:, ds(it + (j * KB + a * H))]

                    for a in range(2):
                        link(v.tensor_scalar(conv[:, a, :], qk_pad[:, a, 0:T], tap(a, 0), tap(a, NT),
                                             ALU.mult, ALU.add))
                        for j in range(1, NT):
                            ins = v.scalar_tensor_tensor(conv[:, a, :], qk_pad[:, a, j:j + T], tap(a, j),
                                                         conv[:, a, :], ALU.mult, ALU.add)
                            if a == 0 or j < NT - 1:
                                link(ins)
                    ins.then_inc(conv_ready, 1)
                    split(gi, 3 + AHEAD)
                    split(gi, 4 + AHEAD)
                    dve.wait_ge(sig_ready, n + 2)
                    link(v.scalar_tensor_tensor(conv[:, 0, :], conv[:, 0, :], QK ** -0.5, sig[:, 0, :],
                                                ALU.mult, ALU.mult))
                    v.tensor_tensor(conv[:, 1, :], conv[:, 1, :], sig[:, 1, :], ALU.mult).then_inc(qkf_ready, 1)
                    dve.wait_ge(vhi_ready, l * (NPAIR + H) + it + (NPAIR + 1))
                    v.tensor_tensor(v_lo[:, :, 0:V], PS[:, 1, :].rearrange("p (a v) -> p a v", v=V),
                                    v_hi[:, :, 0:V].bitcast(F32), ALU.subtract).then_inc(v_ready, 1)
                    dve.wait_ge(qkhi_ready, l * (2 * NPAIR + H) + it + (2 * NPAIR + 1))
                    v.tensor_tensor(qk_lo[:], conv[:], qk_hi[:].bitcast(F32), ALU.subtract).then_inc(qk_ready, 1)
                    split(gi, 5 + AHEAD)
                    dve.wait_ge(s_done, n + 1)
                    dve.wait_ge(w_masked, n * 2 + 2)
                    v.tensor_tensor(S_f, PS[:, 3, 0:CAUSAL], wT, ALU.mult).then_inc(sf_ready, 1)
                    dve.wait_ge(shi_ready, n + 1)
                    v.tensor_tensor(S_lo, S_f, S_hi.bitcast(F32), ALU.subtract).then_inc(s_ready, 1)
                    split(gi, 6 + AHEAD)
                    dve.wait_ge(num_done, n + 1)
                    den = PS[:, 4:6, V:V + 1].rearrange("p a b -> p (a b)")
                    em = emcol[:, :, ds(it)].rearrange("p a b -> p (a b)")
                    link(v.tensor_scalar(st[:, 4, :], den, -1.0, None, ALU.mult))
                    link(v.tensor_tensor(st[:, 4, :], st[:, 4, :], den, ALU.max))
                    link(v.tensor_tensor(st[:, 4, :], st[:, 4, :], em, ALU.max))
                    v.reciprocal(st[:, 2, :], st[:, 4, :]).then_inc(r_ready, 1)
                    split(gi, 7 + AHEAD)
                    dve.wait_ge(sq_ready, n * 2 + 2)
                    link(v.tensor_scalar(st[:, 5, :], st[:, 3, :], 1.0 / V, EPS, ALU.mult, ALU.add))
                    rsqrt(st[:, 5, :], st[:, 7, :], st[:, 6, :])
                    link(v.tensor_tensor(st[:, 6, :], st[:, 5, :], st[:, 2, :], ALU.mult))
                    for t in range(TB):
                        v.tensor_scalar(hmn[:, t, :], PS[:, 4 + t, 0:V], st[:, 6, t:t + 1], None, ALU.mult
                                        ).then_inc(hmn_ready, 1)
                    split(gi, 8 + AHEAD)
                    for b in range(2):
                        dve.wait_ge(ada_used, l * (3 * KB) + (2 * KB + 2 + b) + it * 2)
                        ada_add(0, ds(it * 2 + b), b, (l * 12 + 8 + it + 1) * 16)
                    dve.wait_ge(hmt_done, n + 1)
                    dve.wait_ge(sigo_ready, n + 1)
                    for b in range(2):
                        ins = v.scalar_tensor_tensor(conv[:, b, :], PS[:, 6, b * T:(b + 1) * T],
                                                     par[:, ds(it * 2 + (NT * KB + KB + b))], mo_sb[:, b, :],
                                                     ALU.mult, ALU.mult)
                    ins.then_inc(hmf_ready, 1)
                    dve.wait_ge(hmhi_ready, n + 1)
                    v.tensor_tensor(hm_lo[:, ds(it * 2, 2), :], conv[:], hm_hi[:, ds(it * 2, 2), :].bitcast(F32),
                                    ALU.subtract).then_inc(hm_ready, 1)
                    assert steps.k == N_HEAD, steps.k
                n_ml = n_mid + H * N_HEAD
                steps.at(l * ND + n_ml)
                dve.wait_ge(ada_used, l * (3 * KB) + (3 * KB + 2))
                dve.sem_inc(acc_ready, 1)
                dve.wait_ge(ada_red, l * 3 + 3)
                factor(1, PS[:, 3, 0:KB])
                v.tensor_tensor(g2_sb[:], PS[:, 0:2, :].rearrange("p a b -> p (a b)"), g2_sb[:], ALU.add
                                ).then_inc(g_ready, 1)
                n_ada = n_ml + steps.k

                with dve.Fori(0, KB // 2) as it:
                    gi = g + g_pj + it * (PJ_U // RING)
                    steps.at(l * ND + n_ada + it * 4)
                    for b in range(2):
                        n = l * KB + it * 2 + b
                        split(gi, 2 * b + 1 + AHEAD)
                        split(gi, 2 * b + 2 + AHEAD)
                        dve.wait_ge(sg_ready, n * 2 + 2)
                        used(gi, 2 * b + 2)
                        dve.wait_ge(y_ready, n + 1)
                        link(v.tensor_tensor(y2, PS[:, 4 + b, 0:T], sig[:, 1, :], ALU.mult))
                        link(v.tensor_tensor(y1, PS[:, 4 + b, T:2 * T], sig[:, 0, :], ALU.mult))
                        v.tensor_tensor(y1, y1, y2, ALU.add).then_inc(yf_ready, 1)
                        dve.wait_ge(yhi_ready, n + 1)
                        v.tensor_tensor(h_lo[:, ds(it * 2 + b), :], y1.rearrange("p (a t) -> p a t", a=1),
                                        h_hi[:, ds(it * 2 + b), :].bitcast(F32), ALU.subtract).then_inc(y_ready, 1)
                n_pj = n_ada + KB // 2 * 4
                steps.at(l * ND + n_pj)
                for i in range(8):
                    split(g + g_out, i + 1 + AHEAD, E * KB if i + 1 + AHEAD == 9 else 1024)
                    if i % 4 == 3:
                        used(g + g_out, i + 1)
                        h = i // 4
                        for t in range(TB):
                            bank = (6 if h == 0 else 0) + t
                            link(v.tensor_tensor(h_full[:, t, :], PS[:, bank, :], g1_sb[:, h * 512:(h + 1) * 512],
                                                 ALU.mult))
                            v.tensor_tensor(x_sb[:, t, h * 512:(h + 1) * 512], x_sb[:, t, h * 512:(h + 1) * 512],
                                            h_full[:, t, :], ALU.add).then_inc(mix_added, 1)
                            dve.wait_ge(mix_added, l * 8 + (5 + 2 * h + t))
                split(g + g_out, 9 + AHEAD)
                norm(l * 2 + 1)
                modulated(l * 2 + 1, 1)
                split(g + g_out, 10 + AHEAD)

                dve.wait_ge(rt_ready, l * 1 + 1)
                for t in range(TB):
                    ins = v.tensor_tensor(sel[:, t, :], sc[:, t, :], rb[:], ALU.add)
                link(ins)
                hold(dve, dve_held)
                for t in range(TB):
                    for q in range(N_GROUPS):
                        ins = v.max(m8[:, t, q, :], sel[:, t, q * EG:(q + 1) * EG])
                link(ins)
                v.memset(gp[:, :, N_GROUPS:16], -FAR)
                link(v.tensor_tensor(gp[:, :, 0:N_GROUPS].rearrange("p a (b c) -> p a b c", c=1), m8[:, :, :, 0:1],
                                     m8[:, :, :, 1:2], ALU.add))
                hold(dve, dve_held)
                for t in range(TB):
                    ins = v.max(t8[:, t, :], gp[:, t, :])
                link(ins)
                link(v.memset(t8[:, :, TOPK_GROUPS:8], -FAR))
                hold(dve, dve_held)
                for t in range(TB):
                    ins = v.match_replace(gr[:, t, :], t8[:, t, :], gp[:, t, :], FAR)
                link(ins)
                link(v.tensor_tensor(gm[:, 0, :, :], gr[:, :, 0:N_GROUPS], gp[:, :, 0:N_GROUPS], ALU.not_equal))
                link(v.tensor_scalar(gm[:, 1, :, :], gm[:, 0, :, :], -1.0, -MASKED, ALU.add, ALU.mult))
                for t in range(TB):
                    for q in range(N_GROUPS):
                        e = slice(q * EG, (q + 1) * EG)
                        ins = v.tensor_scalar(sel[:, t, e], sel[:, t, e], gm[:, 0, t, q:q + 1], gm[:, 1, t, q:q + 1],
                                              ALU.mult, ALU.add)
                link(ins)
                hold(dve, dve_held)
                for t in range(TB):
                    ins = v.max(t8[:, t, :], sel[:, t, :])
                link(ins)
                hold(dve, dve_held)
                for t in range(TB):
                    ins = v.match_replace(rep[:, t, :], t8[:, t, :], sel[:, t, :], FAR)
                link(ins)
                link(v.tensor_tensor(rep[:], rep[:], sel[:], ALU.not_equal))
                link(v.tensor_tensor(gts[:], rep[:], sc[:], ALU.mult))
                link(v.tensor_reduce(st[:, 4, :], gts[:], AX.X, ALU.add))
                link(v.reciprocal(st[:, 5, :], st[:, 4, :]))
                for t in range(TB):
                    ins = v.tensor_scalar(gts[:, t, :], gts[:, t, :], st[:, 5, t:t + 1], ROUTED_SCALE,
                                          ALU.mult, ALU.mult)
                ins.then_inc(gts_ready, 1)

                def hidden(n, par, gate):
                    dve.wait_ge(silu_ready, n + 1)
                    ins = v.tensor_tensor(conv[:, par, :], sig[:, par, :], PS[:, 6 + par, T:2 * T], ALU.mult)
                    if gate is not None:
                        link(ins)
                        ins = v.tensor_tensor(conv[:, par, :], conv[:, par, :], gate_b[:, gate, :], ALU.mult)
                    ins.then_inc(hid_full, 1)
                    dve.wait_ge(hidhi_ready, n + 1)
                    v.tensor_tensor(hid_lo[:, par, :], conv[:, par, :], hid_hi[:, par, :].bitcast(F32),
                                    ALU.subtract).then_inc(hid_ready, 1)

                split(g + g_out, 11 + AHEAD)
                hidden(l * EV, 1, None)
                dve.wait_ge(gt_done, l * 1 + 1)
                v.tensor_copy(gT, PS[0:E, 5, 0:T]).then_inc(gT_ready, 1)
                n_moe = n_pj + steps.k
                with dve.Fori(0, E // EXP_IT) as it:
                    gi = g + g_moe + it * 3
                    steps.at(l * ND + n_moe + it * EXP_IT)
                    for e in range(EXP_IT):
                        split(gi, 3 * e + AHEAD)
                        split(gi, 3 * e + 1 + AHEAD)
                        if e % 2 == 0:
                            dve.wait_ge(gate_loaded[e // 2], (l * (E // EXP_IT) + it + 1) * 16)
                        hidden(l * EV + it * EXP_IT + (e + 1), e % 2, e)
                        split(gi, 3 * e + 2 + AHEAD)
                n_post = n_moe + E
                steps.at(l * ND + n_post)
                split(g + g_post, AHEAD)
                hidden(l * EV + (E + 1), 0, None)
                used(g + g_post, 3)
                for t in range(TB):
                    for h in range(2):
                        link(v.tensor_tensor(h_full[:, h, :], PS[:, 2 * t + h, :], g2_sb[:, h * 512:(h + 1) * 512],
                                             ALU.mult))
                        ins = v.tensor_tensor(x_sb[:, t, h * 512:(h + 1) * 512], x_sb[:, t, h * 512:(h + 1) * 512],
                                              h_full[:, h, :], ALU.add)
                        ins.then_inc(mix_added, 1)
                        dve.wait_ge(mix_added, l * 8 + (9 + 2 * t + h))
                total = n_post + steps.k
                assert total == ND, total
            steps.at(L * ND)
            rstd(L * 2)
            dve.wait_ge(par_loaded, (L * N_SMALL + 1) * 16)
            for t in range(TB):
                ins = v.scalar_tensor_tensor(x_sb[:, t, :], x_sb[:, t, :], st[:, 1, t:t + 1], g1_sb[:],
                                             ALU.mult, ALU.mult)
            ins.then_inc(out_ready, 1)

        @block.tensor
        def _(pe):
            mm = nc.tensor.matmul
            pe.sem_inc(unit_used, RING)
            pe.wait_ge(consts, N_CONST)

            def three(out, a, b, start, stop, check=False):
                mm(out, a[0], b[0], start=start, stop=False, skip_group_check=True)
                mm(out, a[0], b[1], start=False, stop=False, skip_group_check=True)
                return mm(out, a[1], b[0], start=False, stop=stop, skip_group_check=True)

            def unit(g, i, n, nk=KB):
                pe.wait_ge(lo_ready, g * RING + (i + 1 + RING))
                s = i % RING
                return [w[:, s, 0:nk * n].rearrange("p (k n) -> p k n", n=n) for w in (w_hi, w_lo)]

            def feat_major(g, i, out, rhs=None):
                w = unit(g, i, P)
                rh, rl = rhs or (h_hi, h_lo)
                for k in range(KB):
                    ins = three(out, (w[0][:, k, :], w[1][:, k, :]), (rh[:, k, :], rl[:, k, :]), k == 0, k == KB - 1)
                ins.then_inc(unit_used, 1)

            def turn(n):
                for t in range(TB):
                    pe.wait_ge(xn_ready, n * 2 + (t + 1))
                    for k in range(KB):
                        col = (k % 2) * T + t * P
                        ins = nc.tensor.transpose(PS[:, k // 2, col:col + P], xn[:, t, k:D:KB], ident[:])
                        if t == 1 and k % 2:
                            ins.then_inc(tr_done, 1)

            def ones_cols(off, out_col, bank):
                for k in range(KB):
                    ins = mm(PS[:, bank, out_col + k:out_col + k + 1], ada_acc[:, off + k:off + D:KB], ones[:, 0:1],
                             start=True, stop=True, skip_group_check=True)
                return ins

            def ones_rows(off, bank):
                for h in range(2):
                    ins = mm(PS[:, bank + h, :], ones[:], ada_acc[:, off + h * 512:off + (h + 1) * 512],
                             start=True, stop=True, skip_group_check=True)
                return ins

            with pe.Fori(0, L) as l:
                g = l * GL
                turn(l * 2)
                pe.wait_ge(par_loaded, (l + 1) * (N_SMALL * 16))
                hold(pe, pe_held)
                nc.tensor.transpose(PS[:, 6, 0:NROW], par_rows[:], ident[0:NROW, 0:NROW]).then_inc(par_t, 1)
                pe.wait_ge(acc_ready, l * 3 + 1)
                ones_cols(0, 0, 7)
                ones_cols(D, KB, 7).then_inc(ada_red, 1)
                pe.wait_ge(h_ready, l * 8 + 4)
                w = unit(g, 0, 2 * H)
                for a in range(2):
                    for k in range(KB):
                        ins = three(PS[0:H, 4, a * T:(a + 1) * T],
                                    (w[0][:, k, a * H:(a + 1) * H], w[1][:, k, a * H:(a + 1) * H]),
                                    (h_hi[:, k, :], h_lo[:, k, :]), k == 0, k == KB - 1)
                ins.then_inc(unit_used, 1)

                with pe.Fori(0, NPAIR // PAIRS_IT) as it:
                    gi = g + g_sb + it * (SB_U // RING)
                    pr = l * NPAIR + it * PAIRS_IT

                    def scores(n, j):
                        pe.wait_ge(qk_ready, l * (NPAIR + H) + (it * PAIRS_IT + j) + 1)
                        for a in range(2):
                            q = slice(a * DH, (a + 1) * DH)
                            bank = 4 + 2 * (j % 2) + a
                            for s in range(TB):
                                o = PS[:, bank, s * T:s * T + T - s * P]
                                three(o, (qk_hi[q, 1, s * P:(s + 1) * P], qk_lo[q, 1, s * P:(s + 1) * P]),
                                      (qk_hi[q, 0, s * P:T], qk_lo[q, 0, s * P:T]), s == 0, False)
                                ins = mm(PS[:, bank, s * T:s * T + P], ident_r[:], negmask[:], start=False, stop=False,
                                         skip_group_check=True)
                        ins.then_inc(z_done, 1)

                    def sums(n, j):
                        pe.wait_ge(splo_ready, n + 1)
                        for a in range(2):
                            bank = 4 + 2 * (j % 2) + a
                            for w in (sp_hi, sp_lo):
                                mm(PS[:, bank, 0:T], negtri[:], w[:, a, 0:T], start=False, stop=False, skip_group_check=True)
                                mm(PS[:, bank, T:CAUSAL], negtri[:], w[:, a, T:CAUSAL], start=False, stop=False,
                                   skip_group_check=True)
                                ins = mm(PS[:, bank, P:T], negones[:], w[:, a, T:CAUSAL], start=False, stop=w is sp_lo,
                                         skip_group_check=True)
                        ins.then_inc(l_done, 1)

                    def values(n, j):
                        pe.wait_ge(attlo_ready, n + 1)
                        for a in range(2):
                            o = PS[:, 3, a * T:(a + 1) * T]
                            three(o, (sv_hi[:, j % 2, 0, :], sv_lo[:, j % 2, 0, :]),
                                  (att_hi[:, a, 0:T], att_lo[:, a, 0:T]), True, False)
                            ins = three(o[:, P:T], (sv_hi[:, j % 2, 1, :], sv_lo[:, j % 2, 1, :]),
                                        (att_hi[:, a, T:CAUSAL], att_lo[:, a, T:CAUSAL]), False, True)
                        ins.then_inc(av_done, 1)

                    for j in range(PAIRS_IT):
                        n = pr + j
                        feat_major(gi, 4 * j + 1, PS[:, 0, 0:T])
                        feat_major(gi, 4 * j + 2, PS[:, 0, T:2 * T])
                        if j:
                            sums(n - 1, j - 1)
                        w = unit(gi, 4 * j + 3, P)
                        for t in range(TB):
                            for k in range(KB):
                                ins = three(PS[:, 1, t * P:(t + 1) * P],
                                            (h_hi[:, k, t * P:(t + 1) * P], h_lo[:, k, t * P:(t + 1) * P]),
                                            (w[0][:, k, :], w[1][:, k, :]), k == 0, k == KB - 1)
                        ins.then_inc(unit_used, 1)
                        scores(n, j)
                        feat_major(gi, 4 * j + 4, PS[:, 2, 0:T])
                        if j:
                            values(n - 1, j - 1)
                    sums(pr + (PAIRS_IT - 1), PAIRS_IT - 1)
                    values(pr + (PAIRS_IT - 1), PAIRS_IT - 1)

                pe.wait_ge(row_v, l * 3 + 4)
                hold(pe, pe_held)
                for r, row in enumerate((0, 2)):
                    for t in range(TB):
                        nc.tensor.transpose(PS[:, 1, (r * TB + t) * H:(r * TB + t + 1) * H],
                                            row_keep[row][:, t * P:(t + 1) * P], ident[0:H, 0:H])
                for h in range(H):
                    ins = mm(PS[:, 6 + h // 2, (h % 2) * T:(h % 2 + 1) * T], head_sel[:, h, :], row_keep[1],
                             start=True, stop=True, skip_group_check=True)
                ins.then_inc(rows_t, 1)
                pe.wait_ge(acc_ready, l * 3 + 2)
                pe.wait_ge(cols_ready, l * 1 + 1)
                ones_cols(D, 64, 1)
                ones_rows(0, 4).then_inc(ada_red, 1)

                with pe.Fori(0, H) as it:
                    gi = g + g_ml + it * (ML_U // RING)
                    n = l * H + it
                    feat_major(gi, 1, PS[:, 0, 0:T])
                    feat_major(gi, 2, PS[:, 0, T:2 * T])
                    pe.wait_ge(g_ready, l * 2 + 1)
                    for q in range(2):
                        w = unit(gi, 3 + q, V, 4)
                        for t in range(TB):
                            for k in range(4):
                                kk = 4 * q + k
                                ins = three(PS[:, 1, t * V:(t + 1) * V],
                                            (h_hi[:, kk, t * P:(t + 1) * P], h_lo[:, kk, t * P:(t + 1) * P]),
                                            (w[0][:, k, :], w[1][:, k, :]), kk == 0 and t == 0, kk == KB - 1)
                        ins.then_inc(unit_used, 1)
                    feat_major(gi, 5, PS[:, 2, 0:T])
                    pe.wait_ge(qk_ready, l * (NPAIR + H) + it + (NPAIR + 1))
                    for s in range(TB):
                        b = slice(s * P, (s + 1) * P)
                        ins = three(PS[:, 3, s * T:s * T + T - s * P], (qk_hi[:, 1, b], qk_lo[:, 1, b]),
                                    (qk_hi[:, 0, s * P:T], qk_lo[:, 0, s * P:T]), True, True)
                    ins.then_inc(s_done, 1)
                    feat_major(gi, 6, PS[:, 2, T:2 * T])
                    pe.wait_ge(v_ready, l * (NPAIR + H) + it + (NPAIR + 1))
                    pe.wait_ge(s_ready, n + 2)
                    for t in range(TB):
                        for s in range(t + 1):
                            col = t * P if s == 0 else T
                            ins = three(PS[:, 4 + t, 0:VA], (S_hi[:, col:col + P], S_lo[:, col:col + P]),
                                        (v_hi[:, s, :], v_lo[:, s, :]), s == 0, s == t)
                    ins.then_inc(num_done, 1)
                    pe.wait_ge(mb_ready, l * 1 + 1)
                    feat_major(gi, 7, PS[:, 7, 0:T])
                    feat_major(gi, 8, PS[:, 7, T:2 * T])
                    for t in range(TB):
                        pe.wait_ge(hmn_ready, n * 2 + (t + 1))
                        for b in range(2):
                            ins = nc.tensor.transpose(PS[:, 6, b * T + t * P:b * T + (t + 1) * P],
                                                      hmn[:, t, b * P:(b + 1) * P], ident[:])
                    ins.then_inc(hmt_done, 1)

                pe.wait_ge(acc_ready, l * 3 + 3)
                ones_cols(0, 0, 3)
                ones_rows(D, 0).then_inc(ada_red, 1)

                with pe.Fori(0, KB // 2) as it:
                    gi = g + g_pj + it * (PJ_U // RING)
                    for b in range(2):
                        pe.wait_ge(yf_ready, l * KB + it * 2 + (b + 1))
                        feat_major(gi, 2 * b + 1, PS[:, 4 + b, 0:T], (hs_hi, hs_lo))
                        pe.wait_ge(hm_ready, l * H + (H + 1))
                        feat_major(gi, 2 * b + 2, PS[:, 4 + b, T:2 * T], (hm_hi, hm_lo))

                pe.wait_ge(g_ready, l * 2 + 2)
                pe.wait_ge(y_ready, l * KB + (KB + 1))
                for i in range(8):
                    w = unit(g + g_out, i + 1, 512, 2)
                    q = i % 4
                    for t in range(TB):
                        bank = (6 if i < 4 else 0) + t
                        for k in range(2):
                            kk = 2 * q + k
                            ins = three(PS[:, bank, :], (h_hi[:, kk, t * P:(t + 1) * P], h_lo[:, kk, t * P:(t + 1) * P]),
                                        (w[0][:, k, :], w[1][:, k, :]), kk == 0, kk == KB - 1)
                    ins.then_inc(unit_used, 1)
                turn(l * 2 + 1)
                pe.wait_ge(h_ready, l * 8 + 8)
                w = unit(g + g_out, 9, E)
                for t in range(TB):
                    for k in range(KB):
                        ins = three(PS[:, 4, t * E:(t + 1) * E],
                                    (h_hi[:, k, t * P:(t + 1) * P], h_lo[:, k, t * P:(t + 1) * P]),
                                    (w[0][:, k, :], w[1][:, k, :]), k == 0, k == KB - 1)
                ins.then_inc(unit_used, 1)

                def hidden(g, i, par):
                    feat_major(g, i, PS[:, 6 + par, 0:T])
                    feat_major(g, i + 1, PS[:, 6 + par, T:2 * T])

                def down(g, i, n, par, stop=False):
                    w = unit(g, i, 512, 2)
                    pe.wait_ge(hid_ready, n + 1)
                    for t in range(TB):
                        for h in range(2):
                            ins = three(PS[:, 2 * t + h, :],
                                        (hid_hi[:, par, t * P:(t + 1) * P], hid_lo[:, par, t * P:(t + 1) * P]),
                                        (w[0][:, h, :], w[1][:, h, :]), False, stop)
                    ins.then_inc(unit_used, 1)
                    return ins

                hidden(g + g_out, 10, 1)
                for b in range(4):
                    mm(PS[:, b, :], zeros_r[:], h_hi[:, 0:2, :].rearrange("p a b -> p (a b)"), start=True, stop=False,
                       skip_group_check=True)
                pe.wait_ge(gts_ready, l * 1 + 1)
                hold(pe, pe_held)
                for t in range(TB):
                    ins = nc.tensor.transpose(PS[0:E, 5, t * P:(t + 1) * P], gts[:, t, :], ident[:])
                ins.then_inc(gt_done, 1)
                with pe.Fori(0, E // EXP_IT) as it:
                    gi = g + g_moe + it * 3
                    for e in range(EXP_IT):
                        hidden(gi, 3 * e, e % 2)
                        down(gi, 3 * e + 2, l * EV + it * EXP_IT + e, 1 - e % 2)
                hidden(g + g_post, 0, 0)
                down(g + g_post, 2, l * EV + E, 1)
                down(g + g_post, 3, l * EV + (E + 1), 0, True)


_INS = ["x", "c", "ada_w", "ada_b", "norm1_w", "w_in", "conv_w", "conv_b", "m_igate_b", "m_fgate_b", "m_norm_w",
        "w_proj_a", "w_proj_b", "w_out", "norm2_w", "router_w", "router_b", "w_gate", "w_up", "w_down",
        "sh_gate", "sh_up", "sh_down", "final_norm_w"]


def kernel(**inputs):
    import numpy as _np
    import concourse.bacc as _bacc
    from concourse import mybir as _mybir
    from concourse.bass_utils import run_bass_kernel_spmd as _run

    nc = _bacc.Bacc("TRN2", target_bir_lowering=False, num_devices=1)
    arrays, args = {}, []
    for name in _INS:
        a = _np.ascontiguousarray(inputs[name])
        arrays[f"in_{name}_dram"] = a
        args.append(nc.dram_tensor(f"in_{name}_dram", a.shape, _mybir.dt.from_np(a.dtype), kind="ExternalInput").ap())
    tokens, experts = inputs["x"].shape[1], inputs["router_w"].shape[2]
    gates = nc.dram_tensor("gates_dram", (experts, tokens), _mybir.dt.float32, kind="Internal").ap()
    out = nc.dram_tensor("out_dram", inputs["x"].shape, _mybir.dt.float32, kind="ExternalOutput").ap()
    trunk(nc, *args, gates, out)
    r = _run(nc, [arrays], core_ids=[0])
    return r.results[0]["out_dram"]
```

```python
from contextlib import ExitStack

import concourse.bass as bass
from concourse import mybir

F32 = mybir.dt.float32
F32R = mybir.dt.float32r
ALU = mybir.AluOpType
ACT = mybir.ActivationFunctionType
AX = mybir.AxisListType

P = 128
EPS = 1e-6
ROUTED_SCALE = 2.5
TOP_K, TOPK_GROUPS, N_GROUPS = 8, 4, 8
RING = 4
AHEAD = RING - 1
MASKED = -1e30
FAR = 3e38
N_SMALL = 11
N_CONST = 17
N_HEAD = 22
STEPS = 227
LEXP = "natural_log_exp_and_others"


def ds(i, n=1):
    return bass.ds(i, n)


def hold(eng, sem):
    eng.sem_inc(sem, 1)


class Steps:

    def __init__(self, eng, sem, per_layer):
        self.eng, self.sem, self.per_layer = eng, sem, per_layer
        self.base, self.k = 0, 0

    def at(self, base):
        self.base, self.k = base, 0

    def count(self, ins):
        self.k += 1
        ins.then_inc(self.sem, 1)

    def wait_for(self, k):
        self.eng.wait_ge(self.sem, self.base + k)

    def link(self, ins):
        self.count(ins)
        self.wait_for(self.k)


def trunk(nc, x, c, ada_w, ada_b, norm1_w, w_in, conv_w, conv_b, m_igate_b, m_fgate_b, m_norm_w,
          w_proj_a, w_proj_b, w_out, norm2_w, router_w, router_b, w_gate, w_up, w_down,
          sh_gate, sh_up, sh_down, final_norm_w, gates_dram, out):
    _, T, D = x.shape
    L = ada_w.shape[0]
    TB, KB = T // P, D // P
    E, FF = w_gate.shape[1], w_gate.shape[3]
    H = m_igate_b.shape[1]
    QK = conv_w.shape[2] // (2 * H)
    V = w_proj_a.shape[1] // H
    DH = 64
    NPAIR = D // (2 * DH)
    NT = conv_w.shape[1]
    assert TB == 2 and KB == 8 and QK == P and V == 2 * P and FF == P and E % 4 == 0 and NPAIR == 8
    sizes = [H * QK, H * QK, H * V, H * V, H, H, D, D, D, D, D]
    MQ, MK, MV, MO, MI, MF, SQ, SK, SV, GA, GB = [sum(sizes[:i]) for i in range(11)]
    EG = E // N_GROUPS
    CAUSAL = T + P

    PAIRS_IT, SB_U = 4, 16
    SBQ = [1, 4, 8, 12]
    ML_U = 8
    PJ_U = 4
    EXP_IT = 4
    g_sb = 0
    g_ml = g_sb + NPAIR // PAIRS_IT * SB_U // RING
    g_pj = g_ml + H * ML_U // RING
    g_out = g_pj + KB // 2 * PJ_U // RING
    g_moe = g_out + 3
    g_post = g_moe + E * 3 // RING
    GL = g_post + 1
    NVAL = NPAIR // 2 + H

    with ExitStack() as ctx:
        def sb(name, shape, dt=F32):
            return ctx.enter_context(nc.sbuf_tensor(name, shape, dt))

        def sem(name):
            return ctx.enter_context(nc.semaphore(name))

        PS = ctx.enter_context(nc.psum_tensor("PS", [P, 8, 512], F32))

        raw = sb("raw", [P, RING, 1024])
        w_hi = sb("w_hi", [P, RING, 1024], F32R)
        w_lo = sb("w_lo", [P, RING, 1024], F32R)
        ada_raw = sb("ada_raw", [P, 2, 2 * D])
        ada_acc = sb("ada_acc", [P, 2 * D])
        x_sb = sb("x_sb", [P, TB, D])
        h_hi = sb("h_hi", [P, KB, T], F32R)
        h_lo = sb("h_lo", [P, KB, T], F32R)
        hm_hi = sb("hm_hi", [P, KB, T], F32R)
        hm_lo = sb("hm_lo", [P, KB, T], F32R)
        hs_hi = sb("hs_hi", [P, KB, T], F32R)
        hs_lo = sb("hs_lo", [P, KB, T], F32R)
        ga_sb = sb("ga_sb", [P, KB, T])
        gb_sb = sb("gb_sb", [P, KB, T])
        xn = ga_sb[:].rearrange("p a b -> p (a b)").rearrange("p (t d) -> p t d", t=TB)
        g1_sb = sb("g1_sb", [P, D])
        g2_sb = sb("g2_sb", [P, D])
        ada0_raw = [ada_raw[:, 0, :], ada_raw[:, 1, :], gb_sb[:].rearrange("p a b -> p (a b)")]
        h_full = gb_sb[:, 0:4, :].rearrange("p (a b) t -> p a (b t)", a=2)
        zt = sb("zt", [P, 2, CAUSAL])
        sp = sb("sp", [P, 2, CAUSAL])
        sp_hi = sb("sp_hi", [P, 2, CAUSAL], F32R)
        sp_lo = sb("sp_lo", [P, 2, CAUSAL], F32R)
        att = sb("att", [P, 2, CAUSAL])
        att_hi = sb("att_hi", [P, 2, CAUSAL], F32R)
        att_lo = sb("att_lo", [P, 2, CAUSAL], F32R)
        qk_hi = sb("qk_hi", [P, 2, T], F32R)
        qk_lo = sb("qk_lo", [P, 2, T], F32R)
        VA = V + 2
        v_hi = sb("v_hi", [P, TB, VA], F32R)
        v_lo = sb("v_lo", [P, TB, VA], F32R)
        sv_hi = sb("sv_hi", [P, TB, 2 * P], F32R)
        sv_lo = sb("sv_lo", [P, TB, 2 * P], F32R)
        qk_pad = sb("qk_pad", [P, 2, NT - 1 + T])
        conv = sb("conv", [P, 2, T])
        sig = sb("sig", [P, 2, T])
        mo_sb = sb("mo_sb", [P, 2, T])
        M_sb = sb("M_sb", [P, H, T])
        assert H == EXP_IT
        gate_b = M_sb
        ident = sb("ident", [P, P])
        ident_r = sb("ident_r", [P, P], F32R)
        ones = sb("ones", [P, P])
        negmask = sb("negmask", [P, P], F32R)
        negtri = sb("negtri", [P, P], F32R)
        negones = sb("negones", [P, P], F32R)
        zeros_r = sb("zeros_r", [P, P], F32R)
        head_sel = sb("head_sel", [H, H, P])
        cond = sb("cond", [P, KB])
        c_sb = sb("c_sb", [P, 2, KB])
        NROW = NT * KB + 2 * KB
        par_rows = sb("par_rows", [NROW, P])
        par = sb("par", [P, NROW])
        bcol = sb("bcol", [P, 4, KB])
        nw = sb("nw", [P, 2, KB])
        ab = sb("ab", [P, 2, 2, KB])
        gbias = sb("gbias", [H, 2])
        ucol = sb("ucol", [P, TB, H])
        emcol = sb("emcol", [P, TB, H])
        st = sb("st", [P, 8, 2])
        rb = sb("rb", [P, E])
        sc = sb("sc", [P, TB, E])
        sel = sb("sel", [P, TB, E])
        rep = sb("rep", [P, TB, E])
        gts = sb("gts", [P, TB, E])
        m8 = sb("m8", [P, TB, N_GROUPS, 8])
        gp = sb("gp", [P, TB, 16])
        gr = sb("gr", [P, TB, 16])
        t8 = sb("t8", [P, TB, 8])
        gm = sb("gm", [P, 2, TB, N_GROUPS])
        gT = mo_sb[0:E, 0, :]
        row_keep = [conv[0:H, 0, :], conv[0:H, 1, :], mo_sb[0:H, 1, :]]

        rows = [sp[0:H, 0, 0:T], att[0:H, 0, 0:T], sp[0:H, 1, 0:T], att[0:H, 1, 0:T],
                zt[0:H, 0, 0:T], zt[0:H, 1, 0:T]]
        r_i, r_f, r_b, r_m, r_t, r_e = rows
        w_s0, w_s1 = M_sb, att[:].rearrange("p a b -> p (a b)")[:, 0:H * P].rearrange("p (h t) -> p h t", h=H)
        S_f, S_hi, S_lo = sp[:, 0, :], sp_hi[:, 0, :], sp_lo[:, 0, :]
        hmn = zt[:, :, 0:V]
        y1, y2 = sp[:, 0, 0:T], sp[:, 1, 0:T]
        hid_hi, hid_lo = qk_hi, qk_lo

        raw_loaded = [sem(f"raw_loaded{i}") for i in range(RING)]
        hi_ready = sem("hi_ready")
        lo_ready = sem("lo_ready")
        unit_used = sem("unit_used")
        x_loaded = sem("x_loaded")
        c_loaded = sem("c_loaded")
        par_loaded = sem("par_loaded")
        ada_loaded = sem("ada_loaded")
        ada_summed = sem("ada_summed")
        ada_scaled = sem("ada_scaled")
        ada_zero = sem("ada_zero")
        ada0_loaded = [sem(f"ada0_loaded{i}") for i in range(3)]
        ada0_used = sem("ada0_used")
        adan_loaded = sem("adan_loaded")
        adan_used = sem("adan_used")
        g2_loaded = sem("g2_loaded")
        consts = sem("consts")
        ss_done = sem("ss_done")
        xn_ready = sem("xn_ready")
        tr_done = sem("tr_done")
        hf_ready = sem("hf_ready")
        hhi_ready = sem("hhi_ready")
        h_ready = sem("h_ready")
        par_t = sem("par_t")
        par_ready = sem("par_ready")
        acc_ready = sem("acc_ready")
        ada_red = sem("ada_red")
        ab_ready = sem("ab_ready")
        row_a = sem("row_a")
        row_v = sem("row_v")
        rows_t = sem("rows_t")
        cols_ready = sem("cols_ready")
        mb_ready = sem("mb_ready")
        g_ready = sem("g_ready")
        qkhi_ready = sem("qkhi_ready")
        qk_ready = sem("qk_ready")
        vhi_ready = sem("vhi_ready")
        v_ready = sem("v_ready")
        z_done = sem("z_done")
        ln_ready = sem("ln_ready")
        sp_ready = sem("sp_ready")
        sphi_ready = sem("sphi_ready")
        splo_ready = sem("splo_ready")
        l_done = sem("l_done")
        att_ready = sem("att_ready")
        atthi_ready = sem("atthi_ready")
        attlo_ready = sem("attlo_ready")
        av_done = sem("av_done")
        hshi_ready = sem("hshi_ready")
        hs_ready = sem("hs_ready")
        g_evac = sem("g_evac")
        pad_ready = sem("pad_ready")
        conv_ready = sem("conv_ready")
        sig_ready = sem("sig_ready")
        qkf_ready = sem("qkf_ready")
        w_ready = sem("w_ready")
        w_masked = sem("w_masked")
        s_done = sem("s_done")
        sf_ready = sem("sf_ready")
        shi_ready = sem("shi_ready")
        s_ready = sem("s_ready")
        num_done = sem("num_done")
        r_ready = sem("r_ready")
        sq_ready = sem("sq_ready")
        hmn_ready = sem("hmn_ready")
        sigo_ready = sem("sigo_ready")
        hmt_done = sem("hmt_done")
        hmf_ready = sem("hmf_ready")
        hmhi_ready = sem("hmhi_ready")
        hm_ready = sem("hm_ready")
        sg_ready = sem("sg_ready")
        yf_ready = sem("yf_ready")
        yhi_ready = sem("yhi_ready")
        y_ready = sem("y_ready")
        mix_added = sem("mix_added")
        rt_ready = sem("rt_ready")
        gts_ready = sem("gts_ready")
        gt_done = sem("gt_done")
        gT_ready = sem("gT_ready")
        gT_stored = sem("gT_stored")
        gate_loaded = [sem("gate_loaded0"), sem("gate_loaded1")]
        silu_ready = sem("silu_ready")
        hid_full = sem("hid_full")
        hidhi_ready = sem("hidhi_ready")
        hid_ready = sem("hid_ready")
        out_ready = sem("out_ready")
        stored = sem("stored")
        dve_step = sem("dve_step")
        pool_held, pe_held, dve_held = sem("pool_held"), sem("pe_held"), sem("dve_held")

        EV = E + 2
        ND = STEPS
        block = ctx.enter_context(nc.Block())

        def dram_rows(w, l):
            return w[ds(l)].rearrange("o a b -> (o a) b")

        @block.sync
        def _(sp_e):
            sp_e.dma_start(x_sb[:], x.rearrange("o (t p) d -> p (o t) d", p=P)).then_inc(x_loaded, 16)

            def load(src, g, i, width=1024):
                sp_e.wait_ge(lo_ready, g * RING + i + 1)
                sp_e.dma_start(raw[:, i % RING, 0:width].rearrange("p (k n) -> p k n", n=src.shape[-1]),
                               src).then_inc(raw_loaded[i % RING], 16)

            def cols(w, l, col, n=P, k0=0, nk=KB):
                v = w[ds(l), :, ds(col, n)].rearrange("o (p k) n -> (o p) k n", k=KB)
                return v[:, k0:k0 + nk, :]

            def cols_std(w, l, col, n=P, k0=0, nk=KB):
                v = w[ds(l), k0 * P:(k0 + nk) * P, ds(col, n)]
                return v.rearrange("o (k p) n -> (o p) k n", p=P)

            for k in range(KB):
                if k >= 3:
                    sp_e.wait_ge(ada0_used, k - 2)
                sp_e.dma_start(ada0_raw[k % 3], ada_w[0:1, :, 0:2 * D].rearrange("o (p k) n -> (o p) k n", k=KB)[:, k, :]
                               ).then_inc(ada0_loaded[k % 3], 16)

            with sp_e.Fori(0, L) as l:
                g = l * GL
                load(cols(w_in, l, MI, 2 * H), g, 0, 2 * H * KB)
                with sp_e.Fori(0, NPAIR // PAIRS_IT) as it:
                    gi = g + g_sb + it * (SB_U // RING)
                    col = it * (PAIRS_IT * P)
                    for j in range(PAIRS_IT):
                        load(cols(w_in, l, col + (SQ + j * P)), gi, SBQ[j])
                        load(cols(w_in, l, col + (SK + j * P)), gi, SBQ[j] + 1)
                        load(cols(w_in, l, col + (SV + j // 2 * 2 * P), 2 * P, j % 2 * 4, 4), gi, SBQ[j] + 2)
                        if j:
                            load(cols(w_in, l, col + (GA + (j - 1) * P)), gi, SBQ[j] + 3)
                    load(cols(w_in, l, col + (GA + (PAIRS_IT - 1) * P)), gi, SB_U)
                with sp_e.Fori(0, H) as it:
                    gi = g + g_ml + it * (ML_U // RING)
                    load(cols(w_in, l, it * QK + MQ), gi, 1)
                    load(cols(w_in, l, it * QK + MK), gi, 2)
                    load(cols(w_in, l, it * V + MV, V, 0, 4), gi, 3)
                    load(cols(w_in, l, it * V + MV, V, 4, 4), gi, 4)
                    load(cols(w_in, l, it * V + MO), gi, 5)
                    load(cols(w_in, l, it * V + (MO + P)), gi, 6)
                    load(cols(w_in, l, it * V + GB), gi, 7)
                    load(cols(w_in, l, it * V + (GB + P)), gi, 8)
                with sp_e.Fori(0, KB // 2) as it:
                    gi = g + g_pj + it * (PJ_U // RING)
                    for n in range(2):
                        load(cols_std(w_proj_b, l, it * (2 * P) + n * P), gi, 1 + 2 * n)
                        load(cols_std(w_proj_a, l, it * (2 * P) + n * P), gi, 2 + 2 * n)
                for n in range(8):
                    load(cols_std(w_out, l, (n // 4) * 512, 512, 2 * (n % 4), 2), g + g_out, 1 + n)
                load(cols(router_w, l, 0, E), g + g_out, 9, E * KB)

                def expert_in(w, l, e):
                    return w[ds(l), ds(e)].rearrange("o q (p k) f -> (o q p) k f", k=KB)

                def expert_out(l, e):
                    return w_down[ds(l), ds(e)].rearrange("o q p (k d) -> (o q p) k d", d=D)

                def shared_out(l, b):
                    return sh_down[ds(l), b * P:(b + 1) * P].rearrange("o p (k d) -> (o p) k d", d=D)

                load(cols(sh_gate, l, 0), g + g_out, 10)
                load(cols(sh_up, l, 0), g + g_out, 11)

                def expert_units(e, gi, i, down):
                    load(expert_in(w_gate, l, e), gi, i)
                    load(expert_in(w_up, l, e), gi, i + 1)
                    load(down, gi, i + 2)

                expert_units(0, g + g_moe, 0, shared_out(l, 0))
                with sp_e.Fori(0, E // EXP_IT - 1) as it:
                    for n in range(EXP_IT):
                        expert_units(it * EXP_IT + (n + 1), g + g_moe + it * 3, 3 * (n + 1),
                                     expert_out(l, it * EXP_IT + n))
                for n in range(EXP_IT - 1):
                    e = E - EXP_IT + 1 + n
                    expert_units(e, g + g_moe + (E // EXP_IT - 1) * 3, 3 * (n + 1), expert_out(l, e - 1))
                load(cols(sh_gate, l, P), g + g_post, 0)
                load(cols(sh_up, l, P), g + g_post, 1)
                load(expert_out(l, E - 1), g + g_post, 2)
                load(shared_out(l, 1), g + g_post, 3)
            sp_e.wait_ge(out_ready, 1)
            sp_e.dma_start(out.rearrange("o (t p) d -> p (o t) d", p=P), x_sb[:]).then_inc(stored, 16)
            sp_e.wait_ge(stored, 16)

        @block.gpsimd
        def _(pool):
            pool.sem_inc(ada_summed, 2)
            pool.dma_start(c_sb[:, 0, :], c.rearrange("o (p k) -> (o p) k", k=KB)).then_inc(c_loaded, 16)
            ks = [0]

            def step(ins):
                ks[0] += 1
                ins.then_inc(consts, 1)
                pool.wait_ge(consts, ks[0])

            step(nc.gpsimd.memset(ones[:], 1.0))
            step(nc.gpsimd.memset(ident[:], 0.0))
            step(nc.gpsimd.affine_select(out=ident[:], in_=ident[:], compare_op=ALU.not_equal, fill=1.0,
                                         base=0, pattern=[[-1, P]], channel_multiplier=1))
            step(nc.gpsimd.tensor_copy(ident_r[:], ident[:]))
            f = sp[:, 0, 0:P]
            step(nc.gpsimd.memset(f, 0.0))
            step(nc.gpsimd.tensor_copy(zeros_r[:], f))
            step(nc.gpsimd.affine_select(out=f, in_=f, compare_op=ALU.is_gt, fill=MASKED,
                                         base=0, pattern=[[1, P]], channel_multiplier=-1))
            step(nc.gpsimd.tensor_copy(negmask[:], f))
            step(nc.gpsimd.memset(f, -1.0))
            step(nc.gpsimd.tensor_copy(negones[:], f))
            step(nc.gpsimd.affine_select(out=f, in_=f, compare_op=ALU.is_ge, fill=0.0,
                                         base=0, pattern=[[-1, P]], channel_multiplier=1))
            step(nc.gpsimd.tensor_copy(negtri[:], f))
            step(nc.gpsimd.memset(head_sel[:], 0.0))
            step(nc.gpsimd.affine_select(out=head_sel[:], in_=head_sel[:], compare_op=ALU.not_equal, fill=1.0,
                                         base=0, pattern=[[-1, H], [0, P]], channel_multiplier=1))
            step(nc.gpsimd.memset(v_lo[:].bitcast(F32), 0.0))
            step(nc.gpsimd.tensor_copy(v_hi[:, :, V:VA], ones[:, 0:4].rearrange("p (a b) -> p a b", b=2)))
            step(nc.gpsimd.memset(qk_pad[:], 0.0))

            def conditioning(l, part):
                pool.wait_ge(ada_red, l * 3 + part)
                hold(pool, pool_held)
                nc.gpsimd.memset(ada_acc[:], 0.0).then_inc(ada_zero, 1)
                pool.wait_ge(ada_zero, l * 3 + part)
                hold(pool, pool_held)
                with pool.Fori(0, KB // 2) as it:
                    n = l * KB + (part - 1) * (KB // 2) + it
                    pool.wait_ge(ada_summed, n * 2 + 2)
                    hold(pool, pool_held)
                    for j in range(2):
                        pool.dma_start(ada_raw[:, j, :],
                                       ada_w[ds(l), :, part * 2 * D:(part + 1) * 2 * D].rearrange(
                                           "o (p k) n -> (o p) k n", k=KB)[:, ds(it * 2 + j), :]).then_inc(ada_loaded, 16)
                    pool.wait_ge(ada_loaded, n * 32 + 32)
                    hold(pool, pool_held)
                    for j in range(2):
                        nc.gpsimd.tensor_tensor(ada_raw[:, j, :], ada_raw[:, j, :],
                                                cond[:, ds(it * 2 + j)].to_broadcast([P, 2 * D]), ALU.mult
                                                ).then_inc(ada_scaled, 1)
                    for j in range(2):
                        pool.wait_ge(ada_scaled, l * 16 + n * 2 + (j + 1))
                        pool.wait_ge(ada_summed, n * 2 + (j + 2))
                        hold(pool, pool_held)
                        nc.gpsimd.tensor_tensor(ada_acc[:], ada_acc[:], ada_raw[:, j, :], ALU.add).then_inc(ada_summed, 1)
                pool.wait_ge(ada_summed, l * 16 + (8 * part + 2))
                pool.sem_inc(acc_ready, 1)

            assert ks[0] == N_CONST, ks[0]
            with pool.Fori(0, L) as l:
                pool.wait_ge(adan_used, l * 16 + 1)
                pool.sem_inc(acc_ready, 1)
                small = []

                def load_small(dst, src):
                    small.append(pool.dma_start(dst, src).then_inc(par_loaded, 16))

                load_small(par_rows[0:NT * KB, :], conv_w[ds(l)].rearrange("o t (b p) -> (o t b) p", p=P))
                load_small(par_rows[NT * KB:NT * KB + KB, :], conv_b[ds(l), :].rearrange("o (b p) -> (o b) p", p=P))
                load_small(par_rows[NT * KB + KB:NROW, :], m_norm_w[ds(l), :].rearrange("o (b p) -> (o b) p", p=P))
                bv = ada_b[ds(l), :].rearrange("o (s p k) -> (o p) s k", k=KB, p=P)
                load_small(bcol[:, 0:2, :], bv[:, 0:2, :])
                load_small(bcol[:, 2:4, :], bv[:, 3:5, :])
                load_small(nw[:, 0, :], norm1_w[ds(l), :].rearrange("o (p k) -> (o p) k", k=KB))
                load_small(nw[:, 1, :], norm2_w[ds(l), :].rearrange("o (p k) -> (o p) k", k=KB))
                load_small(gbias[:, 0:1], m_igate_b[ds(l), :].rearrange("o h -> h o"))
                load_small(gbias[:, 1:2], m_fgate_b[ds(l), :].rearrange("o h -> h o"))
                load_small(g1_sb[:], ada_b[ds(l), 2 * D:3 * D].to_broadcast([P, D]))
                load_small(rb[:], router_b[ds(l), :].to_broadcast([P, E]))
                assert len(small) == N_SMALL
                pool.wait_ge(mix_added, l * 8 + 4)
                hold(pool, pool_held)
                pool.dma_start(g2_sb[:], ada_b[ds(l), 5 * D:6 * D].to_broadcast([P, D])).then_inc(g2_loaded, 16)
                conditioning(l, 1)
                pool.wait_ge(w_ready, l * (2 * H) + 2 * H)
                hold(pool, pool_held)
                for w in (w_s0[:, :, 0:P], w_s1):
                    nc.gpsimd.affine_select(out=w, in_=w, compare_op=ALU.is_ge, fill=0.0, base=0,
                                            pattern=[[0, H], [1, P]], channel_multiplier=-1).then_inc(w_masked, 1)
                conditioning(l, 2)
                pool.wait_ge(gT_ready, l * 1 + 1)
                hold(pool, pool_held)
                pool.dma_start(gates_dram, gT).then_inc(gT_stored, 16)
                pool.wait_ge(gT_stored, l * 16 + 16)
                hold(pool, pool_held)
                pool.wait_ge(ada_red, l * 3 + 3)
                hold(pool, pool_held)
                nc.gpsimd.memset(ada_acc[:], 0.0).then_inc(ada_zero, 1)
                pool.wait_ge(ada_zero, l * 3 + 3)
                hold(pool, pool_held)
                with pool.Fori(0, 2) as half, pool.Fori(0, KB) as k:
                    it = half * KB + k
                    for s in range(2):
                        pool.wait_ge(hid_full, l * EV + it * EXP_IT + (2 * s + 2))
                        hold(pool, pool_held)
                        src = gates_dram[ds(it * EXP_IT + 2 * s, 2), :].rearrange("(o e) t -> o (e t)", o=1).to_broadcast([P, 2 * T])
                        pool.dma_start(gate_b[:, 2 * s:2 * s + 2, :].rearrange("p e t -> p (e t)"), src
                                       ).then_inc(gate_loaded[s], 16)
                    with pool.If_lt(pool.to_reg(l), L - 1):
                        pool.wait_ge(adan_used, l * 16 + it + 1)
                        hold(pool, pool_held)
                        nl = nc.s_assert_within(l + 1, 0, L - 1,
                                                skip_runtime_bounds_check_because="l < L - 1 in this branch")
                        pool.dma_start(ada_raw[:, 0, 0:D],
                                       ada_w[ds(nl), :, ds(half * D, D)].rearrange(
                                           "o (p k) n -> (o p) k n", k=KB)[:, ds(k), :]).then_inc(adan_loaded, 16)
                        pool.wait_ge(adan_loaded, (l * 16 + it + 1) * 16)
                        hold(pool, pool_held)
                        nc.gpsimd.tensor_tensor(ada_raw[:, 0, 0:D], ada_raw[:, 0, 0:D],
                                                cond[:, ds(k)].to_broadcast([P, D]), ALU.mult).then_inc(ada_scaled, 1)
                        pool.wait_ge(ada_scaled, l * 32 + it + 17)
                        hold(pool, pool_held)
                        nc.gpsimd.tensor_tensor(ada_acc[:, ds(half * D, D)], ada_acc[:, ds(half * D, D)],
                                                ada_raw[:, 0, 0:D], ALU.add).then_inc(adan_used, 1)
            pool.wait_ge(mix_added, L * 8 + 4)
            pool.dma_start(g1_sb[:], final_norm_w.rearrange("(o d) -> o d", o=1).to_broadcast([P, D])
                           ).then_inc(par_loaded, 16)

        @block.scalar
        def _(act):
            act.wait_ge(c_loaded, 16)
            nc.scalar.activation(c_sb[:, 1, :], c_sb[:, 0, :], ACT.Sigmoid).then_inc(sig_ready, 1)

            def split(g, i, width=1024):
                act.wait_ge(unit_used, g * RING + i + 1)
                act.wait_ge(raw_loaded[i % RING], (g + i // RING + 1) * 16)
                nc.scalar.activation(w_hi[:, i % RING, 0:width], raw[:, i % RING, 0:width], ACT.Copy
                                     ).then_inc(hi_ready, 1)

            def used(g, i):
                act.wait_ge(unit_used, g * RING + (i + 1 + RING))

            def norm_in(n, whole=None):
                for t in range(TB):
                    if whole:
                        act.wait_ge(mix_added, whole[t])
                    nc.scalar.activation(xn[:, t, :], x_sb[:, t, :], ACT.Square,
                                         accum_out=st[:, 0, t:t + 1]).then_inc(ss_done, 1)

            def norm_hi(n):
                for b in range(4):
                    act.wait_ge(hf_ready, n * 4 + (b + 1))
                    nc.scalar.activation(h_hi[:, 2 * b:2 * b + 2, :], h_full[:, b % 2, :].rearrange(
                        "p (k t) -> p k t", t=T), ACT.Copy).then_inc(hhi_ready, 1)

            act.wait_ge(mix_added, 4)
            with act.Fori(0, L) as l:
                g = l * GL
                split(g, 0, 2 * H * KB)
                split(g, 1)
                split(g, 2)
                norm_in(l * 2, [l * 8 + 2, l * 8 + 4])
                norm_hi(l * 2)
                split(g, 3)
                nc.scalar.preload_act_table_set(LEXP)
                act.wait_ge(row_v, l * 3 + 3)
                nc.scalar.activation(r_t, r_t, ACT.Exp, scale=-1.0).then_inc(row_a, 1)
                act.wait_ge(row_a, l * 3 + 1)
                nc.scalar.activation(r_t, r_t, ACT.Ln, bias=1.0).then_inc(row_a, 1)
                act.wait_ge(row_v, l * 3 + 4)
                nc.scalar.activation(r_e, r_e, ACT.Exp, scale=-1.0).then_inc(row_a, 1)

                with act.Fori(0, NPAIR // PAIRS_IT) as it:
                    gi = g + g_sb + it * (SB_U // RING)
                    pr = l * NPAIR + it * PAIRS_IT

                    def att_part(n):
                        act.wait_ge(l_done, n + 1)
                        zb = PS[:, 4 + 2 * par2:6 + 2 * par2, 0:CAUSAL]
                        nc.scalar.activation(att[:], zb, ACT.Exp).then_inc(att_ready, 1)
                        act.wait_ge(att_ready, n + 1)
                        nc.scalar.activation(att_hi[:], att[:], ACT.Copy).then_inc(atthi_ready, 1)

                    def av_part(n, jj):
                        act.wait_ge(av_done, n + 1)
                        for a in range(2):
                            q = slice(a * DH, (a + 1) * DH)
                            nc.scalar.activation(hs_hi[q, ds(jj), :],
                                                 PS[q, 3:4, a * T:(a + 1) * T], ACT.Copy).then_inc(hshi_ready, 1)

                    def ga_part(i, jj, bank=2):
                        split(gi, i + AHEAD)
                        used(gi, i)
                        nc.scalar.activation(ga_sb[:, ds(jj), :], PS[:, bank:bank + 1, 0:T], ACT.Copy).then_inc(g_evac, 1)

                    for j in range(PAIRS_IT):
                        n, u = pr + j, SBQ[j]
                        split(gi, u + AHEAD)
                        split(gi, u + 1 + AHEAD)
                        used(gi, u + 1)
                        nc.scalar.activation(qk_hi[:, 0, :], PS[:, 0, 0:T], ACT.Copy, scale=DH ** -0.5
                                             ).then_inc(qkhi_ready, 1)
                        nc.scalar.activation(qk_hi[:, 1, :], PS[:, 0, T:2 * T], ACT.Copy).then_inc(qkhi_ready, 1)
                        if j:
                            par2 = (j - 1) % 2
                            att_part(n - 1)
                        split(gi, u + 2 + AHEAD)
                        if j % 2:
                            used(gi, u + 2)
                            nc.scalar.activation(sv_hi[:].rearrange("p a b -> p (a b)"), PS[:, 1, :], ACT.Copy
                                                 ).then_inc(vhi_ready, 1)
                        act.wait_ge(z_done, n + 1)
                        nc.scalar.activation(zt[:], PS[:, 4 + 2 * (j % 2):6 + 2 * (j % 2), 0:CAUSAL], ACT.Abs
                                             ).then_inc(ln_ready, 1)
                        act.wait_ge(ln_ready, n * 3 + 1)
                        nc.scalar.activation(zt[:], zt[:], ACT.Exp, scale=-1.0).then_inc(ln_ready, 1)
                        act.wait_ge(ln_ready, n * 3 + 2)
                        nc.scalar.activation(zt[:], zt[:], ACT.Ln, bias=1.0).then_inc(ln_ready, 1)
                        if j:
                            ga_part(u + 3, it * PAIRS_IT + (j - 1))
                            av_part(n - 1, it * PAIRS_IT + (j - 1))
                    par2 = (PAIRS_IT - 1) % 2
                    att_part(pr + (PAIRS_IT - 1))
                    ga_part(SB_U, it * PAIRS_IT + (PAIRS_IT - 1), 0)
                    av_part(pr + (PAIRS_IT - 1), it * PAIRS_IT + (PAIRS_IT - 1))

                act.wait_ge(rows_t, l * 1 + 1)
                nc.scalar.activation(M_sb[:].rearrange("p (a b) t -> p a (b t)", a=2), PS[:, 6:8, :], ACT.Copy
                                     ).then_inc(mb_ready, 1)

                act.wait_ge(mb_ready, l * 1 + 1)
                act.wait_ge(cols_ready, l * 2 + 1)
                for h in range(H):
                    nc.scalar.activation(w_s1[:, h, :], M_sb[:, h, P:T], ACT.Exp, bias=ucol[:, 1, h:h + 1],
                                         scale=-1.0).then_inc(w_ready, 1)
                act.wait_ge(w_ready, l * (2 * H) + H)
                for h in range(H):
                    nc.scalar.activation(w_s0[:, h, :], M_sb[:, h, :], ACT.Exp, bias=ucol[:, 0, h:h + 1],
                                         scale=-1.0).then_inc(w_ready, 1)

                with act.Fori(0, H) as it:
                    gi = g + g_ml + it * (ML_U // RING)
                    n = l * H + it
                    split(gi, 1 + AHEAD)
                    split(gi, 2 + AHEAD)
                    used(gi, 2)
                    nc.scalar.activation(qk_pad[:, :, NT - 1:NT - 1 + T], PS[:, 0, :].rearrange(
                        "p (a t) -> p a t", t=T), ACT.Copy).then_inc(pad_ready, 1)
                    split(gi, 3 + AHEAD)
                    act.wait_ge(conv_ready, n + 1)
                    nc.scalar.activation(sig[:], conv[:], ACT.Sigmoid).then_inc(sig_ready, 1)
                    used(gi, 4)
                    nc.scalar.activation(v_hi[:, :, 0:V], PS[:, 1, :].rearrange("p (a v) -> p a v", v=V), ACT.Copy
                                         ).then_inc(vhi_ready, 1)
                    act.wait_ge(qkf_ready, n + 1)
                    nc.scalar.activation(qk_hi[:], conv[:], ACT.Copy).then_inc(qkhi_ready, 1)
                    split(gi, 4 + AHEAD)
                    split(gi, 5 + AHEAD)
                    act.wait_ge(sf_ready, n + 1)
                    nc.scalar.activation(S_hi, S_f, ACT.Copy).then_inc(shi_ready, 1)
                    split(gi, 6 + AHEAD)
                    split(gi, 7 + AHEAD)
                    used(gi, 6)
                    nc.scalar.activation(mo_sb[:], PS[:, 2, :].rearrange("p (a t) -> p a t", t=T), ACT.Sigmoid
                                         ).then_inc(sigo_ready, 1)
                    act.wait_ge(r_ready, n + 1)
                    for t in range(TB):
                        nc.scalar.activation(hmn[:, t, :], PS[:, 4 + t, 0:V], ACT.Square, scale=st[:, 2, t:t + 1],
                                             accum_out=st[:, 3, t:t + 1]).then_inc(sq_ready, 1)
                    split(gi, 8 + AHEAD)
                    used(gi, 8)
                    nc.scalar.activation(gb_sb[:, ds(it * 2, 2), :], PS[:, 7, :].rearrange("p (a t) -> p a t", t=T),
                                         ACT.Copy).then_inc(g_evac, 1)
                    act.wait_ge(hmf_ready, n + 1)
                    nc.scalar.activation(hm_hi[:, ds(it * 2, 2), :], conv[:], ACT.Copy).then_inc(hmhi_ready, 1)

                with act.Fori(0, KB // 2) as it:
                    gi = g + g_pj + it * (PJ_U // RING)
                    for b in range(2):
                        n = l * KB + it * 2 + b
                        split(gi, 2 * b + 1 + AHEAD)
                        act.wait_ge(yf_ready, n + 2)
                        nc.scalar.activation(sig[:, 0, :], ga_sb[:, ds(it * 2 + b), :].rearrange("p a t -> p (a t)"),
                                             ACT.Sigmoid).then_inc(sg_ready, 1)
                        nc.scalar.activation(sig[:, 1, :], gb_sb[:, ds(it * 2 + b), :].rearrange("p a t -> p (a t)"),
                                             ACT.Sigmoid).then_inc(sg_ready, 1)
                        split(gi, 2 * b + 2 + AHEAD)
                        act.wait_ge(yf_ready, n + 3)
                        nc.scalar.activation(h_hi[:, ds(it * 2 + b), :], y1.rearrange("p (a t) -> p a t", a=1),
                                             ACT.Copy).then_inc(yhi_ready, 1)
                for i in range(8):
                    split(g + g_out, i + 1 + AHEAD, E * KB if i + 1 + AHEAD == 9 else 1024)
                split(g + g_out, 9 + AHEAD)
                norm_in(l * 2 + 1, [l * 8 + 7, l * 8 + 8])
                norm_hi(l * 2 + 1)
                used(g + g_out, 9)
                nc.scalar.activation(sc[:], PS[:, 4, 0:TB * E].rearrange("p (t e) -> p t e", e=E), ACT.Sigmoid
                                     ).then_inc(rt_ready, 1)
                split(g + g_out, 10 + AHEAD)

                def hidden(n, par, gi, i):
                    used(gi, i)
                    nc.scalar.activation(sig[:, par, :], PS[:, 6 + par, 0:T], ACT.Silu).then_inc(silu_ready, 1)
                    act.wait_ge(hid_full, n + 4)
                    nc.scalar.activation(hid_hi[:, par, :], conv[:, par, :], ACT.Copy).then_inc(hidhi_ready, 1)

                split(g + g_out, 11 + AHEAD)
                hidden(l * EV, 1, g + g_out, 11)
                with act.Fori(0, E // EXP_IT) as it:
                    gi = g + g_moe + it * 3
                    for e in range(EXP_IT):
                        split(gi, 3 * e + AHEAD)
                        split(gi, 3 * e + 1 + AHEAD)
                        hidden(l * EV + it * EXP_IT + (e + 1), e % 2, gi, 3 * e + 1)
                        split(gi, 3 * e + 2 + AHEAD)
                split(g + g_post, AHEAD)
                hidden(l * EV + (E + 1), 0, g + g_post, 1)
            act.wait_ge(mix_added, L * 8 + 4)
            norm_in(L * 2)

        @block.vector
        def _(dve):
            steps = Steps(dve, dve_step, ND)
            link = steps.link
            v = nc.vector
            dve.sem_inc(lo_ready, RING)
            dve.sem_inc(s_ready, 1)
            dve.sem_inc(yf_ready, 2)
            dve.sem_inc(hm_ready, 1)
            dve.sem_inc(y_ready, 1)
            dve.sem_inc(hid_full, 3)
            dve.wait_ge(x_loaded, 16)
            dve.sem_inc(mix_added, 4)
            dve.wait_ge(sig_ready, 1)
            v.tensor_tensor(cond[:], c_sb[:, 0, :], c_sb[:, 1, :], ALU.mult).then_inc(row_v, 1)
            dve.wait_ge(row_v, 1)
            v.memset(ada_acc[:], 0.0).then_inc(row_v, 1)
            dve.wait_ge(row_v, 2)
            for k in range(KB):
                dve.wait_ge(ada0_loaded[k % 3], (k // 3 + 1) * 16)
                v.scalar_tensor_tensor(ada_acc[:], ada0_raw[k % 3], cond[:, k:k + 1], ada_acc[:], ALU.mult, ALU.add
                                       ).then_inc(ada0_used, 1)
                dve.wait_ge(ada0_used, k + 1)
            dve.sem_inc(adan_used, 1)

            def split(g, i, width=1024):
                dve.wait_ge(hi_ready, g * RING + i + 1)
                s = i % RING
                v.tensor_tensor(w_lo[:, s, 0:width], raw[:, s, 0:width], w_hi[:, s, 0:width].bitcast(F32),
                                ALU.subtract).then_inc(lo_ready, 1)

            def used(g, i):
                dve.wait_ge(unit_used, g * RING + (i + 1 + RING))

            def rsqrt(a, y, t):
                link(v.tensor_scalar(y.bitcast(mybir.dt.int32), a.bitcast(mybir.dt.int32), -0.5, 1597463007.0,
                                     ALU.mult, ALU.add))
                for i in range(3):
                    link(v.scalar_tensor_tensor(t, y, -0.5, y, ALU.mult, ALU.mult))
                    link(v.tensor_tensor(t, t, a, ALU.mult))
                    link(v.scalar_tensor_tensor(a if i == 2 else y, t, 1.5, y, ALU.add, ALU.mult))

            def rstd(n):
                dve.wait_ge(ss_done, n * 2 + 2)
                link(v.tensor_scalar(st[:, 1, :], st[:, 0, :], 1.0 / D, EPS, ALU.mult, ALU.add))
                rsqrt(st[:, 1, :], st[:, 7, :], st[:, 6, :])

            def norm(n):
                rstd(n)
                for t in range(TB):
                    v.tensor_scalar(xn[:, t, :], x_sb[:, t, :], st[:, 1, t:t + 1], None, ALU.mult
                                    ).then_inc(xn_ready, 1)

            def modulated(n, which):
                def full(b):
                    if b >= 2:
                        dve.wait_ge(h_ready, n * 4 + (b - 1))
                    dve.wait_ge(tr_done, n * 4 + b + 1)
                    for k in range(2):
                        kk = 2 * b + k
                        ins = v.tensor_scalar(h_full[:, b % 2, k * T:(k + 1) * T], PS[:, b, k * T:(k + 1) * T],
                                              ab[:, which, 0, kk:kk + 1], ab[:, which, 1, kk:kk + 1],
                                              ALU.mult, ALU.add)
                    ins.then_inc(hf_ready, 1)

                def low(b):
                    dve.wait_ge(hhi_ready, n * 4 + b + 1)
                    v.tensor_tensor(h_lo[:, 2 * b:2 * b + 2, :], h_full[:, b % 2, :].rearrange("p (k t) -> p k t", t=T),
                                    h_hi[:, 2 * b:2 * b + 2, :].bitcast(F32), ALU.subtract).then_inc(h_ready, 1)

                full(0)
                for b in range(1, 4):
                    full(b)
                    low(b - 1)
                low(3)

            def factor(which, cols):
                link(v.tensor_tensor(ab[:, which, 0, :], cols, bcol[:, 2 * which + 1, :], ALU.add))
                link(v.scalar_tensor_tensor(ab[:, which, 0, :], ab[:, which, 0, :], 1.0, nw[:, which, :],
                                            ALU.add, ALU.mult))

            with dve.Fori(0, L) as l:
                g = l * GL
                steps.at(l * ND)
                split(g, 0, 2 * H * KB)
                split(g, 1)
                split(g, 2)
                norm(l * 2)
                dve.wait_ge(par_t, l * 1 + 1)
                link(v.tensor_copy(par[:], PS[:, 6, 0:NROW]))
                dve.wait_ge(ada_red, l * 3 + 1)
                link(v.tensor_tensor(ab[:, 0, 1, :], PS[:, 7, 0:KB], bcol[:, 0, :], ALU.add))
                factor(0, PS[:, 7, KB:2 * KB])
                modulated(l * 2, 0)
                split(g, 3)
                used(g, 0)
                link(v.tensor_scalar(r_i, PS[0:H, 4, 0:T], gbias[:, 0:1], None, ALU.add))
                link(v.tensor_scalar(r_f, PS[0:H, 4, T:2 * T], gbias[:, 1:2], None, ALU.add))
                link(v.tensor_scalar(r_b, r_f, -1.0, None, ALU.mult))
                v.tensor_tensor(r_t, r_f, r_b, ALU.max).then_inc(row_v, 1)
                dve.wait_ge(row_a, l * 3 + 2)
                link(v.scalar_tensor_tensor(r_f, r_f, 0.0, r_t, ALU.min, ALU.subtract))
                link(v.memset(r_m, 0.0))
                link(v.tensor_tensor_scan(r_b, r_f, r_m, 0.0, ALU.add, ALU.add))
                link(v.tensor_tensor(r_i, r_i, r_b, ALU.subtract))
                link(v.tensor_tensor_scan(r_f, r_i, r_m, 0.0, ALU.max, ALU.max))
                v.tensor_tensor(r_e, r_b, r_f, ALU.add).then_inc(row_v, 1)
                dve.wait_ge(row_a, l * 3 + 3)
                for r, src in enumerate((r_i, r_f, r_e)):
                    ins = v.tensor_copy(row_keep[r], src)
                ins.then_inc(row_v, 1)
                n_head = steps.k

                with dve.Fori(0, NPAIR // PAIRS_IT) as it:
                    gi = g + g_sb + it * (SB_U // RING)
                    pr = l * NPAIR + it * PAIRS_IT

                    def att_part(n):
                        dve.wait_ge(atthi_ready, n + 1)
                        v.tensor_tensor(att_lo[:], att[:], att_hi[:].bitcast(F32), ALU.subtract).then_inc(attlo_ready, 1)

                    def av_part(n, jj):
                        dve.wait_ge(hshi_ready, n * 2 + 2)
                        for a in range(2):
                            q = slice(a * DH, (a + 1) * DH)
                            ins = v.tensor_tensor(hs_lo[q, ds(jj), :], PS[q, 3:4, a * T:(a + 1) * T],
                                                  hs_hi[q, ds(jj), :].bitcast(F32), ALU.subtract)
                        ins.then_inc(hs_ready, 1)

                    for j in range(PAIRS_IT):
                        n, u = pr + j, SBQ[j]
                        split(gi, u + AHEAD)
                        split(gi, u + 1 + AHEAD)
                        dve.wait_ge(qkhi_ready, l * (2 * NPAIR + H) + (it * (2 * PAIRS_IT) + 2 * j) + 2)
                        v.scalar_tensor_tensor(qk_lo[:, 0, :], PS[:, 0, 0:T], DH ** -0.5, qk_hi[:, 0, :].bitcast(F32),
                                               ALU.mult, ALU.subtract)
                        v.tensor_tensor(qk_lo[:, 1, :], PS[:, 0, T:2 * T], qk_hi[:, 1, :].bitcast(F32),
                                        ALU.subtract).then_inc(qk_ready, 1)
                        if j:
                            att_part(n - 1)
                        split(gi, u + 2 + AHEAD)
                        if j % 2:
                            dve.wait_ge(vhi_ready, l * NVAL + it * (PAIRS_IT // 2) + (j // 2 + 1))
                            v.tensor_tensor(sv_lo[:].rearrange("p a b -> p (a b)"), PS[:, 1, :],
                                            sv_hi[:].rearrange("p a b -> p (a b)").bitcast(F32),
                                            ALU.subtract).then_inc(v_ready, 1)
                        dve.wait_ge(ln_ready, n * 3 + 3)
                        v.scalar_tensor_tensor(sp[:], PS[:, 4 + 2 * (j % 2):6 + 2 * (j % 2), 0:CAUSAL], 0.0, zt[:],
                                               ALU.max, ALU.add).then_inc(sp_ready, 1)
                        dve.wait_ge(sp_ready, n + 1)
                        v.tensor_copy(sp_hi[:], sp[:]).then_inc(sphi_ready, 1)
                        dve.wait_ge(sphi_ready, n + 1)
                        v.tensor_tensor(sp_lo[:], sp[:], sp_hi[:].bitcast(F32), ALU.subtract).then_inc(splo_ready, 1)
                        if j:
                            split(gi, u + 3 + AHEAD)
                            av_part(n - 1, it * PAIRS_IT + (j - 1))
                    att_part(pr + (PAIRS_IT - 1))
                    split(gi, SB_U + AHEAD)
                    av_part(pr + (PAIRS_IT - 1), it * PAIRS_IT + (PAIRS_IT - 1))

                steps.at(l * ND + n_head)
                dve.wait_ge(rows_t, l * 1 + 1)
                v.tensor_copy(ucol[:], PS[:, 1, 0:TB * H].rearrange("p (a h) -> p a h", h=H))
                v.tensor_copy(emcol[:], PS[:, 1, TB * H:2 * TB * H].rearrange("p (a h) -> p a h", h=H)
                              ).then_inc(cols_ready, 1)
                dve.wait_ge(ada_red, l * 3 + 2)
                v.tensor_tensor(ab[:, 1, 1, :], PS[:, 1, 64:64 + KB], bcol[:, 2, :], ALU.add).then_inc(cols_ready, 1)
                v.tensor_tensor(g1_sb[:], PS[:, 4:6, :].rearrange("p a b -> p (a b)"), g1_sb[:], ALU.add
                                ).then_inc(g_ready, 1)
                dve.wait_ge(cols_ready, l * 2 + 2)
                hold(dve, dve_held)
                n_mid = n_head + steps.k

                with dve.Fori(0, H) as it:
                    gi = g + g_ml + it * (ML_U // RING)
                    n = l * H + it
                    steps.at(l * ND + n_mid + it * N_HEAD)
                    split(gi, 1 + AHEAD)
                    split(gi, 2 + AHEAD)
                    dve.wait_ge(hm_ready, n + 1)
                    dve.wait_ge(pad_ready, n + 1)

                    base_conv = steps.k

                    def tap(a, j):
                        return par[:, ds(it + (j * KB + a * H))]

                    for j in range(NT):
                        for a in range(2):
                            if j == 0:
                                ins = v.tensor_scalar(conv[:, a, :], qk_pad[:, a, 0:T], tap(a, 0), tap(a, NT),
                                                      ALU.mult, ALU.add)
                            else:
                                steps.wait_for(base_conv + 2 * j - 1 + a)
                                ins = v.scalar_tensor_tensor(conv[:, a, :], qk_pad[:, a, j:j + T], tap(a, j),
                                                             conv[:, a, :], ALU.mult, ALU.add)
                            if j < NT - 1:
                                steps.count(ins)
                    ins.then_inc(conv_ready, 1)
                    split(gi, 3 + AHEAD)
                    dve.wait_ge(conv_ready, n + 1)
                    dve.wait_ge(sig_ready, n + 2)
                    link(v.scalar_tensor_tensor(conv[:, 0, :], conv[:, 0, :], QK ** -0.5, sig[:, 0, :],
                                                ALU.mult, ALU.mult))
                    v.tensor_tensor(conv[:, 1, :], conv[:, 1, :], sig[:, 1, :], ALU.mult).then_inc(qkf_ready, 1)
                    dve.wait_ge(qkhi_ready, l * (2 * NPAIR + H) + it + (2 * NPAIR + 1))
                    v.tensor_tensor(qk_lo[:], conv[:], qk_hi[:].bitcast(F32), ALU.subtract).then_inc(qk_ready, 1)
                    dve.wait_ge(vhi_ready, l * NVAL + it + (NPAIR // 2 + 1))
                    v.tensor_tensor(v_lo[:, :, 0:V], PS[:, 1, :].rearrange("p (a v) -> p a v", v=V),
                                    v_hi[:, :, 0:V].bitcast(F32), ALU.subtract).then_inc(v_ready, 1)
                    split(gi, 4 + AHEAD)
                    split(gi, 5 + AHEAD)
                    dve.wait_ge(s_done, n + 1)
                    dve.wait_ge(w_masked, l * 2 + 2)
                    v.tensor_tensor(S_f[:, 0:T], PS[:, 3, 0:T], w_s0[:, ds(it), :].rearrange("p a t -> p (a t)"),
                                    ALU.mult)
                    v.tensor_tensor(S_f[:, T:CAUSAL], PS[:, 3, T:CAUSAL],
                                    w_s1[:, ds(it), :].rearrange("p a t -> p (a t)"), ALU.mult).then_inc(sf_ready, 1)
                    dve.wait_ge(shi_ready, n + 1)
                    v.tensor_tensor(S_lo, S_f, S_hi.bitcast(F32), ALU.subtract).then_inc(s_ready, 1)
                    split(gi, 6 + AHEAD)
                    split(gi, 7 + AHEAD)
                    dve.wait_ge(num_done, n + 1)
                    den = PS[:, 4:6, V:V + 1].rearrange("p a b -> p (a b)")
                    em = emcol[:, :, ds(it)].rearrange("p a b -> p (a b)")
                    link(v.tensor_scalar(st[:, 4, :], den, -1.0, None, ALU.mult))
                    link(v.tensor_tensor(st[:, 4, :], st[:, 4, :], den, ALU.max))
                    link(v.tensor_tensor(st[:, 4, :], st[:, 4, :], em, ALU.max))
                    v.reciprocal(st[:, 2, :], st[:, 4, :]).then_inc(r_ready, 1)
                    dve.wait_ge(sq_ready, n * 2 + 2)
                    link(v.tensor_scalar(st[:, 5, :], st[:, 3, :], 1.0 / V, EPS, ALU.mult, ALU.add))
                    rsqrt(st[:, 5, :], st[:, 7, :], st[:, 6, :])
                    link(v.tensor_tensor(st[:, 6, :], st[:, 5, :], st[:, 2, :], ALU.mult))
                    for t in range(TB):
                        v.tensor_scalar(hmn[:, t, :], PS[:, 4 + t, 0:V], st[:, 6, t:t + 1], None, ALU.mult
                                        ).then_inc(hmn_ready, 1)
                    split(gi, 8 + AHEAD)
                    dve.wait_ge(hmt_done, n + 1)
                    dve.wait_ge(sigo_ready, n + 1)
                    for b in range(2):
                        ins = v.scalar_tensor_tensor(conv[:, b, :], PS[:, 6, b * T:(b + 1) * T],
                                                     par[:, ds(it * 2 + (NT * KB + KB + b))], mo_sb[:, b, :],
                                                     ALU.mult, ALU.mult)
                    ins.then_inc(hmf_ready, 1)
                    dve.wait_ge(hmhi_ready, n + 1)
                    v.tensor_tensor(hm_lo[:, ds(it * 2, 2), :], conv[:], hm_hi[:, ds(it * 2, 2), :].bitcast(F32),
                                    ALU.subtract).then_inc(hm_ready, 1)
                    assert steps.k == N_HEAD, steps.k
                n_ml = n_mid + H * N_HEAD
                steps.at(l * ND + n_ml)
                dve.wait_ge(ada_red, l * 3 + 3)
                factor(1, PS[:, 3, 0:KB])
                dve.wait_ge(g2_loaded, l * 16 + 16)
                v.tensor_tensor(g2_sb[:], PS[:, 0:2, :].rearrange("p a b -> p (a b)"), g2_sb[:], ALU.add
                                ).then_inc(g_ready, 1)
                n_ada = n_ml + steps.k

                with dve.Fori(0, KB // 2) as it:
                    gi = g + g_pj + it * (PJ_U // RING)
                    steps.at(l * ND + n_ada + it * 4)
                    for b in range(2):
                        n = l * KB + it * 2 + b
                        split(gi, 2 * b + 1 + AHEAD)
                        split(gi, 2 * b + 2 + AHEAD)
                        dve.wait_ge(sg_ready, n * 2 + 2)
                        used(gi, 2 * b + 2)
                        dve.wait_ge(y_ready, n + 1)
                        link(v.tensor_tensor(y2, PS[:, 4 + b, 0:T], sig[:, 1, :], ALU.mult))
                        link(v.tensor_tensor(y1, PS[:, 4 + b, T:2 * T], sig[:, 0, :], ALU.mult))
                        v.tensor_tensor(y1, y1, y2, ALU.add).then_inc(yf_ready, 1)
                        dve.wait_ge(yhi_ready, n + 1)
                        v.tensor_tensor(h_lo[:, ds(it * 2 + b), :], y1.rearrange("p (a t) -> p a t", a=1),
                                        h_hi[:, ds(it * 2 + b), :].bitcast(F32), ALU.subtract).then_inc(y_ready, 1)
                n_pj = n_ada + KB // 2 * 4
                steps.at(l * ND + n_pj)
                for i in range(8):
                    split(g + g_out, i + 1 + AHEAD, E * KB if i + 1 + AHEAD == 9 else 1024)
                    if i % 4 == 3:
                        used(g + g_out, i + 1)
                        h = i // 4
                        for t in range(TB):
                            bank = (6 if h == 0 else 0) + t
                            link(v.tensor_tensor(h_full[:, t, :], PS[:, bank, :], g1_sb[:, h * 512:(h + 1) * 512],
                                                 ALU.mult))
                            v.tensor_tensor(x_sb[:, t, h * 512:(h + 1) * 512], x_sb[:, t, h * 512:(h + 1) * 512],
                                            h_full[:, t, :], ALU.add).then_inc(mix_added, 1)
                            dve.wait_ge(mix_added, l * 8 + (5 + 2 * h + t))
                split(g + g_out, 9 + AHEAD)
                norm(l * 2 + 1)
                modulated(l * 2 + 1, 1)
                split(g + g_out, 10 + AHEAD)

                dve.wait_ge(rt_ready, l * 1 + 1)
                for t in range(TB):
                    ins = v.tensor_tensor(sel[:, t, :], sc[:, t, :], rb[:], ALU.add)
                link(ins)
                hold(dve, dve_held)
                for t in range(TB):
                    for q in range(N_GROUPS):
                        ins = v.max(m8[:, t, q, :], sel[:, t, q * EG:(q + 1) * EG])
                link(ins)
                v.memset(gp[:, :, N_GROUPS:16], -FAR)
                link(v.tensor_tensor(gp[:, :, 0:N_GROUPS].rearrange("p a (b c) -> p a b c", c=1), m8[:, :, :, 0:1],
                                     m8[:, :, :, 1:2], ALU.add))
                hold(dve, dve_held)
                for t in range(TB):
                    ins = v.max(t8[:, t, :], gp[:, t, :])
                link(ins)
                link(v.memset(t8[:, :, TOPK_GROUPS:8], -FAR))
                hold(dve, dve_held)
                for t in range(TB):
                    ins = v.match_replace(gr[:, t, :], t8[:, t, :], gp[:, t, :], FAR)
                link(ins)
                link(v.tensor_tensor(gm[:, 0, :, :], gr[:, :, 0:N_GROUPS], gp[:, :, 0:N_GROUPS], ALU.not_equal))
                link(v.tensor_scalar(gm[:, 1, :, :], gm[:, 0, :, :], -1.0, -MASKED, ALU.add, ALU.mult))
                for t in range(TB):
                    for q in range(N_GROUPS):
                        e = slice(q * EG, (q + 1) * EG)
                        ins = v.tensor_scalar(sel[:, t, e], sel[:, t, e], gm[:, 0, t, q:q + 1], gm[:, 1, t, q:q + 1],
                                              ALU.mult, ALU.add)
                link(ins)
                hold(dve, dve_held)
                for t in range(TB):
                    ins = v.max(t8[:, t, :], sel[:, t, :])
                link(ins)
                hold(dve, dve_held)
                for t in range(TB):
                    ins = v.match_replace(rep[:, t, :], t8[:, t, :], sel[:, t, :], FAR)
                link(ins)
                link(v.tensor_tensor(rep[:], rep[:], sel[:], ALU.not_equal))
                link(v.tensor_tensor(gts[:], rep[:], sc[:], ALU.mult))
                link(v.tensor_reduce(st[:, 4, :], gts[:], AX.X, ALU.add))
                link(v.reciprocal(st[:, 5, :], st[:, 4, :]))
                for t in range(TB):
                    ins = v.tensor_scalar(gts[:, t, :], gts[:, t, :], st[:, 5, t:t + 1], ROUTED_SCALE,
                                          ALU.mult, ALU.mult)
                ins.then_inc(gts_ready, 1)

                def hidden(n, par, gate):
                    dve.wait_ge(silu_ready, n + 1)
                    ins = v.tensor_tensor(conv[:, par, :], sig[:, par, :], PS[:, 6 + par, T:2 * T], ALU.mult)
                    if gate is not None:
                        link(ins)
                        ins = v.tensor_tensor(conv[:, par, :], conv[:, par, :], gate_b[:, gate, :], ALU.mult)
                    ins.then_inc(hid_full, 1)
                    dve.wait_ge(hidhi_ready, n + 1)
                    v.tensor_tensor(hid_lo[:, par, :], conv[:, par, :], hid_hi[:, par, :].bitcast(F32),
                                    ALU.subtract).then_inc(hid_ready, 1)

                split(g + g_out, 11 + AHEAD)
                hidden(l * EV, 1, None)
                dve.wait_ge(gt_done, l * 1 + 1)
                v.tensor_copy(gT, PS[0:E, 5, 0:T]).then_inc(gT_ready, 1)
                n_moe = n_pj + steps.k
                with dve.Fori(0, E // EXP_IT) as it:
                    gi = g + g_moe + it * 3
                    steps.at(l * ND + n_moe + it * EXP_IT)
                    for e in range(EXP_IT):
                        split(gi, 3 * e + AHEAD)
                        split(gi, 3 * e + 1 + AHEAD)
                        if e % 2 == 0:
                            dve.wait_ge(gate_loaded[e // 2], (l * (E // EXP_IT) + it + 1) * 16)
                        hidden(l * EV + it * EXP_IT + (e + 1), e % 2, e)
                        split(gi, 3 * e + 2 + AHEAD)
                n_post = n_moe + E
                steps.at(l * ND + n_post)
                split(g + g_post, AHEAD)
                hidden(l * EV + (E + 1), 0, None)
                used(g + g_post, 3)
                for t in range(TB):
                    for h in range(2):
                        link(v.tensor_tensor(h_full[:, h, :], PS[:, 2 * t + h, :], g2_sb[:, h * 512:(h + 1) * 512],
                                             ALU.mult))
                        ins = v.tensor_tensor(x_sb[:, t, h * 512:(h + 1) * 512], x_sb[:, t, h * 512:(h + 1) * 512],
                                              h_full[:, h, :], ALU.add)
                        ins.then_inc(mix_added, 1)
                        dve.wait_ge(mix_added, l * 8 + (9 + 2 * t + h))
                total = n_post + steps.k
                assert total == ND, total
            steps.at(L * ND)
            rstd(L * 2)
            dve.wait_ge(par_loaded, (L * N_SMALL + 1) * 16)
            for t in range(TB):
                ins = v.scalar_tensor_tensor(x_sb[:, t, :], x_sb[:, t, :], st[:, 1, t:t + 1], g1_sb[:],
                                             ALU.mult, ALU.mult)
            ins.then_inc(out_ready, 1)

        @block.tensor
        def _(pe):
            mm = nc.tensor.matmul
            pe.sem_inc(unit_used, RING)
            pe.wait_ge(consts, N_CONST)

            def three(out, a, b, start, stop, check=False):
                mm(out, a[0], b[0], start=start, stop=False, skip_group_check=True)
                mm(out, a[0], b[1], start=False, stop=False, skip_group_check=True)
                return mm(out, a[1], b[0], start=False, stop=stop, skip_group_check=True)

            def unit(g, i, n, nk=KB):
                pe.wait_ge(lo_ready, g * RING + (i + 1 + RING))
                s = i % RING
                return [w[:, s, 0:nk * n].rearrange("p (k n) -> p k n", n=n) for w in (w_hi, w_lo)]

            def feat_major(g, i, out, rhs=None):
                w = unit(g, i, P)
                rh, rl = rhs or (h_hi, h_lo)
                for k in range(KB):
                    ins = three(out, (w[0][:, k, :], w[1][:, k, :]), (rh[:, k, :], rl[:, k, :]), k == 0, k == KB - 1)
                ins.then_inc(unit_used, 1)

            def token_major(g, i, q):
                w = unit(g, i, V, 4)
                for t in range(TB):
                    for k in range(4):
                        kk = 4 * q + k
                        ins = three(PS[:, 1, t * V:(t + 1) * V],
                                    (h_hi[:, kk, t * P:(t + 1) * P], h_lo[:, kk, t * P:(t + 1) * P]),
                                    (w[0][:, k, :], w[1][:, k, :]), kk == 0 and t == 0, kk == KB - 1)
                ins.then_inc(unit_used, 1)

            def turn(n):
                for t in range(TB):
                    pe.wait_ge(xn_ready, n * 2 + (t + 1))
                    for k in range(KB):
                        col = (k % 2) * T + t * P
                        ins = nc.tensor.transpose(PS[:, k // 2, col:col + P], xn[:, t, k:D:KB], ident[:])
                        if t == 1 and k % 2:
                            ins.then_inc(tr_done, 1)

            def ones_cols(off, out_col, bank):
                for k in range(KB):
                    ins = mm(PS[:, bank, out_col + k:out_col + k + 1], ada_acc[:, off + k:off + D:KB], ones[:, 0:1],
                             start=True, stop=True, skip_group_check=True)
                return ins

            def ones_rows(off, bank):
                for h in range(2):
                    ins = mm(PS[:, bank + h, :], ones[:], ada_acc[:, off + h * 512:off + (h + 1) * 512],
                             start=True, stop=True, skip_group_check=True)
                return ins

            with pe.Fori(0, L) as l:
                g = l * GL
                turn(l * 2)
                pe.wait_ge(par_loaded, (l + 1) * (N_SMALL * 16))
                hold(pe, pe_held)
                nc.tensor.transpose(PS[:, 6, 0:NROW], par_rows[:], ident[0:NROW, 0:NROW]).then_inc(par_t, 1)
                pe.wait_ge(acc_ready, l * 3 + 1)
                ones_cols(0, 0, 7)
                ones_cols(D, KB, 7).then_inc(ada_red, 1)
                w = unit(g, 0, 2 * H)
                for a in range(2):
                    for k in range(KB):
                        if a == 0 and k % 2 == 0:
                            pe.wait_ge(h_ready, l * 8 + (k // 2 + 1))
                        ins = three(PS[0:H, 4, a * T:(a + 1) * T],
                                    (w[0][:, k, a * H:(a + 1) * H], w[1][:, k, a * H:(a + 1) * H]),
                                    (h_hi[:, k, :], h_lo[:, k, :]), k == 0, k == KB - 1)
                ins.then_inc(unit_used, 1)

                with pe.Fori(0, NPAIR // PAIRS_IT) as it:
                    gi = g + g_sb + it * (SB_U // RING)
                    pr = l * NPAIR + it * PAIRS_IT

                    def scores(n, j):
                        pe.wait_ge(qk_ready, l * (NPAIR + H) + (it * PAIRS_IT + j) + 1)
                        for a in range(2):
                            q = slice(a * DH, (a + 1) * DH)
                            bank = 4 + 2 * (j % 2) + a
                            for s in range(TB):
                                o = PS[:, bank, s * T:s * T + T - s * P]
                                three(o, (qk_hi[q, 1, s * P:(s + 1) * P], qk_lo[q, 1, s * P:(s + 1) * P]),
                                      (qk_hi[q, 0, s * P:T], qk_lo[q, 0, s * P:T]), s == 0, False)
                                ins = mm(PS[:, bank, s * T:s * T + P], ident_r[:], negmask[:], start=False, stop=False,
                                         skip_group_check=True)
                        ins.then_inc(z_done, 1)

                    def sums(n, j):
                        pe.wait_ge(splo_ready, n + 1)
                        for a in range(2):
                            bank = 4 + 2 * (j % 2) + a
                            for w in (sp_hi, sp_lo):
                                mm(PS[:, bank, 0:T], negtri[:], w[:, a, 0:T], start=False, stop=False, skip_group_check=True)
                                mm(PS[:, bank, T:CAUSAL], negtri[:], w[:, a, T:CAUSAL], start=False, stop=False,
                                   skip_group_check=True)
                                ins = mm(PS[:, bank, P:T], negones[:], w[:, a, T:CAUSAL], start=False, stop=w is sp_lo,
                                         skip_group_check=True)
                        ins.then_inc(l_done, 1)

                    def values(n, j):
                        pe.wait_ge(v_ready, l * NVAL + it * (PAIRS_IT // 2) + (j // 2 + 1))
                        pe.wait_ge(attlo_ready, n + 1)
                        f = slice(j % 2 * P, (j % 2 + 1) * P)
                        for a in range(2):
                            o = PS[:, 3, a * T:(a + 1) * T]
                            three(o, (sv_hi[:, 0, f], sv_lo[:, 0, f]),
                                  (att_hi[:, a, 0:T], att_lo[:, a, 0:T]), True, False)
                            ins = three(o[:, P:T], (sv_hi[:, 1, f], sv_lo[:, 1, f]),
                                        (att_hi[:, a, T:CAUSAL], att_lo[:, a, T:CAUSAL]), False, True)
                        ins.then_inc(av_done, 1)

                    for j in range(PAIRS_IT):
                        n, u = pr + j, SBQ[j]
                        feat_major(gi, u, PS[:, 0, 0:T])
                        feat_major(gi, u + 1, PS[:, 0, T:2 * T])
                        if j:
                            sums(n - 1, j - 1)
                        token_major(gi, u + 2, j % 2)
                        scores(n, j)
                        if j:
                            feat_major(gi, u + 3, PS[:, 2, 0:T])
                            values(n - 1, j - 1)
                    sums(pr + (PAIRS_IT - 1), PAIRS_IT - 1)
                    feat_major(gi, SB_U, PS[:, 0, 0:T])
                    values(pr + (PAIRS_IT - 1), PAIRS_IT - 1)
                    pe.wait_ge(g_evac, l * (NPAIR + H) + (it * PAIRS_IT + PAIRS_IT))

                pe.wait_ge(row_v, l * 3 + 5)
                hold(pe, pe_held)
                for r, row in enumerate((0, 2)):
                    for t in range(TB):
                        nc.tensor.transpose(PS[:, 1, (r * TB + t) * H:(r * TB + t + 1) * H],
                                            row_keep[row][:, t * P:(t + 1) * P], ident[0:H, 0:H])
                for h in range(H):
                    ins = mm(PS[:, 6 + h // 2, (h % 2) * T:(h % 2 + 1) * T], head_sel[:, h, :], row_keep[1],
                             start=True, stop=True, skip_group_check=True)
                ins.then_inc(rows_t, 1)
                pe.wait_ge(acc_ready, l * 3 + 2)
                pe.wait_ge(cols_ready, l * 2 + 1)
                ones_cols(D, 64, 1)
                ones_rows(0, 4).then_inc(ada_red, 1)

                with pe.Fori(0, H) as it:
                    gi = g + g_ml + it * (ML_U // RING)
                    n = l * H + it
                    feat_major(gi, 1, PS[:, 0, 0:T])
                    feat_major(gi, 2, PS[:, 0, T:2 * T])
                    pe.wait_ge(cols_ready, l * 2 + 2)
                    token_major(gi, 3, 0)
                    token_major(gi, 4, 1)
                    feat_major(gi, 5, PS[:, 2, 0:T])
                    pe.wait_ge(qk_ready, l * (NPAIR + H) + it + (NPAIR + 1))
                    for s in range(TB):
                        b = slice(s * P, (s + 1) * P)
                        ins = three(PS[:, 3, s * T:s * T + T - s * P], (qk_hi[:, 1, b], qk_lo[:, 1, b]),
                                    (qk_hi[:, 0, s * P:T], qk_lo[:, 0, s * P:T]), True, True)
                    ins.then_inc(s_done, 1)
                    feat_major(gi, 6, PS[:, 2, T:2 * T])
                    pe.wait_ge(v_ready, l * NVAL + it + (NPAIR // 2 + 1))
                    pe.wait_ge(s_ready, n + 2)
                    pe.wait_ge(g_ready, l * 2 + 1)
                    for t in range(TB):
                        for s in range(t + 1):
                            col = t * P if s == 0 else T
                            ins = three(PS[:, 4 + t, 0:VA], (S_hi[:, col:col + P], S_lo[:, col:col + P]),
                                        (v_hi[:, s, :], v_lo[:, s, :]), s == 0, s == t)
                    ins.then_inc(num_done, 1)
                    pe.wait_ge(mb_ready, l * 1 + 1)
                    feat_major(gi, 7, PS[:, 7, 0:T])
                    feat_major(gi, 8, PS[:, 7, T:2 * T])
                    for t in range(TB):
                        pe.wait_ge(hmn_ready, n * 2 + (t + 1))
                        for b in range(2):
                            ins = nc.tensor.transpose(PS[:, 6, b * T + t * P:b * T + (t + 1) * P],
                                                      hmn[:, t, b * P:(b + 1) * P], ident[:])
                    ins.then_inc(hmt_done, 1)

                pe.wait_ge(acc_ready, l * 3 + 3)
                ones_cols(0, 0, 3)
                ones_rows(D, 0).then_inc(ada_red, 1)

                with pe.Fori(0, KB // 2) as it:
                    gi = g + g_pj + it * (PJ_U // RING)
                    for b in range(2):
                        pe.wait_ge(yf_ready, l * KB + it * 2 + (b + 1))
                        feat_major(gi, 2 * b + 1, PS[:, 4 + b, 0:T], (hs_hi, hs_lo))
                        pe.wait_ge(hm_ready, l * H + (H + 1))
                        feat_major(gi, 2 * b + 2, PS[:, 4 + b, T:2 * T], (hm_hi, hm_lo))

                pe.wait_ge(g_ready, l * 2 + 2)
                for i in range(8):
                    w = unit(g + g_out, i + 1, 512, 2)
                    q = i % 4
                    pe.wait_ge(y_ready, l * KB + (2 * q + 3))
                    for t in range(TB):
                        bank = (6 if i < 4 else 0) + t
                        for k in range(2):
                            kk = 2 * q + k
                            ins = three(PS[:, bank, :], (h_hi[:, kk, t * P:(t + 1) * P], h_lo[:, kk, t * P:(t + 1) * P]),
                                        (w[0][:, k, :], w[1][:, k, :]), kk == 0, kk == KB - 1)
                    ins.then_inc(unit_used, 1)
                turn(l * 2 + 1)
                w = unit(g + g_out, 9, E)
                for t in range(TB):
                    for k in range(KB):
                        if t == 0 and k % 2 == 0:
                            pe.wait_ge(h_ready, l * 8 + (k // 2 + 5))
                        ins = three(PS[:, 4, t * E:(t + 1) * E],
                                    (h_hi[:, k, t * P:(t + 1) * P], h_lo[:, k, t * P:(t + 1) * P]),
                                    (w[0][:, k, :], w[1][:, k, :]), k == 0, k == KB - 1)
                ins.then_inc(unit_used, 1)

                def hidden(g, i, par):
                    feat_major(g, i, PS[:, 6 + par, 0:T])
                    feat_major(g, i + 1, PS[:, 6 + par, T:2 * T])

                def down(g, i, n, par, stop=False):
                    w = unit(g, i, 512, 2)
                    pe.wait_ge(hid_ready, n + 1)
                    for t in range(TB):
                        for h in range(2):
                            ins = three(PS[:, 2 * t + h, :],
                                        (hid_hi[:, par, t * P:(t + 1) * P], hid_lo[:, par, t * P:(t + 1) * P]),
                                        (w[0][:, h, :], w[1][:, h, :]), False, stop)
                    ins.then_inc(unit_used, 1)
                    return ins

                hidden(g + g_out, 10, 1)
                for b in range(4):
                    mm(PS[:, b, :], zeros_r[:], h_hi[:, 0:2, :].rearrange("p a b -> p (a b)"), start=True, stop=False,
                       skip_group_check=True)
                pe.wait_ge(gts_ready, l * 1 + 1)
                hold(pe, pe_held)
                for t in range(TB):
                    ins = nc.tensor.transpose(PS[0:E, 5, t * P:(t + 1) * P], gts[:, t, :], ident[:])
                ins.then_inc(gt_done, 1)
                with pe.Fori(0, E // EXP_IT) as it:
                    gi = g + g_moe + it * 3
                    for e in range(EXP_IT):
                        hidden(gi, 3 * e, e % 2)
                        down(gi, 3 * e + 2, l * EV + it * EXP_IT + e, 1 - e % 2)
                hidden(g + g_post, 0, 0)
                down(g + g_post, 2, l * EV + E, 1)
                down(g + g_post, 3, l * EV + (E + 1), 0, True)


_INS = ["x", "c", "ada_w", "ada_b", "norm1_w", "w_in", "conv_w", "conv_b", "m_igate_b", "m_fgate_b", "m_norm_w",
        "w_proj_a", "w_proj_b", "w_out", "norm2_w", "router_w", "router_b", "w_gate", "w_up", "w_down",
        "sh_gate", "sh_up", "sh_down", "final_norm_w"]


def kernel(**inputs):
    import numpy as _np
    import concourse.bacc as _bacc
    from concourse import mybir as _mybir
    from concourse.bass_utils import run_bass_kernel_spmd as _run

    nc = _bacc.Bacc("TRN2", target_bir_lowering=False, num_devices=1)
    arrays, args = {}, []
    for name in _INS:
        a = _np.ascontiguousarray(inputs[name])
        arrays[f"in_{name}_dram"] = a
        args.append(nc.dram_tensor(f"in_{name}_dram", a.shape, _mybir.dt.from_np(a.dtype), kind="ExternalInput").ap())
    tokens, experts = inputs["x"].shape[1], inputs["router_w"].shape[2]
    gates = nc.dram_tensor("gates_dram", (experts, tokens), _mybir.dt.float32, kind="Internal").ap()
    out = nc.dram_tensor("out_dram", inputs["x"].shape, _mybir.dt.float32, kind="ExternalOutput").ap()
    trunk(nc, *args, gates, out)
    r = _run(nc, [arrays], core_ids=[0])
    return r.results[0]["out_dram"]
```

```python
from contextlib import ExitStack

import concourse.bass as bass
from concourse import mybir

F32 = mybir.dt.float32
F32R = mybir.dt.float32r
ALU = mybir.AluOpType
ACT = mybir.ActivationFunctionType
AX = mybir.AxisListType

P = 128
EPS = 1e-6
ROUTED_SCALE = 2.5
TOP_K, TOPK_GROUPS, N_GROUPS = 8, 4, 8
RING = 4
AHEAD = RING - 1
MASKED = -1e30
FAR = 3e38
N_SMALL = 11
N_CONST = 17
N_HEAD = 25
N_NORM = 15
STEPS = 248
LEXP = "natural_log_exp_and_others"


def ds(i, n=1):
    return bass.ds(i, n)


def hold(eng, sem):
    eng.sem_inc(sem, 1)


class Steps:

    def __init__(self, eng, sem, per_layer):
        self.eng, self.sem, self.per_layer = eng, sem, per_layer
        self.base, self.k = 0, 0

    def at(self, base):
        self.base, self.k = base, 0

    def count(self, ins):
        self.k += 1
        ins.then_inc(self.sem, 1)

    def wait_for(self, k):
        self.eng.wait_ge(self.sem, self.base + k)

    def link(self, ins):
        self.count(ins)
        self.wait_for(self.k)


def trunk(nc, x, c, ada_w, ada_b, norm1_w, w_in, conv_w, conv_b, m_igate_b, m_fgate_b, m_norm_w,
          w_proj_a, w_proj_b, w_out, norm2_w, router_w, router_b, w_gate, w_up, w_down,
          sh_gate, sh_up, sh_down, final_norm_w, gates_dram, out):
    _, T, D = x.shape
    L = ada_w.shape[0]
    TB, KB = T // P, D // P
    E, FF = w_gate.shape[1], w_gate.shape[3]
    H = m_igate_b.shape[1]
    QK = conv_w.shape[2] // (2 * H)
    V = w_proj_a.shape[1] // H
    DH = 64
    NPAIR = D // (2 * DH)
    NT = conv_w.shape[1]
    assert TB == 2 and KB == 8 and QK == P and V == 2 * P and FF == P and E % 4 == 0 and NPAIR == 8
    sizes = [H * QK, H * QK, H * V, H * V, H, H, D, D, D, D, D]
    MQ, MK, MV, MO, MI, MF, SQ, SK, SV, GA, GB = [sum(sizes[:i]) for i in range(11)]
    EG = E // N_GROUPS
    CAUSAL = T + P

    PAIRS_IT, SB_U = 4, 16
    SBQ = [1, 4, 8, 12]
    ML_U = 8
    PJ_U = 4
    EXP_IT = 4
    g_sb = 0
    g_ml = g_sb + NPAIR // PAIRS_IT * SB_U // RING
    g_pj = g_ml + H * ML_U // RING
    g_out = g_pj + KB // 2 * PJ_U // RING
    g_moe = g_out + 3
    g_post = g_moe + E * 3 // RING
    GL = g_post + 1
    NVAL = NPAIR // 2 + H

    with ExitStack() as ctx:
        def sb(name, shape, dt=F32):
            return ctx.enter_context(nc.sbuf_tensor(name, shape, dt))

        def sem(name):
            return ctx.enter_context(nc.semaphore(name))

        PS = ctx.enter_context(nc.psum_tensor("PS", [P, 8, 512], F32))

        raw = sb("raw", [P, RING, 1024])
        w_hi = sb("w_hi", [P, RING, 1024], F32R)
        w_lo = sb("w_lo", [P, RING, 1024], F32R)
        ada_raw = sb("ada_raw", [P, 2, 2 * D])
        ada_acc = sb("ada_acc", [P, 2 * D])
        x_sb = sb("x_sb", [P, TB, D])
        h_hi = sb("h_hi", [P, KB, T], F32R)
        h_lo = sb("h_lo", [P, KB, T], F32R)
        hm_hi = sb("hm_hi", [P, KB, T], F32R)
        hm_lo = sb("hm_lo", [P, KB, T], F32R)
        hs_hi = sb("hs_hi", [P, KB, T], F32R)
        hs_lo = sb("hs_lo", [P, KB, T], F32R)
        ga_sb = sb("ga_sb", [P, KB, T])
        gb_sb = sb("gb_sb", [P, KB, T])
        xn = ga_sb[:].rearrange("p a b -> p (a b)").rearrange("p (t d) -> p t d", t=TB)
        g1_sb = sb("g1_sb", [P, D])
        g2_sb = sb("g2_sb", [P, D])
        ada0_raw = [ada_raw[:, 0, :], ada_raw[:, 1, :], gb_sb[:].rearrange("p a b -> p (a b)")]
        h_full = gb_sb[:, 0:4, :].rearrange("p (a b) t -> p a (b t)", a=2)
        h_part = gb_sb[:].rearrange("p (a b) t -> p a (b t)", b=2)
        qz_hi, qz_lo = hm_hi[:, 0:2, :], hm_lo[:, 0:2, :]
        zt = sb("zt", [P, 2, CAUSAL])
        sp = sb("sp", [P, 2, CAUSAL])
        sp_hi = sb("sp_hi", [P, 2, CAUSAL], F32R)
        sp_lo = sb("sp_lo", [P, 2, CAUSAL], F32R)
        att = sb("att", [P, 2, CAUSAL])
        att_hi = sb("att_hi", [P, 2, CAUSAL], F32R)
        att_lo = sb("att_lo", [P, 2, CAUSAL], F32R)
        ztf, spf, spf_hi, spf_lo, attf, attf_hi, attf_lo = [w[:].rearrange("p a b -> p (a b)") for w in (
            zt, sp, sp_hi, sp_lo, att, att_hi, att_lo)]
        qk_hi = sb("qk_hi", [P, 2, T], F32R)
        qk_lo = sb("qk_lo", [P, 2, T], F32R)
        VA = V + 2
        v_hi = sb("v_hi", [P, TB, VA], F32R)
        v_lo = sb("v_lo", [P, TB, VA], F32R)
        sv_hi = sb("sv_hi", [P, TB, 2 * P], F32R)
        sv_lo = sb("sv_lo", [P, TB, 2 * P], F32R)
        qk_pad = sb("qk_pad", [P, 2, NT - 1 + T])
        conv = sb("conv", [P, 2, T])
        sig = sb("sig", [P, 2, T])
        mo_sb = sb("mo_sb", [P, 2, T])
        M_sb = sb("M_sb", [P, H, T])
        assert H == EXP_IT
        gate_b = M_sb
        ident = sb("ident", [P, P])
        ident_r = sb("ident_r", [P, P], F32R)
        ones = sb("ones", [P, P])
        negmask = sb("negmask", [P, P], F32R)
        negtri = sb("negtri", [P, P], F32R)
        negones = sb("negones", [P, P], F32R)
        zeros_r = sb("zeros_r", [P, P], F32R)
        head_sel = sb("head_sel", [H, H, P])
        cond = sb("cond", [P, KB])
        c_sb = sb("c_sb", [P, 2, KB])
        NROW = NT * KB + 2 * KB
        par_rows = sb("par_rows", [NROW, P])
        par = sb("par", [P, NROW])
        bcol = sb("bcol", [P, 4, KB])
        nw = sb("nw", [P, 2, KB])
        ab = sb("ab", [P, 2, 2, KB])
        gbias = sb("gbias", [H, 2])
        ucol = sb("ucol", [P, TB, H])
        emcol = sb("emcol", [P, TB, H])
        st = sb("st", [P, 8, 2])
        rb = sb("rb", [P, E])
        sc = sb("sc", [P, TB, E])
        sel = sb("sel", [P, TB, E])
        rep = sb("rep", [P, TB, E])
        gts = sb("gts", [P, TB, E])
        m8 = sb("m8", [P, TB, N_GROUPS, 8])
        gp = sb("gp", [P, TB, 16])
        gr = sb("gr", [P, TB, 16])
        t8 = sb("t8", [P, TB, 8])
        gm = sb("gm", [P, 2, TB, N_GROUPS])
        gT, scT = mo_sb[0:E, 0, :], mo_sb[0:E, 1, :]
        row_keep = [conv[0:H, 0, :], conv[0:H, 1, :], mo_sb[0:H, 1, :]]

        rows = [sp[0:H, 0, 0:T], att[0:H, 0, 0:T], sp[0:H, 1, 0:T], att[0:H, 1, 0:T],
                zt[0:H, 0, 0:T], zt[0:H, 1, 0:T]]
        r_i, r_f, r_b, r_m, r_t, r_e = rows
        w_s0, w_s1 = M_sb, att[:].rearrange("p a b -> p (a b)")[:, 0:H * P].rearrange("p (h t) -> p h t", h=H)
        S_f, S_hi, S_lo = sp[:, 0, :], sp_hi[:, 0, :], sp_lo[:, 0, :]
        hmn = zt[:, :, 0:V]
        y1, y2 = sp[:, 0, 0:T], sp[:, 1, 0:T]
        hid_hi, hid_lo = qk_hi, qk_lo

        raw_loaded = [sem(f"raw_loaded{i}") for i in range(RING)]
        hi_ready = sem("hi_ready")
        lo_ready = sem("lo_ready")
        unit_used = sem("unit_used")
        x_loaded = sem("x_loaded")
        c_loaded = sem("c_loaded")
        par_loaded = sem("par_loaded")
        ada_loaded = [sem("ada_loaded0"), sem("ada_loaded1")]
        ada_summed = sem("ada_summed")
        ada_scaled = sem("ada_scaled")
        ada_zero = sem("ada_zero")
        ada0_loaded = [sem(f"ada0_loaded{i}") for i in range(3)]
        ada0_used = sem("ada0_used")
        adan_loaded = sem("adan_loaded")
        adan_used = sem("adan_used")
        g2_loaded = sem("g2_loaded")
        consts = sem("consts")
        ss_done = sem("ss_done")
        xn_ready = sem("xn_ready")
        tr_done = sem("tr_done")
        hf_ready = sem("hf_ready")
        hfa_ready = sem("hfa_ready")
        hhi_ready = sem("hhi_ready")
        h_ready = sem("h_ready")
        par_t = sem("par_t")
        acc_ready = sem("acc_ready")
        ada_red = sem("ada_red")
        ab_ready = sem("ab_ready")
        row_a = sem("row_a")
        row_v = sem("row_v")
        rows_t = sem("rows_t")
        cols_ready = sem("cols_ready")
        mb_ready = sem("mb_ready")
        g_ready = sem("g_ready")
        qkhi_ready = sem("qkhi_ready")
        qk_ready = sem("qk_ready")
        q_zeroed = sem("q_zeroed")
        vhi_ready = sem("vhi_ready")
        v_ready = sem("v_ready")
        z_done = sem("z_done")
        ln_ready = sem("ln_ready")
        sp_ready = sem("sp_ready")
        sphi_ready = sem("sphi_ready")
        splo_ready = sem("splo_ready")
        l_done = sem("l_done")
        att_ready = sem("att_ready")
        atthi_ready = sem("atthi_ready")
        attlo_ready = sem("attlo_ready")
        av_done = sem("av_done")
        hshi_ready = sem("hshi_ready")
        hs_ready = sem("hs_ready")
        g_evac = sem("g_evac")
        pad_ready = sem("pad_ready")
        conv_ready = sem("conv_ready")
        sig_ready = sem("sig_ready")
        qkf_ready = sem("qkf_ready")
        w_ready = sem("w_ready")
        w_masked = sem("w_masked")
        s_done = sem("s_done")
        sf_ready = sem("sf_ready")
        shi_ready = sem("shi_ready")
        s_ready = sem("s_ready")
        num_done = sem("num_done")
        r_ready = sem("r_ready")
        sq_ready = sem("sq_ready")
        hmn_ready = sem("hmn_ready")
        sigo_ready = sem("sigo_ready")
        hmt_done = sem("hmt_done")
        hmf_ready = sem("hmf_ready")
        hmhi_ready = sem("hmhi_ready")
        hm_ready = sem("hm_ready")
        sg_ready = sem("sg_ready")
        yf_ready = sem("yf_ready")
        yhi_ready = sem("yhi_ready")
        y_ready = sem("y_ready")
        bank_done = sem("bank_done")
        mix_added = sem("mix_added")
        rt_ready = sem("rt_ready")
        sc_turned = sem("sc_turned")
        gts_ready = sem("gts_ready")
        gt_done = sem("gt_done")
        gT_ready = sem("gT_ready")
        gb_done = sem("gb_done")
        gate_ready = sem("gate_ready")
        gT_stored = sem("gT_stored")
        gate_loaded = [sem("gate_loaded0"), sem("gate_loaded1")]
        silu_ready = sem("silu_ready")
        hid_full = sem("hid_full")
        hidhi_ready = sem("hidhi_ready")
        hid_ready = sem("hid_ready")
        out_ready = sem("out_ready")
        stored = sem("stored")
        dve_step = sem("dve_step")
        pool_held, pe_held, dve_held = sem("pool_held"), sem("pe_held"), sem("dve_held")

        EV = E + 2
        ND = STEPS
        block = ctx.enter_context(nc.Block())

        BY_ROWS = [(0, 0), (0, 1), (1, 0), (1, 1)]
        BY_HALVES = [(0, 0), (1, 0), (0, 1), (1, 1)]

        def two(w):
            return w.rearrange("p (a t) -> p a t", a=2)

        def scores_bank(par):
            return PS[:, 4 + 2 * par:6 + 2 * par, :].rearrange("p a b -> p (a b)")[:, 0:2 * CAUSAL]

        @block.sync
        def _(sp_e):
            sp_e.dma_start(c_sb[:, 0, :], c.rearrange("o (p k) -> (o p) k", k=KB)).then_inc(c_loaded, 16)
            sp_e.dma_start(x_sb[:], x.rearrange("o (t p) d -> p (o t) d", p=P)).then_inc(x_loaded, 16)

            def load(src, g, i, width=1024):
                sp_e.wait_ge(lo_ready, g * RING + i + 1)
                sp_e.dma_start(raw[:, i % RING, 0:width].rearrange("p (k n) -> p k n", n=src.shape[-1]),
                               src).then_inc(raw_loaded[i % RING], 16)

            def cols(w, l, col, n=P, k0=0, nk=KB):
                v = w[ds(l), :, ds(col, n)].rearrange("o (p k) n -> (o p) k n", k=KB)
                return v[:, k0:k0 + nk, :]

            def cols_std(w, l, col, n=P, k0=0, nk=KB):
                v = w[ds(l), k0 * P:(k0 + nk) * P, ds(col, n)]
                return v.rearrange("o (k p) n -> (o p) k n", p=P)

            for k in range(KB):
                if k >= 3:
                    sp_e.wait_ge(ada0_used, k - 2)
                sp_e.dma_start(ada0_raw[k % 3], ada_w[0:1, :, 0:2 * D].rearrange("o (p k) n -> (o p) k n", k=KB)[:, k, :]
                               ).then_inc(ada0_loaded[k % 3], 16)

            with sp_e.Fori(0, L) as l:
                g = l * GL
                load(cols(w_in, l, MI, 2 * H), g, 0, 2 * H * KB)
                with sp_e.Fori(0, NPAIR // PAIRS_IT) as it:
                    gi = g + g_sb + it * (SB_U // RING)
                    col = it * (PAIRS_IT * P)
                    for j in range(PAIRS_IT):
                        load(cols(w_in, l, col + (SQ + j * P)), gi, SBQ[j])
                        load(cols(w_in, l, col + (SK + j * P)), gi, SBQ[j] + 1)
                        load(cols(w_in, l, col + (SV + j // 2 * 2 * P), 2 * P, j % 2 * 4, 4), gi, SBQ[j] + 2)
                        if j:
                            load(cols(w_in, l, col + (GA + (j - 1) * P)), gi, SBQ[j] + 3)
                    load(cols(w_in, l, col + (GA + (PAIRS_IT - 1) * P)), gi, SB_U)
                with sp_e.Fori(0, H) as it:
                    gi = g + g_ml + it * (ML_U // RING)
                    load(cols(w_in, l, it * QK + MQ), gi, 1)
                    load(cols(w_in, l, it * QK + MK), gi, 2)
                    load(cols(w_in, l, it * V + MV, V, 0, 4), gi, 3)
                    load(cols(w_in, l, it * V + MV, V, 4, 4), gi, 4)
                    load(cols(w_in, l, it * V + MO), gi, 5)
                    load(cols(w_in, l, it * V + (MO + P)), gi, 6)
                    load(cols(w_in, l, it * V + GB), gi, 7)
                    load(cols(w_in, l, it * V + (GB + P)), gi, 8)
                with sp_e.Fori(0, KB // 2) as it:
                    gi = g + g_pj + it * (PJ_U // RING)
                    for n in range(2):
                        load(cols_std(w_proj_b, l, it * (2 * P) + n * P), gi, 1 + 2 * n)
                        load(cols_std(w_proj_a, l, it * (2 * P) + n * P), gi, 2 + 2 * n)
                for n in range(8):
                    load(cols_std(w_out, l, (n // 4) * 512, 512, 2 * (n % 4), 2), g + g_out, 1 + n)
                load(cols(router_w, l, 0, E), g + g_out, 9, E * KB)

                def expert_in(w, l, e):
                    return w[ds(l), ds(e)].rearrange("o q (p k) f -> (o q p) k f", k=KB)

                def expert_out(l, e):
                    return w_down[ds(l), ds(e)].rearrange("o q p (k d) -> (o q p) k d", d=D)

                def shared_out(l, b):
                    return sh_down[ds(l), b * P:(b + 1) * P].rearrange("o p (k d) -> (o p) k d", d=D)

                load(cols(sh_gate, l, 0), g + g_out, 10)
                load(cols(sh_up, l, 0), g + g_out, 11)

                def expert_units(e, gi, i, down):
                    load(expert_in(w_gate, l, e), gi, i)
                    load(expert_in(w_up, l, e), gi, i + 1)
                    load(down, gi, i + 2)

                expert_units(0, g + g_moe, 0, shared_out(l, 0))
                with sp_e.Fori(0, E // EXP_IT - 1) as it:
                    for n in range(EXP_IT):
                        expert_units(it * EXP_IT + (n + 1), g + g_moe + it * 3, 3 * (n + 1),
                                     expert_out(l, it * EXP_IT + n))
                for n in range(EXP_IT - 1):
                    e = E - EXP_IT + 1 + n
                    expert_units(e, g + g_moe + (E // EXP_IT - 1) * 3, 3 * (n + 1), expert_out(l, e - 1))
                load(cols(sh_gate, l, P), g + g_post, 0)
                load(cols(sh_up, l, P), g + g_post, 1)
                load(expert_out(l, E - 1), g + g_post, 2)
                load(shared_out(l, 1), g + g_post, 3)
            for t in range(TB):
                sp_e.wait_ge(out_ready, t + 1)
                sp_e.dma_start(out[0, t * P:(t + 1) * P, :], x_sb[:, t, :]).then_inc(stored, 16)
            sp_e.wait_ge(stored, TB * 16)

        @block.gpsimd
        def _(pool):
            pool.sem_inc(ada_summed, 2)
            ks = [0]

            def step(ins):
                ks[0] += 1
                ins.then_inc(consts, 1)
                pool.wait_ge(consts, ks[0])

            step(nc.gpsimd.memset(ones[:], 1.0))
            step(nc.gpsimd.memset(ident[:], 0.0))
            step(nc.gpsimd.affine_select(out=ident[:], in_=ident[:], compare_op=ALU.not_equal, fill=1.0,
                                         base=0, pattern=[[-1, P]], channel_multiplier=1))
            step(nc.gpsimd.tensor_copy(ident_r[:], ident[:]))
            f = sp[:, 0, 0:P]
            step(nc.gpsimd.memset(f, 0.0))
            step(nc.gpsimd.tensor_copy(zeros_r[:], f))
            step(nc.gpsimd.affine_select(out=f, in_=f, compare_op=ALU.is_gt, fill=MASKED,
                                         base=0, pattern=[[1, P]], channel_multiplier=-1))
            step(nc.gpsimd.tensor_copy(negmask[:], f))
            step(nc.gpsimd.memset(f, -1.0))
            step(nc.gpsimd.tensor_copy(negones[:], f))
            step(nc.gpsimd.affine_select(out=f, in_=f, compare_op=ALU.is_ge, fill=0.0,
                                         base=0, pattern=[[-1, P]], channel_multiplier=1))
            step(nc.gpsimd.tensor_copy(negtri[:], f))
            step(nc.gpsimd.memset(head_sel[:], 0.0))
            step(nc.gpsimd.affine_select(out=head_sel[:], in_=head_sel[:], compare_op=ALU.not_equal, fill=1.0,
                                         base=0, pattern=[[-1, H], [0, P]], channel_multiplier=1))
            step(nc.gpsimd.memset(v_lo[:].bitcast(F32), 0.0))
            step(nc.gpsimd.tensor_copy(v_hi[:, :, V:VA], ones[:, 0:4].rearrange("p (a b) -> p a b", b=2)))
            step(nc.gpsimd.memset(qk_pad[:], 0.0))

            def conditioning(l, part):
                pool.wait_ge(ada_red, l * 3 + part)
                hold(pool, pool_held)
                nc.gpsimd.memset(ada_acc[:], 0.0).then_inc(ada_zero, 1)
                pool.wait_ge(ada_zero, l * 3 + part)
                hold(pool, pool_held)

                def load(k, j):
                    pool.dma_start(ada_raw[:, j, :],
                                   ada_w[ds(l), :, part * 2 * D:(part + 1) * 2 * D].rearrange(
                                       "o (p k) n -> (o p) k n", k=KB)[:, ds(k), :]).then_inc(ada_loaded[j], 16)

                def two_pieces(it, more):
                    n = l * KB + (part - 1) * (KB // 2) + it
                    for j in range(2):
                        pool.wait_ge(ada_loaded[j], n * 16 + 16)
                        hold(pool, pool_held)
                        nc.gpsimd.tensor_tensor(ada_raw[:, j, :], ada_raw[:, j, :],
                                                cond[:, ds(it * 2 + j)].to_broadcast([P, 2 * D]), ALU.mult
                                                ).then_inc(ada_scaled, 1)
                        pool.wait_ge(ada_scaled, l * 16 + n * 2 + (j + 1))
                        pool.wait_ge(ada_summed, n * 2 + (j + 2))
                        hold(pool, pool_held)
                        nc.gpsimd.tensor_tensor(ada_acc[:], ada_acc[:], ada_raw[:, j, :], ALU.add).then_inc(ada_summed, 1)
                        if more:
                            pool.wait_ge(ada_summed, n * 2 + (j + 3))
                            hold(pool, pool_held)
                            load(it * 2 + (j + 2), j)

                for j in range(2):
                    load(j, j)
                with pool.Fori(0, KB // 2 - 1) as it:
                    two_pieces(it, True)
                two_pieces(KB // 2 - 1, False)
                pool.wait_ge(ada_summed, l * 16 + (8 * part + 2))
                pool.sem_inc(acc_ready, 1)

            assert ks[0] == N_CONST, ks[0]
            with pool.Fori(0, L) as l:
                small = []

                def load_small(dst, src):
                    small.append(pool.dma_start(dst, src).then_inc(par_loaded, 16))

                load_small(par_rows[0:NT * KB, :], conv_w[ds(l)].rearrange("o t (b p) -> (o t b) p", p=P))
                load_small(par_rows[NT * KB:NT * KB + KB, :], conv_b[ds(l), :].rearrange("o (b p) -> (o b) p", p=P))
                load_small(par_rows[NT * KB + KB:NROW, :], m_norm_w[ds(l), :].rearrange("o (b p) -> (o b) p", p=P))
                bv = ada_b[ds(l), :].rearrange("o (s p k) -> (o p) s k", k=KB, p=P)
                load_small(bcol[:, 0:2, :], bv[:, 0:2, :])
                load_small(bcol[:, 2:4, :], bv[:, 3:5, :])
                load_small(nw[:, 0, :], norm1_w[ds(l), :].rearrange("o (p k) -> (o p) k", k=KB))
                load_small(nw[:, 1, :], norm2_w[ds(l), :].rearrange("o (p k) -> (o p) k", k=KB))
                load_small(gbias[:, 0:1], m_igate_b[ds(l), :].rearrange("o h -> h o"))
                load_small(gbias[:, 1:2], m_fgate_b[ds(l), :].rearrange("o h -> h o"))
                load_small(g1_sb[:], ada_b[ds(l), 2 * D:3 * D].to_broadcast([P, D]))
                load_small(rb[:], router_b[ds(l), :].to_broadcast([P, E]))
                assert len(small) == N_SMALL
                pool.wait_ge(adan_used, l * 16 + 1)
                pool.sem_inc(acc_ready, 1)
                pool.wait_ge(mix_added, l * 8 + 4)
                hold(pool, pool_held)
                for w in (qz_hi, qz_lo):
                    nc.gpsimd.memset(w.bitcast(F32), 0.0).then_inc(q_zeroed, 1)
                pool.dma_start(g2_sb[:], ada_b[ds(l), 5 * D:6 * D].to_broadcast([P, D])).then_inc(g2_loaded, 16)
                conditioning(l, 1)
                pool.wait_ge(w_ready, l * (2 * H) + 2 * H)
                hold(pool, pool_held)
                for w in (w_s0[:, :, 0:P], w_s1):
                    nc.gpsimd.affine_select(out=w, in_=w, compare_op=ALU.is_ge, fill=0.0, base=0,
                                            pattern=[[0, H], [1, P]], channel_multiplier=-1).then_inc(w_masked, 1)
                conditioning(l, 2)
                pool.wait_ge(ada_red, l * 3 + 3)
                hold(pool, pool_held)
                nc.gpsimd.memset(ada_acc[:], 0.0).then_inc(ada_zero, 1)
                pool.wait_ge(ada_zero, l * 3 + 3)
                hold(pool, pool_held)
                pool.wait_ge(gT_ready, l * 1 + 1)
                hold(pool, pool_held)
                pool.dma_start(gates_dram, gT).then_inc(gT_stored, 16)
                pool.wait_ge(gT_stored, l * 16 + 16)
                hold(pool, pool_held)
                for e in (2, 3):
                    pool.dma_start(gate_b[:, e, :], gates_dram[e:e + 1, :].to_broadcast([P, T])).then_inc(gate_loaded[1], 16)
                with pool.Fori(0, 2) as half, pool.Fori(0, KB) as k:
                    it = half * KB + k
                    with pool.If_lt(pool.to_reg(l), L - 1):
                        pool.wait_ge(adan_used, l * 16 + it + 1)
                        hold(pool, pool_held)
                        nl = nc.s_assert_within(l + 1, 0, L - 1,
                                                skip_runtime_bounds_check_because="l < L - 1 in this branch")
                        pool.dma_start(ada_raw[:, 0, 0:D],
                                       ada_w[ds(nl), :, ds(half * D, D)].rearrange(
                                           "o (p k) n -> (o p) k n", k=KB)[:, ds(k), :]).then_inc(adan_loaded, 16)
                        pool.wait_ge(adan_loaded, (l * 16 + it + 1) * 16)
                        hold(pool, pool_held)
                        nc.gpsimd.tensor_tensor(ada_raw[:, 0, 0:D], ada_raw[:, 0, 0:D],
                                                cond[:, ds(k)].to_broadcast([P, D]), ALU.mult).then_inc(ada_scaled, 1)
                        pool.wait_ge(ada_scaled, l * 32 + it + 17)
                        hold(pool, pool_held)
                        nc.gpsimd.tensor_tensor(ada_acc[:, ds(half * D, D)], ada_acc[:, ds(half * D, D)],
                                                ada_raw[:, 0, 0:D], ALU.add).then_inc(adan_used, 1)
                    with pool.If_lt(pool.to_reg(it), E // EXP_IT - 1):
                        nx = nc.s_assert_within(it + 1, 0, E // EXP_IT - 1,
                                                skip_runtime_bounds_check_because="it is below the last in this branch")
                        for e in range(EXP_IT):
                            if e == 2:
                                pool.wait_ge(gate_loaded[0], (l * (E // EXP_IT - 1) + it + 1) * 32)
                                pool.sem_inc(gate_ready, 1)
                            pool.wait_ge(hid_full, l * EV + it * EXP_IT + (e + 5))
                            hold(pool, pool_held)
                            pool.dma_start(gate_b[:, e, :], gates_dram[ds(nx * EXP_IT + e), :].to_broadcast([P, T])
                                           ).then_inc(gate_loaded[e // 2], 16)
            pool.wait_ge(mix_added, L * 8 + 4)
            pool.dma_start(g1_sb[:], final_norm_w.rearrange("(o d) -> o d", o=1).to_broadcast([P, D])
                           ).then_inc(par_loaded, 16)

        @block.scalar
        def _(act):
            act.wait_ge(c_loaded, 16)
            nc.scalar.activation(c_sb[:, 1, :], c_sb[:, 0, :], ACT.Sigmoid).then_inc(sig_ready, 1)

            def split(g, i, width=1024):
                act.wait_ge(unit_used, g * RING + i + 1)
                act.wait_ge(raw_loaded[i % RING], (g + i // RING + 1) * 16)
                nc.scalar.activation(w_hi[:, i % RING, 0:width], raw[:, i % RING, 0:width], ACT.Copy
                                     ).then_inc(hi_ready, 1)

            def used(g, i):
                act.wait_ge(unit_used, g * RING + (i + 1 + RING))

            def norm_in(order, whole):
                for t, h in order:
                    act.wait_ge(mix_added, whole)
                    whole = whole + 1
                    nc.scalar.activation(xn[:, t, h * 512:(h + 1) * 512], x_sb[:, t, h * 512:(h + 1) * 512],
                                         ACT.Square, accum_out=st[:, h, t:t + 1]).then_inc(ss_done, 1)

            def norm_hi(n, which):
                def full(b):
                    if b:
                        act.wait_ge(h_ready, n * 4 + (b - 1))
                    act.wait_ge(tr_done, n * 4 + b + 1)
                    for k in range(2):
                        kk = 2 * b + k
                        ins = nc.scalar.activation(h_full[:, b % 2, k * T:(k + 1) * T], PS[:, b, k * T:(k + 1) * T],
                                                   ACT.Identity, scale=ab[:, which, 0, kk:kk + 1],
                                                   bias=ab[:, which, 1, kk:kk + 1])
                    ins.then_inc(hfa_ready, 1)
                    act.wait_ge(hfa_ready, n * 2 + (b // 2 + 1))

                def high(b):
                    nc.scalar.activation(h_hi[:, 2 * b:2 * b + 2, :], h_full[:, b % 2, :].rearrange(
                        "p (k t) -> p k t", t=T), ACT.Copy).then_inc(hhi_ready, 1)

                act.wait_ge(ab_ready, n + 1)
                for b in (0, 2):
                    full(b)
                    high(b)
                    act.wait_ge(hf_ready, n * 2 + (b // 2 + 1))
                    high(b + 1)

            norm_in(BY_ROWS, 1)
            with act.Fori(0, L) as l:
                g = l * GL
                split(g, 0, 2 * H * KB)
                split(g, 1)
                split(g, 2)
                norm_hi(l * 2, 0)
                split(g, 3)
                nc.scalar.preload_act_table_set(LEXP)
                act.wait_ge(row_v, l * 3 + 3)
                nc.scalar.activation(r_t, r_t, ACT.Exp, scale=-1.0).then_inc(row_a, 1)
                act.wait_ge(row_a, l * 3 + 1)
                nc.scalar.activation(r_t, r_t, ACT.Ln, bias=1.0).then_inc(row_a, 1)
                act.wait_ge(row_v, l * 3 + 4)
                nc.scalar.activation(r_e, r_e, ACT.Exp, scale=-1.0).then_inc(row_a, 1)

                with act.Fori(0, NPAIR // PAIRS_IT) as it:
                    gi = g + g_sb + it * (SB_U // RING)
                    pr = l * NPAIR + it * PAIRS_IT

                    def att_part(n):
                        act.wait_ge(l_done, n + 1)
                        nc.scalar.activation(attf, scores_bank(par2), ACT.Exp).then_inc(att_ready, 1)
                        act.wait_ge(att_ready, n + 1)
                        nc.scalar.activation(att_hi[:], att[:], ACT.Copy).then_inc(atthi_ready, 1)

                    def av_part(n, jj):
                        act.wait_ge(av_done, n + 1)
                        for a in range(2):
                            q = slice(a * DH, (a + 1) * DH)
                            nc.scalar.activation(hs_hi[q, ds(jj), :],
                                                 PS[q, 3:4, a * T:(a + 1) * T], ACT.Copy).then_inc(hshi_ready, 1)

                    def ga_part(i, jj, bank=2):
                        split(gi, i + AHEAD)
                        used(gi, i)
                        nc.scalar.activation(ga_sb[:, ds(jj), :], PS[:, bank:bank + 1, 0:T], ACT.Copy).then_inc(g_evac, 1)

                    for j in range(PAIRS_IT):
                        n, u = pr + j, SBQ[j]
                        split(gi, u + AHEAD)
                        split(gi, u + 1 + AHEAD)
                        used(gi, u + 1)
                        act.wait_ge(q_zeroed, l * 2 + 2)
                        for a in range(2):
                            q = slice(a * DH, (a + 1) * DH)
                            nc.scalar.activation(qz_hi[q, a, :], PS[q, 0, 0:T], ACT.Copy, scale=DH ** -0.5)
                        nc.scalar.activation(qk_hi[:, 1, :], PS[:, 0, T:2 * T], ACT.Copy).then_inc(qkhi_ready, 1)
                        if j:
                            par2 = (j - 1) % 2
                            att_part(n - 1)
                        split(gi, u + 2 + AHEAD)
                        if j % 2:
                            used(gi, u + 2)
                            nc.scalar.activation(sv_hi[:].rearrange("p a b -> p (a b)"), PS[:, 1, :], ACT.Copy
                                                 ).then_inc(vhi_ready, 1)
                        act.wait_ge(z_done, n + 1)
                        nc.scalar.activation(ztf, scores_bank(j % 2), ACT.Abs
                                             ).then_inc(ln_ready, 1)
                        act.wait_ge(ln_ready, n * 3 + 1)
                        nc.scalar.activation(zt[:], zt[:], ACT.Exp, scale=-1.0).then_inc(ln_ready, 1)
                        act.wait_ge(ln_ready, n * 3 + 2)
                        nc.scalar.activation(zt[:], zt[:], ACT.Ln, bias=1.0).then_inc(ln_ready, 1)
                        if j:
                            ga_part(u + 3, it * PAIRS_IT + (j - 1))
                            av_part(n - 1, it * PAIRS_IT + (j - 1))
                    par2 = (PAIRS_IT - 1) % 2
                    att_part(pr + (PAIRS_IT - 1))
                    ga_part(SB_U, it * PAIRS_IT + (PAIRS_IT - 1), 0)
                    av_part(pr + (PAIRS_IT - 1), it * PAIRS_IT + (PAIRS_IT - 1))

                act.wait_ge(rows_t, l * 1 + 1)
                nc.scalar.activation(M_sb[:].rearrange("p (a b) t -> p a (b t)", a=2), PS[:, 6:8, :], ACT.Copy
                                     ).then_inc(mb_ready, 1)

                act.wait_ge(mb_ready, l * 1 + 1)
                act.wait_ge(cols_ready, l * 2 + 1)
                for h in range(H):
                    nc.scalar.activation(w_s1[:, h, :], M_sb[:, h, P:T], ACT.Exp, bias=ucol[:, 1, h:h + 1],
                                         scale=-1.0).then_inc(w_ready, 1)
                act.wait_ge(w_ready, l * (2 * H) + H)
                for h in range(H):
                    nc.scalar.activation(w_s0[:, h, :], M_sb[:, h, :], ACT.Exp, bias=ucol[:, 0, h:h + 1],
                                         scale=-1.0).then_inc(w_ready, 1)

                with act.Fori(0, H) as it:
                    gi = g + g_ml + it * (ML_U // RING)
                    n = l * H + it
                    split(gi, 1 + AHEAD)
                    split(gi, 2 + AHEAD)
                    used(gi, 2)
                    nc.scalar.activation(qk_pad[:, :, NT - 1:NT - 1 + T], PS[:, 0, :].rearrange(
                        "p (a t) -> p a t", t=T), ACT.Copy).then_inc(pad_ready, 1)
                    split(gi, 3 + AHEAD)
                    act.wait_ge(conv_ready, n + 1)
                    nc.scalar.activation(sig[:], conv[:], ACT.Sigmoid).then_inc(sig_ready, 1)
                    used(gi, 4)
                    nc.scalar.activation(v_hi[:, :, 0:V], PS[:, 1, :].rearrange("p (a v) -> p a v", v=V), ACT.Copy
                                         ).then_inc(vhi_ready, 1)
                    act.wait_ge(qkf_ready, n + 1)
                    nc.scalar.activation(qk_hi[:], conv[:], ACT.Copy).then_inc(qkhi_ready, 1)
                    split(gi, 4 + AHEAD)
                    split(gi, 5 + AHEAD)
                    act.wait_ge(sf_ready, n + 1)
                    nc.scalar.activation(S_hi, S_f, ACT.Copy).then_inc(shi_ready, 1)
                    split(gi, 6 + AHEAD)
                    split(gi, 7 + AHEAD)
                    used(gi, 6)
                    nc.scalar.activation(mo_sb[:], PS[:, 2, :].rearrange("p (a t) -> p a t", t=T), ACT.Sigmoid
                                         ).then_inc(sigo_ready, 1)
                    act.wait_ge(r_ready, n + 1)
                    for t in range(TB):
                        nc.scalar.activation(hmn[:, t, :], PS[:, 4 + t, 0:V], ACT.Square, scale=st[:, 2, t:t + 1],
                                             accum_out=st[:, 3, t:t + 1]).then_inc(sq_ready, 1)
                    split(gi, 8 + AHEAD)
                    used(gi, 8)
                    nc.scalar.activation(gb_sb[:, ds(it * 2, 2), :], PS[:, 7, :].rearrange("p (a t) -> p a t", t=T),
                                         ACT.Copy).then_inc(g_evac, 1)
                    act.wait_ge(hmf_ready, n + 1)
                    nc.scalar.activation(hm_hi[:, ds(it * 2, 2), :], conv[:], ACT.Copy).then_inc(hmhi_ready, 1)

                with act.Fori(0, KB // 2) as it:
                    gi = g + g_pj + it * (PJ_U // RING)
                    for b in range(2):
                        n = l * KB + it * 2 + b
                        split(gi, 2 * b + 1 + AHEAD)
                        act.wait_ge(yf_ready, n + 2)
                        nc.scalar.activation(sig[:, 0, :], ga_sb[:, ds(it * 2 + b), :].rearrange("p a t -> p (a t)"),
                                             ACT.Sigmoid).then_inc(sg_ready, 1)
                        nc.scalar.activation(sig[:, 1, :], gb_sb[:, ds(it * 2 + b), :].rearrange("p a t -> p (a t)"),
                                             ACT.Sigmoid).then_inc(sg_ready, 1)
                        split(gi, 2 * b + 2 + AHEAD)
                        act.wait_ge(yf_ready, n + 3)
                        nc.scalar.activation(h_hi[:, ds(it * 2 + b), :], y1.rearrange("p (a t) -> p a t", a=1),
                                             ACT.Copy).then_inc(yhi_ready, 1)
                for i in range(8):
                    split(g + g_out, i + 1 + AHEAD, E * KB if i + 1 + AHEAD == 9 else 1024)
                norm_in(BY_HALVES, l * 8 + 5)
                split(g + g_out, 9 + AHEAD)
                norm_hi(l * 2 + 1, 1)
                used(g + g_out, 9)
                nc.scalar.activation(scT, PS[0:E, 4, 0:T], ACT.Sigmoid
                                     ).then_inc(rt_ready, 1)
                split(g + g_out, 10 + AHEAD)

                def hidden(n, par, gi, i):
                    used(gi, i)
                    nc.scalar.activation(sig[:, par, :], PS[:, 6 + par, 0:T], ACT.Silu).then_inc(silu_ready, 1)
                    act.wait_ge(hid_full, n + 4)
                    nc.scalar.activation(hid_hi[:, par, :], conv[:, par, :], ACT.Copy).then_inc(hidhi_ready, 1)

                split(g + g_out, 11 + AHEAD)
                hidden(l * EV, 1, g + g_out, 11)
                act.wait_ge(gb_done, l * 1 + 1)
                nc.scalar.activation(gate_b[:, 0:2, :], two(PS[:, 5, :]), ACT.Copy).then_inc(gate_ready, 1)
                with act.Fori(0, E // EXP_IT) as it:
                    gi = g + g_moe + it * 3
                    for e in range(EXP_IT):
                        split(gi, 3 * e + AHEAD)
                        split(gi, 3 * e + 1 + AHEAD)
                        hidden(l * EV + it * EXP_IT + (e + 1), e % 2, gi, 3 * e + 1)
                        split(gi, 3 * e + 2 + AHEAD)
                split(g + g_post, AHEAD)
                hidden(l * EV + (E + 1), 0, g + g_post, 1)
                norm_in(BY_ROWS, l * 8 + 9)

        @block.vector
        def _(dve):
            steps = Steps(dve, dve_step, ND)
            link = steps.link
            v = nc.vector
            dve.sem_inc(lo_ready, RING)
            dve.sem_inc(s_ready, 1)
            dve.sem_inc(yf_ready, 2)
            dve.sem_inc(hm_ready, 1)
            dve.sem_inc(y_ready, 1)
            dve.sem_inc(hid_full, 3)
            v.memset(ada_acc[:], 0.0).then_inc(row_v, 1)
            dve.wait_ge(x_loaded, 16)
            dve.sem_inc(mix_added, 4)
            dve.wait_ge(sig_ready, 1)
            v.tensor_tensor(cond[:], c_sb[:, 0, :], c_sb[:, 1, :], ALU.mult).then_inc(row_v, 1)
            def split(g, i, width=1024):
                dve.wait_ge(hi_ready, g * RING + i + 1)
                s = i % RING
                v.tensor_tensor(w_lo[:, s, 0:width], raw[:, s, 0:width], w_hi[:, s, 0:width].bitcast(F32),
                                ALU.subtract).then_inc(lo_ready, 1)

            def used(g, i):
                dve.wait_ge(unit_used, g * RING + (i + 1 + RING))

            def rsqrt(b, y, t):
                link(v.tensor_scalar(y.bitcast(mybir.dt.int32), b.bitcast(mybir.dt.int32), -0.5,
                                     1597463007.0 - 2.0 ** 22 - 2.0 ** 31, ALU.mult, ALU.add))
                col = [slice(0, 1), slice(1, 2)]
                for i in range(3):
                    for c in col:
                        if i:
                            steps.wait_for(steps.k - 1)
                        steps.count(v.scalar_tensor_tensor(t[:, c], y[:, c], b[:, c], y[:, c], ALU.mult, ALU.mult))
                    for c in col:
                        steps.wait_for(steps.k - 1)
                        steps.count(v.scalar_tensor_tensor(y[:, c], t[:, c], 1.5, y[:, c], ALU.subtract, ALU.mult))
                steps.wait_for(steps.k)

            def rstd(n):
                dve.wait_ge(ss_done, n * 4 + 4)
                link(v.tensor_tensor(st[:, 1, :], st[:, 0, :], st[:, 1, :], ALU.add))
                link(v.tensor_scalar(st[:, 1, :], st[:, 1, :], 0.5 / D, 0.5 * EPS, ALU.mult, ALU.add))
                rsqrt(st[:, 1, :], st[:, 7, :], st[:, 6, :])

            def norm(n):
                rstd(n)
                for t in range(TB):
                    v.tensor_scalar(xn[:, t, :], x_sb[:, t, :], st[:, 7, t:t + 1], None, ALU.mult
                                    ).then_inc(xn_ready, 1)

            def modulated(n, which):
                def full(b):
                    if b == 3:
                        dve.wait_ge(h_ready, n * 4 + (b - 1))
                    dve.wait_ge(tr_done, n * 4 + b + 1)
                    for k in range(2):
                        kk = 2 * b + k
                        ins = v.tensor_scalar(h_full[:, b % 2, k * T:(k + 1) * T], PS[:, b, k * T:(k + 1) * T],
                                              ab[:, which, 0, kk:kk + 1], ab[:, which, 1, kk:kk + 1],
                                              ALU.mult, ALU.add)
                    ins.then_inc(hf_ready, 1)

                def low(b):
                    dve.wait_ge(hhi_ready, n * 4 + b + 1)
                    v.tensor_tensor(h_lo[:, 2 * b:2 * b + 2, :], h_full[:, b % 2, :].rearrange("p (k t) -> p k t", t=T),
                                    h_hi[:, 2 * b:2 * b + 2, :].bitcast(F32), ALU.subtract).then_inc(h_ready, 1)

                for b in (1, 3):
                    full(b)
                    low(b - 1)
                    low(b)

            def factor(which, cols):
                link(v.tensor_tensor(ab[:, which, 0, :], cols, bcol[:, 2 * which + 1, :], ALU.add))
                link(v.scalar_tensor_tensor(ab[:, which, 0, :], ab[:, which, 0, :], 1.0, nw[:, which, :],
                                            ALU.add, ALU.mult))
                dve.sem_inc(ab_ready, 1)

            dve.wait_ge(row_v, 2)
            for k in range(KB):
                dve.wait_ge(ada0_loaded[k % 3], (k // 3 + 1) * 16)
                v.scalar_tensor_tensor(ada_acc[:], ada0_raw[k % 3], cond[:, k:k + 1], ada_acc[:], ALU.mult, ALU.add
                                       ).then_inc(ada0_used, 1)
                dve.wait_ge(ada0_used, k + 1)
                if k == 3:
                    norm(0)
            dve.sem_inc(adan_used, 1)
            assert steps.k == N_NORM, steps.k

            with dve.Fori(0, L) as l:
                g = l * GL
                steps.at(l * ND + N_NORM)
                split(g, 0, 2 * H * KB)
                split(g, 1)
                dve.wait_ge(par_t, l * 1 + 1)
                link(v.tensor_copy(par[:], PS[:, 6, 0:NROW]))
                dve.wait_ge(ada_red, l * 3 + 1)
                link(v.tensor_tensor(ab[:, 0, 1, :], PS[:, 7, 0:KB], bcol[:, 0, :], ALU.add))
                factor(0, PS[:, 7, KB:2 * KB])
                modulated(l * 2, 0)
                split(g, 2)
                split(g, 3)
                used(g, 0)
                link(v.tensor_scalar(r_i, PS[0:H, 4, 0:T], gbias[:, 0:1], None, ALU.add))
                link(v.tensor_scalar(r_f, PS[0:H, 4, T:2 * T], gbias[:, 1:2], None, ALU.add))
                link(v.tensor_scalar(r_b, r_f, -1.0, None, ALU.mult))
                v.tensor_tensor(r_t, r_f, r_b, ALU.max).then_inc(row_v, 1)
                dve.wait_ge(row_a, l * 3 + 2)
                link(v.scalar_tensor_tensor(r_f, r_f, 0.0, r_t, ALU.min, ALU.subtract))
                link(v.memset(r_m, 0.0))
                link(v.tensor_tensor_scan(r_b, r_f, r_m, 0.0, ALU.add, ALU.add))
                link(v.tensor_tensor(r_i, r_i, r_b, ALU.subtract))
                link(v.tensor_tensor_scan(r_f, r_i, r_m, 0.0, ALU.max, ALU.max))
                v.tensor_tensor(r_e, r_b, r_f, ALU.add).then_inc(row_v, 1)
                dve.wait_ge(row_a, l * 3 + 3)
                for r, src in enumerate((r_i, r_f, r_e)):
                    ins = v.tensor_copy(row_keep[r], src)
                ins.then_inc(row_v, 1)
                n_head = steps.k

                with dve.Fori(0, NPAIR // PAIRS_IT) as it:
                    gi = g + g_sb + it * (SB_U // RING)
                    pr = l * NPAIR + it * PAIRS_IT

                    def att_part(n):
                        dve.wait_ge(atthi_ready, n + 1)
                        v.tensor_tensor(att_lo[:], att[:], att_hi[:].bitcast(F32), ALU.subtract).then_inc(attlo_ready, 1)

                    def av_part(n, jj):
                        dve.wait_ge(hshi_ready, n * 2 + 2)
                        for a in range(2):
                            q = slice(a * DH, (a + 1) * DH)
                            ins = v.tensor_tensor(hs_lo[q, ds(jj), :], PS[q, 3:4, a * T:(a + 1) * T],
                                                  hs_hi[q, ds(jj), :].bitcast(F32), ALU.subtract)
                        ins.then_inc(hs_ready, 1)

                    for j in range(PAIRS_IT):
                        n, u = pr + j, SBQ[j]
                        split(gi, u + AHEAD)
                        split(gi, u + 1 + AHEAD)
                        dve.wait_ge(qkhi_ready, l * (NPAIR + H) + it * PAIRS_IT + (j + 1))
                        dve.wait_ge(q_zeroed, l * 2 + 2)
                        for a in range(2):
                            q = slice(a * DH, (a + 1) * DH)
                            v.scalar_tensor_tensor(qz_lo[q, a, :], PS[q, 0, 0:T], DH ** -0.5,
                                                   qz_hi[q, a, :].bitcast(F32), ALU.mult, ALU.subtract)
                        v.tensor_tensor(qk_lo[:, 1, :], PS[:, 0, T:2 * T], qk_hi[:, 1, :].bitcast(F32),
                                        ALU.subtract).then_inc(qk_ready, 1)
                        if j:
                            att_part(n - 1)
                        split(gi, u + 2 + AHEAD)
                        if j % 2:
                            dve.wait_ge(vhi_ready, l * NVAL + it * (PAIRS_IT // 2) + (j // 2 + 1))
                            v.tensor_tensor(sv_lo[:].rearrange("p a b -> p (a b)"), PS[:, 1, :],
                                            sv_hi[:].rearrange("p a b -> p (a b)").bitcast(F32),
                                            ALU.subtract).then_inc(v_ready, 1)
                        dve.wait_ge(ln_ready, n * 3 + 3)
                        v.scalar_tensor_tensor(spf, scores_bank(j % 2), 0.0, ztf,
                                               ALU.max, ALU.add).then_inc(sp_ready, 1)
                        dve.wait_ge(sp_ready, n + 1)
                        v.tensor_copy(sp_hi[:], sp[:]).then_inc(sphi_ready, 1)
                        dve.wait_ge(sphi_ready, n + 1)
                        v.tensor_tensor(sp_lo[:], sp[:], sp_hi[:].bitcast(F32), ALU.subtract).then_inc(splo_ready, 1)
                        if j:
                            split(gi, u + 3 + AHEAD)
                            av_part(n - 1, it * PAIRS_IT + (j - 1))
                    att_part(pr + (PAIRS_IT - 1))
                    split(gi, SB_U + AHEAD)
                    av_part(pr + (PAIRS_IT - 1), it * PAIRS_IT + (PAIRS_IT - 1))

                steps.at(l * ND + N_NORM + n_head)
                dve.wait_ge(rows_t, l * 1 + 1)
                v.tensor_copy(ucol[:], PS[:, 1, 0:TB * H].rearrange("p (a h) -> p a h", h=H))
                v.tensor_copy(emcol[:], PS[:, 1, TB * H:2 * TB * H].rearrange("p (a h) -> p a h", h=H)
                              ).then_inc(cols_ready, 1)
                dve.wait_ge(ada_red, l * 3 + 2)
                v.tensor_tensor(ab[:, 1, 1, :], PS[:, 1, 64:64 + KB], bcol[:, 2, :], ALU.add).then_inc(cols_ready, 1)
                v.tensor_tensor(g1_sb[:], PS[:, 4:6, :].rearrange("p a b -> p (a b)"), g1_sb[:], ALU.add
                                ).then_inc(g_ready, 1)
                dve.wait_ge(cols_ready, l * 2 + 2)
                hold(dve, dve_held)
                n_mid = n_head + steps.k

                with dve.Fori(0, H) as it:
                    gi = g + g_ml + it * (ML_U // RING)
                    n = l * H + it
                    steps.at(l * ND + N_NORM + n_mid + it * N_HEAD)
                    split(gi, 1 + AHEAD)
                    split(gi, 2 + AHEAD)
                    dve.wait_ge(hm_ready, n + 1)
                    dve.wait_ge(pad_ready, n + 1)

                    base_conv = steps.k

                    def tap(a, j):
                        return par[:, ds(it + (j * KB + a * H))]

                    for j in range(NT):
                        for a in range(2):
                            if j == 0:
                                ins = v.tensor_scalar(conv[:, a, :], qk_pad[:, a, 0:T], tap(a, 0), tap(a, NT),
                                                      ALU.mult, ALU.add)
                            else:
                                steps.wait_for(base_conv + 2 * j - 1 + a)
                                ins = v.scalar_tensor_tensor(conv[:, a, :], qk_pad[:, a, j:j + T], tap(a, j),
                                                             conv[:, a, :], ALU.mult, ALU.add)
                            if j < NT - 1:
                                steps.count(ins)
                    ins.then_inc(conv_ready, 1)
                    split(gi, 3 + AHEAD)
                    dve.wait_ge(conv_ready, n + 1)
                    dve.wait_ge(sig_ready, n + 2)
                    link(v.scalar_tensor_tensor(conv[:, 0, :], conv[:, 0, :], QK ** -0.5, sig[:, 0, :],
                                                ALU.mult, ALU.mult))
                    v.tensor_tensor(conv[:, 1, :], conv[:, 1, :], sig[:, 1, :], ALU.mult).then_inc(qkf_ready, 1)
                    dve.wait_ge(qkhi_ready, l * (NPAIR + H) + it + (NPAIR + 1))
                    v.tensor_tensor(qk_lo[:], conv[:], qk_hi[:].bitcast(F32), ALU.subtract).then_inc(qk_ready, 1)
                    dve.wait_ge(vhi_ready, l * NVAL + it + (NPAIR // 2 + 1))
                    v.tensor_tensor(v_lo[:, :, 0:V], PS[:, 1, :].rearrange("p (a v) -> p a v", v=V),
                                    v_hi[:, :, 0:V].bitcast(F32), ALU.subtract).then_inc(v_ready, 1)
                    split(gi, 4 + AHEAD)
                    dve.wait_ge(s_done, n + 1)
                    dve.wait_ge(w_masked, l * 2 + 2)
                    v.tensor_tensor(S_f[:, 0:T], PS[:, 3, 0:T], w_s0[:, ds(it), :].rearrange("p a t -> p (a t)"),
                                    ALU.mult)
                    v.tensor_tensor(S_f[:, T:CAUSAL], PS[:, 3, T:CAUSAL],
                                    w_s1[:, ds(it), :].rearrange("p a t -> p (a t)"), ALU.mult).then_inc(sf_ready, 1)
                    dve.wait_ge(shi_ready, n + 1)
                    v.tensor_tensor(S_lo, S_f, S_hi.bitcast(F32), ALU.subtract).then_inc(s_ready, 1)
                    split(gi, 5 + AHEAD)
                    split(gi, 6 + AHEAD)
                    dve.wait_ge(num_done, n + 1)
                    den = PS[:, 4:6, V:V + 1].rearrange("p a b -> p (a b)")
                    em = emcol[:, :, ds(it)].rearrange("p a b -> p (a b)")
                    link(v.tensor_scalar(st[:, 4, :], den, -1.0, None, ALU.mult))
                    link(v.tensor_tensor(st[:, 4, :], st[:, 4, :], den, ALU.max))
                    link(v.tensor_tensor(st[:, 4, :], st[:, 4, :], em, ALU.max))
                    v.reciprocal(st[:, 2, :], st[:, 4, :]).then_inc(r_ready, 1)
                    split(gi, 7 + AHEAD)
                    dve.wait_ge(sq_ready, n * 2 + 2)
                    link(v.tensor_scalar(st[:, 5, :], st[:, 3, :], 0.5 / V, 0.5 * EPS, ALU.mult, ALU.add))
                    rsqrt(st[:, 5, :], st[:, 7, :], st[:, 6, :])
                    link(v.tensor_tensor(st[:, 6, :], st[:, 7, :], st[:, 2, :], ALU.mult))
                    for t in range(TB):
                        v.tensor_scalar(hmn[:, t, :], PS[:, 4 + t, 0:V], st[:, 6, t:t + 1], None, ALU.mult
                                        ).then_inc(hmn_ready, 1)
                    split(gi, 8 + AHEAD)
                    dve.wait_ge(hmt_done, n + 1)
                    dve.wait_ge(sigo_ready, n + 1)
                    for b in range(2):
                        ins = v.scalar_tensor_tensor(conv[:, b, :], PS[:, 6, b * T:(b + 1) * T],
                                                     par[:, ds(it * 2 + (NT * KB + KB + b))], mo_sb[:, b, :],
                                                     ALU.mult, ALU.mult)
                    ins.then_inc(hmf_ready, 1)
                    dve.wait_ge(hmhi_ready, n + 1)
                    v.tensor_tensor(hm_lo[:, ds(it * 2, 2), :], conv[:], hm_hi[:, ds(it * 2, 2), :].bitcast(F32),
                                    ALU.subtract).then_inc(hm_ready, 1)
                    assert steps.k == N_HEAD, steps.k
                n_ml = n_mid + H * N_HEAD
                steps.at(l * ND + N_NORM + n_ml)
                dve.wait_ge(ada_red, l * 3 + 3)
                factor(1, PS[:, 3, 0:KB])
                dve.wait_ge(g2_loaded, l * 16 + 16)
                v.tensor_tensor(g2_sb[:], PS[:, 0:2, :].rearrange("p a b -> p (a b)"), g2_sb[:], ALU.add
                                ).then_inc(g_ready, 1)
                n_ada = n_ml + steps.k

                with dve.Fori(0, KB // 2) as it:
                    gi = g + g_pj + it * (PJ_U // RING)
                    steps.at(l * ND + N_NORM + n_ada + it * 4)
                    for b in range(2):
                        n = l * KB + it * 2 + b
                        split(gi, 2 * b + 1 + AHEAD)
                        split(gi, 2 * b + 2 + AHEAD)
                        dve.wait_ge(sg_ready, n * 2 + 2)
                        used(gi, 2 * b + 2)
                        dve.wait_ge(y_ready, n + 1)
                        link(v.tensor_tensor(y2, PS[:, 4 + b, 0:T], sig[:, 1, :], ALU.mult))
                        link(v.tensor_tensor(y1, PS[:, 4 + b, T:2 * T], sig[:, 0, :], ALU.mult))
                        v.tensor_tensor(y1, y1, y2, ALU.add).then_inc(yf_ready, 1)
                        dve.wait_ge(yhi_ready, n + 1)
                        v.tensor_tensor(h_lo[:, ds(it * 2 + b), :], y1.rearrange("p (a t) -> p a t", a=1),
                                        h_hi[:, ds(it * 2 + b), :].bitcast(F32), ALU.subtract).then_inc(y_ready, 1)
                n_pj = n_ada + KB // 2 * 4
                steps.at(l * ND + N_NORM + n_pj)
                for i in range(8):
                    if i < 7:
                        split(g + g_out, i + 1 + AHEAD, E * KB if i + 1 + AHEAD == 9 else 1024)
                    if i % 4 == 3:
                        h = i // 4
                        for t in range(TB):
                            if t == 0:
                                dve.wait_ge(bank_done, l * 5 + (h + 1))
                            else:
                                used(g + g_out, i + 1)
                            bank = (6 if h == 0 else 0) + t
                            link(v.tensor_tensor(h_full[:, t, :], PS[:, bank, :], g1_sb[:, h * 512:(h + 1) * 512],
                                                 ALU.mult))
                            v.tensor_tensor(x_sb[:, t, h * 512:(h + 1) * 512], x_sb[:, t, h * 512:(h + 1) * 512],
                                            h_full[:, t, :], ALU.add).then_inc(mix_added, 1)
                            dve.wait_ge(mix_added, l * 8 + (5 + 2 * h + t))
                norm(l * 2 + 1)
                split(g + g_out, 8 + AHEAD)
                split(g + g_out, 9 + AHEAD)
                modulated(l * 2 + 1, 1)
                split(g + g_out, 10 + AHEAD)

                dve.wait_ge(sc_turned, l * 1 + 1)
                v.tensor_copy(sc[:].rearrange("p t e -> p (t e)"), PS[:, 5, 0:TB * E])
                for t in range(TB):
                    ins = v.tensor_tensor(sel[:, t, :], PS[:, 5, t * E:(t + 1) * E], rb[:], ALU.add)
                link(ins)
                hold(dve, dve_held)
                for t in range(TB):
                    for q in range(N_GROUPS):
                        ins = v.max(m8[:, t, q, :], sel[:, t, q * EG:(q + 1) * EG])
                link(ins)
                v.memset(gp[:, :, N_GROUPS:16], -FAR)
                link(v.tensor_tensor(gp[:, :, 0:N_GROUPS].rearrange("p a (b c) -> p a b c", c=1), m8[:, :, :, 0:1],
                                     m8[:, :, :, 1:2], ALU.add))
                hold(dve, dve_held)
                for t in range(TB):
                    ins = v.max(t8[:, t, :], gp[:, t, :])
                link(ins)
                link(v.memset(t8[:, :, TOPK_GROUPS:8], -FAR))
                hold(dve, dve_held)
                for t in range(TB):
                    ins = v.match_replace(gr[:, t, :], t8[:, t, :], gp[:, t, :], FAR)
                link(ins)
                link(v.tensor_tensor(gm[:, 0, :, :], gr[:, :, 0:N_GROUPS], gp[:, :, 0:N_GROUPS], ALU.not_equal))
                link(v.tensor_scalar(gm[:, 1, :, :], gm[:, 0, :, :], -1.0, -MASKED, ALU.add, ALU.mult))
                by_group = sel[:].rearrange("p t (q e) -> p (t q) e", e=EG)

                def each(i):
                    return gm[:, i, :, :].rearrange("p t (q o) -> p (t q) o", o=1).to_broadcast([P, TB * N_GROUPS, EG])

                link(v.tensor_tensor(by_group, by_group, each(0), ALU.mult))
                link(v.tensor_tensor(by_group, by_group, each(1), ALU.add))
                split(g + g_out, 11 + AHEAD)
                hold(dve, dve_held)
                for t in range(TB):
                    ins = v.max(t8[:, t, :], sel[:, t, :])
                link(ins)
                hold(dve, dve_held)
                for t in range(TB):
                    ins = v.match_replace(rep[:, t, :], t8[:, t, :], sel[:, t, :], FAR)
                link(ins)
                link(v.tensor_tensor(rep[:], rep[:], sel[:], ALU.not_equal))
                link(v.tensor_tensor(gts[:], rep[:], sc[:], ALU.mult))
                link(v.tensor_reduce(st[:, 4, :], gts[:], AX.X, ALU.add))
                link(v.reciprocal(st[:, 5, :], st[:, 4, :]))
                for t in range(TB):
                    ins = v.tensor_scalar(gts[:, t, :], gts[:, t, :], st[:, 5, t:t + 1], ROUTED_SCALE,
                                          ALU.mult, ALU.mult)
                ins.then_inc(gts_ready, 1)

                def hidden(n, par, gate):
                    dve.wait_ge(silu_ready, n + 1)
                    ins = v.tensor_tensor(conv[:, par, :], sig[:, par, :], PS[:, 6 + par, T:2 * T], ALU.mult)
                    if gate is not None:
                        link(ins)
                        ins = v.tensor_tensor(conv[:, par, :], conv[:, par, :], gate_b[:, gate, :], ALU.mult)
                    ins.then_inc(hid_full, 1)
                    dve.wait_ge(hidhi_ready, n + 1)
                    v.tensor_tensor(hid_lo[:, par, :], conv[:, par, :], hid_hi[:, par, :].bitcast(F32),
                                    ALU.subtract).then_inc(hid_ready, 1)

                hidden(l * EV, 1, None)
                dve.wait_ge(gt_done, l * 1 + 1)
                v.tensor_copy(gT, PS[0:E, 4, 0:T]).then_inc(gT_ready, 1)
                n_moe = n_pj + steps.k
                with dve.Fori(0, E // EXP_IT) as it:
                    gi = g + g_moe + it * 3
                    steps.at(l * ND + N_NORM + n_moe + it * EXP_IT)
                    for e in range(EXP_IT):
                        split(gi, 3 * e + AHEAD)
                        split(gi, 3 * e + 1 + AHEAD)
                        if e == 0:
                            dve.wait_ge(gate_ready, l * (E // EXP_IT) + it + 1)
                        elif e == 2:
                            dve.wait_ge(gate_loaded[1], (l * (E // EXP_IT) + it + 1) * 32)
                        hidden(l * EV + it * EXP_IT + (e + 1), e % 2, e)
                        split(gi, 3 * e + 2 + AHEAD)
                n_post = n_moe + E
                steps.at(l * ND + N_NORM + n_post)
                split(g + g_post, AHEAD)
                hidden(l * EV + (E + 1), 0, None)
                base = steps.k
                for i in range(5):
                    if i < 4:
                        if i < 3:
                            dve.wait_ge(bank_done, l * 5 + (i + 3))
                        else:
                            used(g + g_post, 3)
                        steps.count(v.tensor_tensor(h_part[:, i, :], PS[:, i, :], g2_sb[:, i % 2 * 512:(i % 2 + 1) * 512],
                                                    ALU.mult))
                    if i:
                        steps.wait_for(base + i)
                        t, h = (i - 1) // 2, (i - 1) % 2
                        v.tensor_tensor(x_sb[:, t, h * 512:(h + 1) * 512], x_sb[:, t, h * 512:(h + 1) * 512],
                                        h_part[:, i - 1, :], ALU.add).then_inc(mix_added, 1)
                dve.wait_ge(mix_added, l * 8 + 12)
                norm(l * 2 + 2)
                total = n_post + steps.k
                assert total == ND, total
            dve.wait_ge(xn_ready, L * 4 + 2)
            dve.wait_ge(par_loaded, (L * N_SMALL + 1) * 16)
            for t in range(TB):
                v.tensor_tensor(x_sb[:, t, :], xn[:, t, :], g1_sb[:], ALU.mult).then_inc(out_ready, 1)

        @block.tensor
        def _(pe):
            mm = nc.tensor.matmul
            pe.sem_inc(unit_used, RING)
            pe.wait_ge(consts, N_CONST)

            def three(out, a, b, start, stop, check=False):
                mm(out, a[0], b[0], start=start, stop=False, skip_group_check=True)
                mm(out, a[0], b[1], start=False, stop=False, skip_group_check=True)
                return mm(out, a[1], b[0], start=False, stop=stop, skip_group_check=True)

            def twice(w):
                return w.to_broadcast([w.shape[0], 2, w.shape[2]])

            def unit(g, i, n, nk=KB):
                pe.wait_ge(lo_ready, g * RING + (i + 1 + RING))
                s = i % RING
                return [w[:, s, 0:nk * n].rearrange("p (k n) -> p k n", n=n) for w in (w_hi, w_lo)]

            def feat_major(g, i, out, rhs=None):
                w = unit(g, i, P)
                rh, rl = rhs or (h_hi, h_lo)
                for k in range(KB):
                    ins = three(out, (w[0][:, k, :], w[1][:, k, :]), (rh[:, k, :], rl[:, k, :]), k == 0, k == KB - 1)
                ins.then_inc(unit_used, 1)

            def token_major(g, i, q):
                w = unit(g, i, V, 4)
                for t in range(TB):
                    for k in range(4):
                        kk = 4 * q + k
                        ins = three(PS[:, 1, t * V:(t + 1) * V],
                                    (h_hi[:, kk, t * P:(t + 1) * P], h_lo[:, kk, t * P:(t + 1) * P]),
                                    (w[0][:, k, :], w[1][:, k, :]), kk == 0 and t == 0, kk == KB - 1)
                ins.then_inc(unit_used, 1)

            def turn(n):
                for t in range(TB):
                    pe.wait_ge(xn_ready, n * 2 + (t + 1))
                    for k in range(KB):
                        col = (k % 2) * T + t * P
                        ins = nc.tensor.transpose(PS[:, k // 2, col:col + P], xn[:, t, k:D:KB], ident[:])
                        if t == 1 and k % 2:
                            ins.then_inc(tr_done, 1)

            def ones_cols(off, out_col, bank):
                for k in range(KB):
                    ins = mm(PS[:, bank, out_col + k:out_col + k + 1], ada_acc[:, off + k:off + D:KB], ones[:, 0:1],
                             start=True, stop=True, skip_group_check=True)
                return ins

            def ones_rows(off, bank):
                for h in range(2):
                    ins = mm(PS[:, bank + h, :], ones[:], ada_acc[:, off + h * 512:off + (h + 1) * 512],
                             start=True, stop=True, skip_group_check=True)
                return ins

            with pe.Fori(0, L) as l:
                g = l * GL
                pe.wait_ge(par_loaded, (l + 1) * (N_SMALL * 16))
                hold(pe, pe_held)
                nc.tensor.transpose(PS[:, 6, 0:NROW], par_rows[:], ident[0:NROW, 0:NROW]).then_inc(par_t, 1)
                pe.wait_ge(acc_ready, l * 3 + 1)
                ones_cols(0, 0, 7)
                ones_cols(D, KB, 7).then_inc(ada_red, 1)
                turn(l * 2)
                w = unit(g, 0, 2 * H)
                for a in range(2):
                    for k in range(KB):
                        if a == 0 and k % 2 == 0:
                            pe.wait_ge(h_ready, l * 8 + (k // 2 + 1))
                        ins = three(PS[0:H, 4, a * T:(a + 1) * T],
                                    (w[0][:, k, a * H:(a + 1) * H], w[1][:, k, a * H:(a + 1) * H]),
                                    (h_hi[:, k, :], h_lo[:, k, :]), k == 0, k == KB - 1)
                ins.then_inc(unit_used, 1)

                with pe.Fori(0, NPAIR // PAIRS_IT) as it:
                    gi = g + g_sb + it * (SB_U // RING)
                    pr = l * NPAIR + it * PAIRS_IT

                    def scores(n, j):
                        pe.wait_ge(qk_ready, l * (NPAIR + H) + (it * PAIRS_IT + j) + 1)
                        o0, o1 = PS[:, 4 + 2 * (j % 2), :], PS[:, 5 + 2 * (j % 2), :]
                        three(o0, (qk_hi[:, 1, 0:P], qk_lo[:, 1, 0:P]), (qz_hi, qz_lo), True, False)
                        three(two(o1[:, 0:T]), (qk_hi[:, 1, P:T], qk_lo[:, 1, P:T]),
                              (qz_hi[:, :, P:T], qz_lo[:, :, P:T]), True, False)
                        for o in (two(o0)[:, :, 0:P], two(o1[:, 0:T])):
                            ins = mm(o, ident_r[:], twice(negmask[:].rearrange("p (a t) -> p a t", a=1)), start=False,
                                     stop=False, skip_group_check=True)
                        ins.then_inc(z_done, 1)

                    def sums(n, j):
                        pe.wait_ge(splo_ready, n + 1)
                        o0, o1 = PS[:, 4 + 2 * (j % 2), :], PS[:, 5 + 2 * (j % 2), :]
                        for w in (spf_hi, spf_lo):
                            mm(o0, negtri[:], w[:, 0:2 * T], start=False, stop=False, skip_group_check=True)
                            mm(two(o0)[:, :, P:T], negones[:], two(w[:, 2 * T:2 * CAUSAL]), start=False,
                               stop=w is spf_lo, skip_group_check=True)
                            ins = mm(o1[:, 0:T], negtri[:], w[:, 2 * T:2 * CAUSAL], start=False, stop=w is spf_lo,
                                     skip_group_check=True)
                        ins.then_inc(l_done, 1)

                    def values(n, j):
                        pe.wait_ge(v_ready, l * NVAL + it * (PAIRS_IT // 2) + (j // 2 + 1))
                        pe.wait_ge(attlo_ready, n + 1)
                        f = slice(j % 2 * P, (j % 2 + 1) * P)
                        o = PS[:, 3, :]
                        three(o, (sv_hi[:, 0, f], sv_lo[:, 0, f]), (attf_hi[:, 0:2 * T], attf_lo[:, 0:2 * T]), True, False)
                        ins = three(two(o)[:, :, P:T], (sv_hi[:, 1, f], sv_lo[:, 1, f]),
                                    (two(attf_hi[:, 2 * T:2 * CAUSAL]), two(attf_lo[:, 2 * T:2 * CAUSAL])), False, True)
                        ins.then_inc(av_done, 1)

                    for j in range(PAIRS_IT):
                        n, u = pr + j, SBQ[j]
                        feat_major(gi, u, PS[:, 0, 0:T])
                        feat_major(gi, u + 1, PS[:, 0, T:2 * T])
                        if j:
                            sums(n - 1, j - 1)
                        token_major(gi, u + 2, j % 2)
                        scores(n, j)
                        if j:
                            feat_major(gi, u + 3, PS[:, 2, 0:T])
                            values(n - 1, j - 1)
                    sums(pr + (PAIRS_IT - 1), PAIRS_IT - 1)
                    feat_major(gi, SB_U, PS[:, 0, 0:T])
                    values(pr + (PAIRS_IT - 1), PAIRS_IT - 1)
                    pe.wait_ge(g_evac, l * (NPAIR + H) + (it * PAIRS_IT + PAIRS_IT))

                pe.wait_ge(row_v, l * 3 + 5)
                hold(pe, pe_held)
                for r, row in enumerate((0, 2)):
                    for t in range(TB):
                        nc.tensor.transpose(PS[:, 1, (r * TB + t) * H:(r * TB + t + 1) * H],
                                            row_keep[row][:, t * P:(t + 1) * P], ident[0:H, 0:H])
                for h in range(H):
                    ins = mm(PS[:, 6 + h // 2, (h % 2) * T:(h % 2 + 1) * T], head_sel[:, h, :], row_keep[1],
                             start=True, stop=True, skip_group_check=True)
                ins.then_inc(rows_t, 1)
                pe.wait_ge(acc_ready, l * 3 + 2)
                pe.wait_ge(cols_ready, l * 2 + 1)
                ones_cols(D, 64, 1)
                ones_rows(0, 4).then_inc(ada_red, 1)

                with pe.Fori(0, H) as it:
                    gi = g + g_ml + it * (ML_U // RING)
                    n = l * H + it
                    feat_major(gi, 1, PS[:, 0, 0:T])
                    feat_major(gi, 2, PS[:, 0, T:2 * T])
                    pe.wait_ge(cols_ready, l * 2 + 2)
                    token_major(gi, 3, 0)
                    token_major(gi, 4, 1)
                    feat_major(gi, 5, PS[:, 2, 0:T])
                    pe.wait_ge(qk_ready, l * (NPAIR + H) + it + (NPAIR + 1))
                    three(PS[:, 3, 0:T], (qk_hi[:, 1, 0:P], qk_lo[:, 1, 0:P]), (qk_hi[:, 0, :], qk_lo[:, 0, :]),
                          True, False)
                    ins = three(two(PS[:, 3, T:2 * T]), (qk_hi[:, 1, P:T], qk_lo[:, 1, P:T]),
                                (twice(qk_hi[:, 0:1, P:T]), twice(qk_lo[:, 0:1, P:T])), False, True)
                    ins.then_inc(s_done, 1)
                    feat_major(gi, 6, PS[:, 2, T:2 * T])
                    pe.wait_ge(v_ready, l * NVAL + it + (NPAIR // 2 + 1))
                    pe.wait_ge(s_ready, n + 2)
                    pe.wait_ge(g_ready, l * 2 + 1)
                    for t in range(TB):
                        for s in range(t + 1):
                            col = t * P if s == 0 else T
                            ins = three(PS[:, 4 + t, 0:VA], (S_hi[:, col:col + P], S_lo[:, col:col + P]),
                                        (v_hi[:, s, :], v_lo[:, s, :]), s == 0, s == t)
                    ins.then_inc(num_done, 1)
                    pe.wait_ge(mb_ready, l * 1 + 1)
                    feat_major(gi, 7, PS[:, 7, 0:T])
                    feat_major(gi, 8, PS[:, 7, T:2 * T])
                    for t in range(TB):
                        pe.wait_ge(hmn_ready, n * 2 + (t + 1))
                        for b in range(2):
                            ins = nc.tensor.transpose(PS[:, 6, b * T + t * P:b * T + (t + 1) * P],
                                                      hmn[:, t, b * P:(b + 1) * P], ident[:])
                    ins.then_inc(hmt_done, 1)

                pe.wait_ge(acc_ready, l * 3 + 3)
                ones_cols(0, 0, 3)
                ones_rows(D, 0).then_inc(ada_red, 1)

                with pe.Fori(0, KB // 2) as it:
                    gi = g + g_pj + it * (PJ_U // RING)
                    for b in range(2):
                        pe.wait_ge(yf_ready, l * KB + it * 2 + (b + 1))
                        feat_major(gi, 2 * b + 1, PS[:, 4 + b, 0:T], (hs_hi, hs_lo))
                        pe.wait_ge(hm_ready, l * H + (H + 1))
                        feat_major(gi, 2 * b + 2, PS[:, 4 + b, T:2 * T], (hm_hi, hm_lo))

                pe.wait_ge(g_ready, l * 2 + 2)
                for i in range(8):
                    w = unit(g + g_out, i + 1, 512, 2)
                    q = i % 4
                    pe.wait_ge(y_ready, l * KB + (2 * q + 3))
                    for t in range(TB):
                        bank = (6 if i < 4 else 0) + t
                        for k in range(2):
                            kk = 2 * q + k
                            ins = three(PS[:, bank, :], (h_hi[:, kk, t * P:(t + 1) * P], h_lo[:, kk, t * P:(t + 1) * P]),
                                        (w[0][:, k, :], w[1][:, k, :]), kk == 0, kk == KB - 1)
                        if q == 3 and t == 0:
                            ins.then_inc(bank_done, 1)
                    ins.then_inc(unit_used, 1)
                turn(l * 2 + 1)
                w = unit(g + g_out, 9, E)
                for k in range(KB):
                    if k % 2 == 0:
                        pe.wait_ge(h_ready, l * 8 + (k // 2 + 5))
                    ins = three(PS[0:E, 4, 0:T], (w[0][:, k, :], w[1][:, k, :]), (h_hi[:, k, :], h_lo[:, k, :]),
                                k == 0, k == KB - 1)
                ins.then_inc(unit_used, 1)

                def hidden(g, i, par):
                    feat_major(g, i, PS[:, 6 + par, 0:T])
                    feat_major(g, i + 1, PS[:, 6 + par, T:2 * T])

                def down(g, i, n, par, stop=False):
                    w = unit(g, i, 512, 2)
                    pe.wait_ge(hid_ready, n + 1)
                    for t in range(TB):
                        for h in range(2):
                            ins = three(PS[:, 2 * t + h, :],
                                        (hid_hi[:, par, t * P:(t + 1) * P], hid_lo[:, par, t * P:(t + 1) * P]),
                                        (w[0][:, h, :], w[1][:, h, :]), False, stop)
                            if stop and 2 * t + h < 3:
                                ins.then_inc(bank_done, 1)
                    ins.then_inc(unit_used, 1)
                    return ins

                feat_major(g + g_out, 10, PS[:, 7, 0:T])
                pe.wait_ge(rt_ready, l * 1 + 1)
                hold(pe, pe_held)
                for t in range(TB):
                    ins = nc.tensor.transpose(PS[:, 5, t * E:(t + 1) * E], scT[:, t * P:(t + 1) * P], ident[0:E, 0:E])
                ins.then_inc(sc_turned, 1)
                feat_major(g + g_out, 11, PS[:, 7, T:2 * T])
                hidden(g + g_moe, 0, 0)
                pe.wait_ge(gts_ready, l * 1 + 1)
                hold(pe, pe_held)
                for t in range(TB):
                    ins = nc.tensor.transpose(PS[0:E, 4, t * P:(t + 1) * P], gts[:, t, :], ident[:])
                ins.then_inc(gt_done, 1)
                for b in range(4):
                    mm(PS[:, b, :], zeros_r[:], h_hi[:, 0:2, :].rearrange("p a b -> p (a b)"), start=True, stop=False,
                       skip_group_check=True)
                pe.wait_ge(gT_ready, l * 1 + 1)
                for e in range(2):
                    ins = mm(PS[:, 5, e * T:(e + 1) * T], head_sel[:, e, :], gT[0:H, :], start=True, stop=True,
                             skip_group_check=True)
                ins.then_inc(gb_done, 1)
                with pe.Fori(0, E // EXP_IT) as it:
                    gi = g + g_moe + it * 3
                    for e in range(EXP_IT):
                        down(gi, 3 * e + 2, l * EV + it * EXP_IT + e, 1 - e % 2)
                        hidden(gi, 3 * e + 3, 1 - e % 2)
                down(g + g_post, 2, l * EV + E, 1)
                down(g + g_post, 3, l * EV + (E + 1), 0, True)


_INS = ["x", "c", "ada_w", "ada_b", "norm1_w", "w_in", "conv_w", "conv_b", "m_igate_b", "m_fgate_b", "m_norm_w",
        "w_proj_a", "w_proj_b", "w_out", "norm2_w", "router_w", "router_b", "w_gate", "w_up", "w_down",
        "sh_gate", "sh_up", "sh_down", "final_norm_w"]


def kernel(**inputs):
    import numpy as _np
    import concourse.bacc as _bacc
    from concourse import mybir as _mybir
    from concourse.bass_utils import run_bass_kernel_spmd as _run

    nc = _bacc.Bacc("TRN2", target_bir_lowering=False, num_devices=1)
    arrays, args = {}, []
    for name in _INS:
        a = _np.ascontiguousarray(inputs[name])
        arrays[f"in_{name}_dram"] = a
        args.append(nc.dram_tensor(f"in_{name}_dram", a.shape, _mybir.dt.from_np(a.dtype), kind="ExternalInput").ap())
    tokens, experts = inputs["x"].shape[1], inputs["router_w"].shape[2]
    gates = nc.dram_tensor("gates_dram", (experts, tokens), _mybir.dt.float32, kind="Internal").ap()
    out = nc.dram_tensor("out_dram", inputs["x"].shape, _mybir.dt.float32, kind="ExternalOutput").ap()
    trunk(nc, *args, gates, out)
    r = _run(nc, [arrays], core_ids=[0])
    return r.results[0]["out_dram"]
```
